# Optimizing a Trainium2 kernel written in Bass

```python
import jax, jax.numpy as jnp
from jax import lax
import numpy as np
import math

D_MODEL = 1024
BATCH = 1
SEQ = 512
DEPTH = 2

HEAD_DIM = 64
N_Q_HEADS = 8
N_KV_HEADS = 2
GQA_GROUP = N_Q_HEADS // N_KV_HEADS
WINDOW = 128
ROPE_THETA = 10000.0
RET_HEADS = 4
RET_QK_DIM = 128
RET_V_DIM = 2 * RET_QK_DIM
RET_CHUNK = 128
RET_THETA = 10000.0
D_FF = 4 * D_MODEL
EPS = 1e-6

ATT_Q = N_Q_HEADS * HEAD_DIM
ATT_KV = N_KV_HEADS * HEAD_DIM
RET_QK = RET_HEADS * RET_QK_DIM
RET_V = RET_HEADS * RET_V_DIM
SPLIT_SIZES = (ATT_Q, ATT_KV, ATT_KV, RET_QK, RET_QK, RET_V, RET_V, D_MODEL, D_MODEL)
W_IN = sum(SPLIT_SIZES)
SPLIT_POINTS = tuple(int(v) for v in np.cumsum(SPLIT_SIZES)[:-1])


def rmsnorm(x, g):
    xf = x.astype(jnp.float32)
    y = xf * lax.rsqrt(jnp.mean(xf * xf, axis=-1, keepdims=True) + EPS)
    return (y * g.astype(jnp.float32)).astype(x.dtype)

def rope_half(x, pos):
    half = x.shape[-1] // 2
    inv = ROPE_THETA ** (-jnp.arange(half, dtype=jnp.float32) / half)
    ang = pos.astype(jnp.float32)[:, None] * inv[None, :]
    cos = jnp.cos(ang)[None, :, None, :]
    sin = jnp.sin(ang)[None, :, None, :]
    xf = x.astype(jnp.float32)
    x1, x2 = xf[..., :half], xf[..., half:]
    return jnp.concatenate([x1 * cos - x2 * sin, x2 * cos + x1 * sin], axis=-1).astype(x.dtype)

def rotate_every_two(x):
    x1, x2 = x[..., ::2], x[..., 1::2]
    return jnp.stack([-x2, x1], axis=-1).reshape(x.shape)

def retention_rotation(x, pos):
    dk = x.shape[-1]
    theta = 1.0 / (RET_THETA ** jnp.linspace(0.0, 1.0, dk // 2, dtype=jnp.float32))
    theta = jnp.repeat(theta, 2)
    ang = pos.astype(jnp.float32)[:, None] * theta[None, :]
    cos = jnp.cos(ang)[None, :, None, :]
    sin = jnp.sin(ang)[None, :, None, :]
    xf = x.astype(jnp.float32)
    return (xf * cos + rotate_every_two(xf) * sin).astype(x.dtype)

def sliding_window_sink_attention(q, k, v, sinks):
    B, S = q.shape[0], q.shape[1]
    C = WINDOW
    nb = S // C
    qb = q.reshape(B, nb, C, N_KV_HEADS, GQA_GROUP, HEAD_DIM)
    kb = k.reshape(B, nb, C, N_KV_HEADS, HEAD_DIM)
    vb = v.reshape(B, nb, C, N_KV_HEADS, HEAD_DIM)

    def band(t):
        prev = jnp.pad(t, ((0, 0), (1, 0), (0, 0), (0, 0), (0, 0)))[:, :-1]
        return jnp.concatenate([prev, t], axis=2)

    kk, vv = band(kb), band(vb)
    s = jnp.einsum('bnqhgd,bnkhd->bnhgqk', qb, kk).astype(jnp.float32) * (HEAD_DIM ** -0.5)
    qi = jnp.arange(C)[:, None] + C
    kj = jnp.arange(2 * C)[None, :]
    rel = qi - kj
    valid = (rel >= 0) & (rel < WINDOW)
    first = (jnp.arange(nb) > 0)[:, None, None] | (kj >= C)[None]
    mask = valid[None] & first
    s = jnp.where(mask[None, :, None, None], s, -jnp.inf)
    sink = jnp.broadcast_to(
        sinks.astype(jnp.float32).reshape(1, 1, N_KV_HEADS, GQA_GROUP, 1, 1),
        s.shape[:-1] + (1,))
    p = jax.nn.softmax(jnp.concatenate([s, sink], axis=-1), axis=-1)[..., :-1]
    o = jnp.einsum('bnhgqk,bnkhd->bnqhgd', p.astype(v.dtype), vv)
    return o.reshape(B, S, ATT_Q)

def chunkwise_retention(q, k, v):
    B, S = q.shape[0], q.shape[1]
    C = RET_CHUNK
    nc = S // C
    log_g = jnp.log(1.0 - 2.0 ** (-5.0 - jnp.arange(RET_HEADS, dtype=jnp.float32)))
    idx = jnp.arange(C, dtype=jnp.float32)
    rel = idx[:, None] - idx[None, :]
    dmask = jnp.where(rel[None] >= 0, jnp.exp(log_g[:, None, None] * jnp.maximum(rel, 0.0)[None]), 0.0)

    qc = q.astype(jnp.float32).reshape(B, nc, C, RET_HEADS, RET_QK_DIM)
    kc = k.astype(jnp.float32).reshape(B, nc, C, RET_HEADS, RET_QK_DIM)
    vc = v.astype(jnp.float32).reshape(B, nc, C, RET_HEADS, RET_V_DIM)

    s = jnp.einsum('bnihd,bnjhd->bnhij', qc, kc) * dmask[None, None]
    inner = jnp.einsum('bnhij,bnjhe->bnihe', s, vc)

    zeta = jnp.exp(log_g[None, :] * (C - 1.0 - idx)[:, None])
    kv = jnp.einsum('bnjhd,bnjhe->nbhde', kc, vc * zeta[None, None, :, :, None])
    g_chunk = jnp.exp(log_g * C)[None, :, None, None]

    def step(R, kv_n):
        return R * g_chunk + kv_n, R

    R0 = jnp.zeros((B, RET_HEADS, RET_QK_DIM, RET_V_DIM), jnp.float32)
    _, R_prev = lax.scan(step, R0, kv)
    xi = jnp.exp(log_g[None, :] * (idx + 1.0)[:, None])
    cross = jnp.einsum('bnihd,nbhde->bnihe', qc, R_prev) * xi[None, None, :, :, None]
    return (inner + cross).reshape(B, S, RET_HEADS, RET_V_DIM)

def hybrid_layer(x, g_mix, w_in, sinks, w_a, w_b, w_out, g_mlp, w_up, w_down):
    B, S, _ = x.shape
    pos = jnp.arange(S)
    h = rmsnorm(x, g_mix)
    z = h @ w_in
    aq, ak, av, rq, rk, rv, rg, ga, gb = jnp.split(z, SPLIT_POINTS, axis=-1)

    aq = rope_half(aq.reshape(B, S, N_Q_HEADS, HEAD_DIM), pos)
    ak = rope_half(ak.reshape(B, S, N_KV_HEADS, HEAD_DIM), pos)
    av = av.reshape(B, S, N_KV_HEADS, HEAD_DIM)
    ya = sliding_window_sink_attention(aq, ak, av, sinks) @ w_a

    rq = retention_rotation(rq.reshape(B, S, RET_HEADS, RET_QK_DIM), pos)
    rk = retention_rotation(rk.reshape(B, S, RET_HEADS, RET_QK_DIM), pos) * (RET_QK_DIM ** -0.5)
    rv = rv.reshape(B, S, RET_HEADS, RET_V_DIM)
    r = chunkwise_retention(rq, rk, rv)
    r = r * lax.rsqrt(jnp.mean(r * r, axis=-1, keepdims=True) + EPS)
    r = r.reshape(B, S, RET_V) * jax.nn.silu(rg.astype(jnp.float32))
    yb = r.astype(x.dtype) @ w_b

    mixed = jax.nn.sigmoid(ga) * ya + jax.nn.sigmoid(gb) * yb
    x = x + mixed @ w_out

    h2 = rmsnorm(x, g_mlp)
    x = x + jnp.square(jax.nn.relu(h2 @ w_up)) @ w_down
    return x

def first_inputs(seed: int = 0) -> dict:
    key = jax.random.key(seed)
    ks = jax.random.split(key, 12)
    f32 = jnp.float32

    def nrm(k, shape, fan_in):
        return jax.random.normal(k, shape, f32) * (fan_in ** -0.5)

    return {
        "x": jax.random.normal(ks[0], (BATCH, SEQ, D_MODEL), f32),
        "g_mix": 1.0 + 0.05 * jax.random.normal(ks[1], (DEPTH, D_MODEL), f32),
        "w_in": nrm(ks[2], (DEPTH, D_MODEL, W_IN), D_MODEL),
        "sinks": 0.5 * jax.random.normal(ks[3], (DEPTH, N_Q_HEADS), f32),
        "w_a": nrm(ks[4], (DEPTH, ATT_Q, D_MODEL), ATT_Q),
        "w_b": nrm(ks[5], (DEPTH, RET_V, D_MODEL), RET_V),
        "w_out": nrm(ks[6], (DEPTH, D_MODEL, D_MODEL), D_MODEL),
        "g_mlp": 1.0 + 0.05 * jax.random.normal(ks[7], (DEPTH, D_MODEL), f32),
        "w_up": nrm(ks[8], (DEPTH, D_MODEL, D_FF), D_MODEL),
        "w_down": nrm(ks[9], (DEPTH, D_FF, D_MODEL), D_FF),
        "g_final": 1.0 + 0.05 * jax.random.normal(ks[10], (D_MODEL,), f32),
    }

def first_block(x, g_mix, w_in, sinks, w_a, w_b, w_out, g_mlp, w_up, w_down, g_final):
    for l in range(DEPTH):
        x = hybrid_layer(x, g_mix[l], w_in[l], sinks[l], w_a[l], w_b[l], w_out[l],
                         g_mlp[l], w_up[l], w_down[l])
    return rmsnorm(x, g_final)


CHUNK = 64
Q_BLOCK = 128
ATT_HEADS = 8
ATT_HEAD_DIM = 64
IDX_HEADS = 8
IDX_DIM = 64
TOPK_MAX = 256
ROPE_THETA_2 = 500000.0
ROPE_FRACTION_DIV = 4
GLA_HEADS = 4
GLA_DK = 128
GLA_DV = 256
GLA_GATE_RANK = 16
GLA_TAU = 16.0
D_FF_2 = 2816
CONV_WIDTH = 3
LN_EPS = 1e-5
DN_ALPHA = (2.0 * DEPTH) ** 0.25
DN_BETA = (8.0 * DEPTH) ** -0.25

ATT_WIDTH = ATT_HEADS * ATT_HEAD_DIM
IDXQ_WIDTH = IDX_HEADS * IDX_DIM
GLA_K_WIDTH = GLA_HEADS * GLA_DK
GLA_V_WIDTH = GLA_HEADS * GLA_DV
IN_SPLITS = (ATT_WIDTH, ATT_WIDTH, ATT_WIDTH,
             IDXQ_WIDTH, IDX_DIM, IDX_HEADS,
             GLA_K_WIDTH, GLA_K_WIDTH, GLA_V_WIDTH, GLA_GATE_RANK, GLA_V_WIDTH,
             D_MODEL, D_MODEL)
IN_WIDTH = sum(IN_SPLITS)


F32 = jnp.float32

def layer_norm(x, g, b):
    xf = x.astype(F32)
    mu = jnp.mean(xf, axis=-1, keepdims=True)
    var = jnp.mean(jnp.square(xf - mu), axis=-1, keepdims=True)
    return ((xf - mu) * lax.rsqrt(var + LN_EPS) * g.astype(F32) + b.astype(F32)).astype(x.dtype)

def partial_rope(x, pos):
    dh = x.shape[-1]
    rd = dh // ROPE_FRACTION_DIV
    half = rd // 2
    inv = ROPE_THETA_2 ** (-jnp.arange(half, dtype=F32) * 2.0 / rd)
    ang = pos.astype(F32)[..., None] * inv
    cos = jnp.cos(ang)[:, :, None, :]
    sin = jnp.sin(ang)[:, :, None, :]
    xr = x[..., :rd].astype(F32)
    x1, x2 = xr[..., :half], xr[..., half:]
    rot = jnp.concatenate([x1 * cos - x2 * sin, x2 * cos + x1 * sin], axis=-1)
    return jnp.concatenate([rot.astype(x.dtype), x[..., rd:]], axis=-1)

def dsa_attention(q, k, v, q_idx, k_idx, w_idx):
    B, S, H, Dh = q.shape
    topk = min(TOPK_MAX, S // 4)
    nb = S // Q_BLOCK
    key_chunk = jnp.arange(S) // CHUNK
    k_idx32 = k_idx.astype(F32)

    def to_blocks(a):
        return jnp.moveaxis(a.reshape((B, nb, Q_BLOCK) + a.shape[2:]), 1, 0)

    def block(args):
        qb, qib, wb, start = args
        q_chunk = (start + jnp.arange(Q_BLOCK)) // CHUNK
        admissible = key_chunk[None, :] <= q_chunk[:, None]
        dots = jnp.einsum('bqhd,bsd->bqhs', qib.astype(F32), k_idx32) * (IDX_DIM ** -0.5)
        score = jnp.einsum('bqhs,bqh->bqs', jax.nn.relu(dots),
                           wb.astype(F32) * (IDX_HEADS ** -0.5))
        score = jnp.where(admissible[None], score, -jnp.inf)
        top_val, top_idx = lax.top_k(score, topk)
        valid = jnp.isfinite(top_val)
        k_sel = jax.vmap(lambda kk, ii: kk[ii])(k, top_idx)
        v_sel = jax.vmap(lambda vv, ii: vv[ii])(v, top_idx)
        logits = jnp.einsum('bqhd,bqkhd->bhqk', qb.astype(F32), k_sel.astype(F32)) * (Dh ** -0.5)
        logits = jnp.where(valid[:, None], logits, -jnp.inf)
        p = jax.nn.softmax(logits, axis=-1)
        return jnp.einsum('bhqk,bqkhd->bqhd', p, v_sel.astype(F32)).astype(q.dtype)

    starts = jnp.arange(nb) * Q_BLOCK
    out = lax.map(block, (to_blocks(q), to_blocks(q_idx), to_blocks(w_idx), starts))
    return jnp.moveaxis(out, 0, 1).reshape(B, S, H, Dh)

def gla_chunked(q, k, v, log_a):
    B, S, H, Dk = q.shape
    Dv = v.shape[-1]
    nc = S // CHUNK

    def chunks(a):
        return jnp.moveaxis(a.astype(F32).reshape((B, nc, CHUNK) + a.shape[2:]), 1, 0)

    def step(state, inp):
        qc, kc, vc, lac = inp
        cum = jnp.cumsum(lac, axis=1)
        total = cum[:, -1]
        k_dec = kc * jnp.exp(total[:, None] - cum)
        state = jnp.exp(total)[..., None] * state + jnp.einsum('bchk,bchv->bhkv', k_dec, vc)
        out = jnp.einsum('bchk,bhkv->bchv', qc, state)
        return state, out

    s0 = jnp.zeros((B, H, Dk, Dv), F32)
    _, o = lax.scan(step, s0, (chunks(q) * (Dk ** -0.5), chunks(k), chunks(v), chunks(log_a)))
    return jnp.moveaxis(o, 0, 1).reshape(B, S, H, Dv)

def hybrid_mixer(x, pos, w_in, gla_w_gate, gla_b_gate, gla_norm_g, p_attn, p_gla, w_out, b_out):
    B, S, _ = x.shape
    proj = x @ w_in
    offsets = np.cumsum(IN_SPLITS)[:-1].tolist()
    (aq, ak, av, iq, ik, iw, gq, gk, gv, g_lr, g_r, gate_a, gate_b) = jnp.split(proj, offsets, axis=-1)

    aq = partial_rope(aq.reshape(B, S, ATT_HEADS, ATT_HEAD_DIM), pos)
    ak = partial_rope(ak.reshape(B, S, ATT_HEADS, ATT_HEAD_DIM), pos)
    av = av.reshape(B, S, ATT_HEADS, ATT_HEAD_DIM)
    iq = partial_rope(iq.reshape(B, S, IDX_HEADS, IDX_DIM), pos)
    ik = partial_rope(ik[:, :, None, :], pos)[:, :, 0, :]
    ya = dsa_attention(aq, ak, av, iq, ik, iw).reshape(B, S, ATT_WIDTH) @ p_attn

    gate_logits = g_lr @ gla_w_gate + gla_b_gate
    log_a = jax.nn.log_sigmoid(gate_logits.astype(F32)) / GLA_TAU
    o = gla_chunked(gq.reshape(B, S, GLA_HEADS, GLA_DK),
                    gk.reshape(B, S, GLA_HEADS, GLA_DK),
                    gv.reshape(B, S, GLA_HEADS, GLA_DV),
                    log_a.reshape(B, S, GLA_HEADS, GLA_DK))
    mu = jnp.mean(o, axis=-1, keepdims=True)
    var = jnp.mean(jnp.square(o - mu), axis=-1, keepdims=True)
    o = (o - mu) * lax.rsqrt(var + LN_EPS) * gla_norm_g.astype(F32).reshape(GLA_HEADS, GLA_DV)
    o = o.reshape(B, S, GLA_V_WIDTH).astype(x.dtype) * jax.nn.silu(g_r)
    yb = o @ p_gla

    merged = jax.nn.sigmoid(gate_a) * ya + jax.nn.sigmoid(gate_b) * yb
    return merged @ w_out + b_out

def conv_ffn(x, w_up, conv_w, conv_b, w_down):
    u = x @ w_up
    c = u.shape[-1]
    u = lax.conv_general_dilated(u, conv_w[:, None, :], window_strides=(1,),
                                 padding=[(CONV_WIDTH - 1, 0)],
                                 dimension_numbers=('NWC', 'WIO', 'NWC'),
                                 feature_group_count=c) + conv_b
    a, b = jnp.split(u, 2, axis=-1)
    return (jax.nn.gelu(a) * b) @ w_down

def second_inputs(seed: int = 0) -> dict:
    key = jax.random.key(seed)
    ks = jax.random.split(key, 20)
    L, D = DEPTH, D_MODEL
    nrm = lambda k, shape, s: jax.random.normal(k, shape, F32) * s
    x = jax.random.normal(ks[0], (BATCH, SEQ, D), F32)
    offs = jax.random.randint(ks[1], (BATCH, 1), 0, 64) * CHUNK
    positions = (offs + jnp.arange(SEQ, dtype=jnp.int32)[None, :]).astype(jnp.int32)
    return {
        "x": x,
        "positions": positions,
        "w_in": nrm(ks[2], (L, D, IN_WIDTH), D ** -0.5),
        "gla_w_gate": nrm(ks[3], (L, GLA_GATE_RANK, GLA_K_WIDTH), GLA_GATE_RANK ** -0.5),
        "gla_b_gate": nrm(ks[4], (L, GLA_K_WIDTH), 0.1) + 1.0,
        "gla_norm_g": 1.0 + nrm(ks[5], (L, GLA_V_WIDTH), 0.02),
        "p_attn": nrm(ks[6], (L, ATT_WIDTH, D), ATT_WIDTH ** -0.5),
        "p_gla": nrm(ks[7], (L, GLA_V_WIDTH, D), GLA_V_WIDTH ** -0.5),
        "w_mix_out": nrm(ks[8], (L, D, D), DN_BETA * D ** -0.5),
        "b_mix_out": nrm(ks[9], (L, D), 0.02),
        "ln1_g": 1.0 + nrm(ks[10], (L, D), 0.02),
        "ln1_b": nrm(ks[11], (L, D), 0.02),
        "w_up": nrm(ks[12], (L, D, 2 * D_FF_2), D ** -0.5),
        "conv_w": nrm(ks[13], (L, CONV_WIDTH, 2 * D_FF_2), CONV_WIDTH ** -0.5),
        "conv_b": nrm(ks[14], (L, 2 * D_FF_2), 0.02),
        "w_down": nrm(ks[15], (L, D_FF_2, D), DN_BETA * D_FF_2 ** -0.5),
        "ln2_g": 1.0 + nrm(ks[16], (L, D), 0.02),
        "ln2_b": nrm(ks[17], (L, D), 0.02),
    }

def second_block(x, positions, w_in, gla_w_gate, gla_b_gate, gla_norm_g, p_attn, p_gla,
              w_mix_out, b_mix_out, ln1_g, ln1_b, w_up, conv_w, conv_b, w_down, ln2_g, ln2_b):
    for l in range(DEPTH):
        y = hybrid_mixer(x, positions, w_in[l], gla_w_gate[l], gla_b_gate[l], gla_norm_g[l],
                         p_attn[l], p_gla[l], w_mix_out[l], b_mix_out[l])
        x = layer_norm(DN_ALPHA * x + y, ln1_g[l], ln1_b[l])
        y = conv_ffn(x, w_up[l], conv_w[l], conv_b[l], w_down[l])
        x = layer_norm(DN_ALPHA * x + y, ln2_g[l], ln2_b[l])
    return x


def setup_inputs(seed=0):
    out = dict(first_inputs(seed))
    for name, value in second_inputs(seed + 1).items():
        if name != "x":
            out[name + "_2"] = value
    return out


def reference(
    x, g_mix, w_in, sinks, w_a, w_b, w_out, g_mlp, w_up, w_down, g_final, positions_2, w_in_2,
    gla_w_gate_2, gla_b_gate_2, gla_norm_g_2, p_attn_2, p_gla_2, w_mix_out_2, b_mix_out_2,
    ln1_g_2, ln1_b_2, w_up_2, conv_w_2, conv_b_2, w_down_2, ln2_g_2, ln2_b_2,
):
    x = first_block(
        x, g_mix, w_in, sinks, w_a, w_b, w_out, g_mlp, w_up, w_down, g_final,
    )
    return second_block(
        x, positions_2, w_in_2, gla_w_gate_2, gla_b_gate_2, gla_norm_g_2, p_attn_2, p_gla_2,
        w_mix_out_2, b_mix_out_2, ln1_g_2, ln1_b_2, w_up_2, conv_w_2, conv_b_2, w_down_2,
        ln2_g_2, ln2_b_2,
    )


_drawn_inputs = setup_inputs


def setup_inputs(seed=0):
    import zlib

    import numpy as np

    out = dict(_drawn_inputs(seed))
    spreads = {}
    factors = {'sinks': 6.766,
     'gla_b_gate_2': 4.4,
     'gla_norm_g_2': 8.0,
     'b_mix_out_2': 2.699,
     'conv_b_2': 6.002}
    for name, (base, spread) in spreads.items():
        noise = np.random.default_rng([zlib.crc32(name.encode()), seed]).standard_normal(out[name].shape)
        drawn = base * np.exp(spread * noise) if base else spread * noise
        out[name] = __import__('jax').numpy.asarray(drawn.astype(out[name].dtype))
    for name, factor in factors.items():
        out[name] = (out[name] * factor).astype(out[name].dtype)
    return out
```

```python
from contextlib import ExitStack

import numpy as np

import concourse.bass as bass
from concourse import mybir

F32 = mybir.dt.float32
F32R = mybir.dt.float32r
I32 = mybir.dt.int32
ALU = mybir.AluOpType
ACT = mybir.ActivationFunctionType
AX = mybir.AxisListType.X

P = 128
D = 1024
S = 512
DEPTH = 2
KD = D // P
NB = S // P
EPS = 1e-6
LN_EPS = 1e-5
NEG = -1.0e30
TAKEN = -3.0e38
PANEL = 2048

HD = 64
WINDOW = 128
RET_HEADS, RET_QK, RET_V = 4, 128, 256
D_FF = 4 * D
FF1_GROUPS = 8
TOPK = min(256, S // 4)
GLA_HEADS, GLA_DK, GLA_DV, GLA_RANK, GLA_TAU = 4, 128, 256, 16, 16.0
D_FF2 = 2816
FF2_GROUPS = D_FF2 // (2 * P)
DN_ALPHA = (2.0 * DEPTH) ** 0.25

NPA = 33 + 4 * FF1_GROUPS
NPB = 39 + 3 * FF2_GROUPS
NPANELS = DEPTH * (NPA + NPB)
CREDIT = 8


def _panel(rows):
    kt = rows.shape[0] // P
    return rows.reshape(kt, P, rows.shape[1]).transpose(1, 0, 2).reshape(P, -1)


def _cols(w, n=256):
    return [_panel(w[:, c:c + n]) for c in range(0, w.shape[1], n)]


def _stream(i):
    out = []
    for l in range(DEPTH):
        w = i["w_in"][l]
        q, k, v, rq, rk, rv, rg, ga, gb = np.split(w, [512, 640, 768, 1280, 1792, 2816, 3840, 4864], axis=1)
        q = q.reshape(D, 2, 4, HD).transpose(0, 2, 1, 3).reshape(D, 512)
        wa = i["w_a"][l].reshape(2, 4, HD, D).transpose(1, 0, 2, 3).reshape(512, D)
        out += _cols(q) + [_panel(np.concatenate([k, v], 1))] + _cols(rq) + _cols(rk) + _cols(ga)
        out += _cols(wa, 512)
        rvp, rgp = _cols(rv), _cols(rg)
        for h in range(RET_HEADS):
            out += [rvp[h], rgp[h]]
        out += _cols(gb) + _cols(i["w_b"][l]) + _cols(i["w_out"][l])
        up = _cols(i["w_up"][l])
        down = [p for g in range(FF1_GROUPS) for p in _cols(i["w_down"][l][g * 512:(g + 1) * 512], 512)]
        out += up[0:2]
        for g in range(FF1_GROUPS):
            out += up[2 * g + 2:2 * g + 4] + down[2 * g:2 * g + 2]
    for l in range(DEPTH):
        w = i["w_in_2"][l]
        aq, ak, av, iq, ik, iw, gq, gk, gv, glr, gr, ga, gb = np.split(
            w, [512, 1024, 1536, 2048, 2112, 2120, 2632, 3144, 4168, 4184, 5208, 6232], axis=1)
        z = np.zeros((D, 1), np.float32)
        misc = np.concatenate([ik, ik, glr, np.repeat(z, 16, 1), iw, np.repeat(z, 88, 1)], axis=1)
        out += _cols(aq) + _cols(ak) + _cols(iq) + [_panel(misc)] + _cols(av) + _cols(ga)
        out += _cols(i["p_attn_2"][l], 512) + _cols(gq) + _cols(gk)
        gvp, grp = _cols(gv), _cols(gr)
        for h in range(GLA_HEADS):
            out += [gvp[h], grp[h]]
        out += _cols(gb) + _cols(i["p_gla_2"][l]) + _cols(i["w_mix_out_2"][l])
        up, down = i["w_up_2"][l], i["w_down_2"][l]
        a, b = _cols(up[:, :D_FF2]), _cols(up[:, D_FF2:])
        dn = [_panel(down[g * 256:(g + 1) * 256]) for g in range(FF2_GROUPS)]
        out += [a[0], b[0]]
        for g in range(FF2_GROUPS):
            if g + 1 < FF2_GROUPS:
                out += [a[g + 1], b[g + 1]]
            out += [dn[g]]
    assert len(out) == NPANELS
    return np.stack(out)


def _tiles(v):
    return v.reshape(-1, P).T


VA = dict(g_mix=0, g_mlp=8, sinks=16)
VB = dict(gla_g=0, b_mix=8, ln1_g=16, ln1_b=24, ln2_g=32, ln2_b=40, conv_b=48, conv_w=92, g_final=224)
VW = 232


def _vectors(i):
    out = np.zeros((2 * DEPTH, P, VW), np.float32)
    for l in range(DEPTH):
        a, b = out[l], out[DEPTH + l]
        a[:, 0:8] = _tiles(i["g_mix"][l])
        a[:, 8:16] = _tiles(i["g_mlp"][l])
        a[:, 16:24] = np.broadcast_to(i["sinks"][l].reshape(2, 4).T.reshape(1, 8), (P, 8))
        a[:, 224:232] = b[:, 224:232] = _tiles(i["g_final"])
        for name, at in (("gla_norm_g_2", 0), ("b_mix_out_2", 8), ("ln1_g_2", 16), ("ln1_b_2", 24),
                         ("ln2_g_2", 32), ("ln2_b_2", 40), ("conv_b_2", 48)):
            t = _tiles(i[name][l])
            b[:, at:at + t.shape[1]] = t
        for c in range(3):
            b[:, 92 + 44 * c:92 + 44 * (c + 1)] = _tiles(i["conv_w_2"][l, c])
    return out


CA = dict(ident=0, ones=128, perm_a=256, perm_r=384, decay=512, xi=1024, zeta=1536, mask=1540)
CB = dict(ident=0, ones=128, perm_b=256, later=384, total=512, inv=514)
CW = 1796


def _swap(pairs):
    m = np.zeros((P, P), np.float32)
    for to, of in pairs:
        m[of, to] = 1.0
    return m


def _constants():
    f = np.float32
    a, b = np.zeros((P, CW), f), np.zeros((P, CW), f)
    for c in (a, b):
        c[:, 0:128] = np.eye(P)
        c[:, 128:256] = 1.0
    half = HD // 2
    a[:, 256:384] = _swap([(r, (r // HD) * HD + (r % HD + half) % HD) for r in range(P)])
    a[:, 384:512] = _swap([(r, r ^ 1) for r in range(P)])
    idx = np.arange(P)
    scale = RET_QK ** -0.5
    for h in range(RET_HEADS):
        lg = np.log1p(-2.0 ** (-5.0 - h))
        rel = idx[None, :] - idx[:, None]
        a[:, 512 + h * P:512 + (h + 1) * P] = np.where(rel >= 0, np.exp(lg * np.maximum(rel, 0)), 0.0) * scale
        a[:, 1024 + h * P:1024 + (h + 1) * P] = np.exp(lg * (idx + 1.0))[None, :]
        a[:, 1536 + h] = np.exp(lg * (P - 1.0 - idx)) * scale
    a[:, 1540:1668] = np.where(idx[None, :] > idx[:, None], 0.0, NEG)
    a[:, 1668:1796] = np.where(idx[None, :] <= idx[:, None], 0.0, NEG)
    b[:, 256:384] = _swap([(r, r // 64 * 64 + (r % 64 + 8) % 16) if r % 64 < 16 else (r, r) for r in range(P)])
    t = np.arange(P)
    b[:, 384:512] = ((t[:, None] > t[None, :]) & (t[:, None] // 64 == t[None, :] // 64)) / GLA_TAU
    b[:, 512:514] = (t[:, None] // 64 == np.arange(2)[None, :]) / GLA_TAU
    inv = np.power(f(500000.0), -np.arange(8, dtype=f) * f(2.0) / f(16.0)).astype(f)
    b[:, 514] = [inv[r % 64 % 8] if r % 64 < 16 else 0.0 for r in range(P)]
    b[:, 515] = [(-1.0 if r % 64 < 8 else 1.0) for r in range(P)]
    rot = np.zeros((2, P, 2, S), f)
    pos = np.arange(S, dtype=f)
    inv = np.power(f(10000.0), -np.arange(half, dtype=f) / f(half)).astype(f)
    ang = (pos[None, :] * inv[np.arange(P) % half][:, None]).astype(f).astype(np.float64)
    sign = np.where(np.arange(P) % HD < half, -1.0, 1.0)[:, None]
    rot[0, :, 0], rot[0, :, 1] = np.cos(ang), np.sin(ang) * sign
    theta = (f(1.0) / np.power(f(10000.0), np.linspace(0.0, 1.0, RET_QK // 2, dtype=f))).astype(f)
    ang = (pos[None, :] * theta[np.arange(P) // 2][:, None]).astype(f).astype(np.float64)
    sign = np.where(np.arange(P) % 2 == 0, -1.0, 1.0)[:, None]
    rot[1, :, 0], rot[1, :, 1] = np.cos(ang), np.sin(ang) * sign
    return np.stack([a, b]), rot


class Steps:

    def __init__(self, eng, name, sem, marks, sems):
        self.eng, self.name, self.sem, self.marks, self.sems = eng, name, sem, marks, sems
        self.n = 0

    def after(self, *names, own=True):
        need = {}
        for name in names:
            if name is None or (name not in self.marks and not self.marks.get("complete")):
                continue
            who, n = self.marks[name]
            need[who] = max(need.get(who, 0), n)
        if own:
            need[self.name] = self.n
        for who, n in need.items():
            if n > 0:
                self.eng.wait_ge(self.sems[who], n)

    def done(self, instruction, *name):
        instruction.then_inc(self.sem, 1)
        self.n += 1
        if name:
            self.marks[name if len(name) > 1 else name[0]] = (self.name, self.n)


def program(nc, stream, x_in, consts_in, rot_in, vec_in, wgate_in, pos_in, out, marks):
    ctx = ExitStack()
    with ctx:
        def sb(name, shape, dt=F32):
            return ctx.enter_context(nc.sbuf_tensor(name, shape, dt))

        def sem(name):
            return ctx.enter_context(nc.semaphore(name))

        X = sb("x", [P, KD, S])
        XH, XL = sb("x_hi", [P, KD, S], F32R), sb("x_lo", [P, KD, S], F32R)
        YH, YL = sb("y_hi", [P, KD, S], F32R), sb("y_lo", [P, KD, S], F32R)
        WH, WL = sb("w_hi", [P, 2, PANEL], F32R), sb("w_lo", [P, 2, PANEL], F32R)
        RAW = sb("w_raw", [P, 2, PANEL])
        AR = sb("arena", [P, 28, S])
        TMP = sb("tmp", [P, 4, S])
        CT = sb("ct", [P, CW])
        ROT = sb("rotary", [P, 2, S])
        VEC = sb("vec", [P, 2, VW])
        ST = sb("stats", [P, 96])
        WG = sb("w_gate", [32, S])
        PS = ctx.enter_context(nc.psum_tensor("ps", [P, 8, S], F32))

        raw_full = [sem("raw_full0"), sem("raw_full1")]
        hi_ready, lo_ready = sem("hi_ready"), sem("lo_ready")
        const_loaded, stored = sem("const_loaded"), sem("stored")
        up_full, down_full, down_added = sem("up_full"), sem("down_full"), sem("down_added")
        sems = dict(pe=sem("pe_done"), act=sem("act_done"), dve=sem("dve_done"), const=const_loaded,
                    down_full=down_full, down_added=down_added)
        up_read, hid_ready, hid_hi, hid_lo = sem("up_read"), sem("hid_ready"), sem("hid_hi"), sem("hid_lo")
        conv_begun, tap_added, gelu_done = sem("conv_begun"), sem("tap_added"), sem("gelu_done")
        block = ctx.enter_context(nc.Block())

        def unit(a, n=1):
            return AR[:, a:a + n, :]

        G = unit(20, 8)
        SB = unit(0, 8)
        n_consts = [0]

        def const_dma(eng, dst, src, name):
            if n_consts[0]:
                eng.wait_ge(const_loaded, 16 * n_consts[0])
            eng.dma_start(dst, src).then_inc(const_loaded, 16)
            n_consts[0] += 1
            marks[name] = ("const", 16 * n_consts[0])

        @block.sync
        def _(sp):
            with sp.Fori(0, NPANELS // 2) as i:
                for s in range(2):
                    sp.wait_ge(lo_ready, 2 * i + s + 1)
                    sp.dma_start(RAW[:, s, :], stream[bass.ds(2 * i + s, 1), :, :].rearrange("o p n -> p (o n)"))\
                        .then_inc(raw_full[s], 16)
            sp.wait_ge(sems["act"], marks.get("x_final", ("act", 1))[1])
            sp.dma_start(out.rearrange("(k p) s -> p k s", p=P), X[:, :, :]).then_inc(stored, 16)
            sp.wait_ge(stored, 16)

        @block.gpsimd
        def _(pool):
            pool.sem_inc(lo_ready, 2)
            with pool.Fori(0, NPANELS // 2) as i:
                for s in range(2):
                    pool.wait_ge(hi_ready, 2 * i + s + 1)
                    nc.gpsimd.tensor_tensor(WL[:, s, :], RAW[:, s, :], WH[:, s, :].bitcast(F32), ALU.subtract)\
                        .then_inc(lo_ready, 1)

        def at_a(l):
            n = NPA * l
            return dict(q=n, kv=n + 2, rq=n + 3, rk=n + 5, ga=n + 7, wa=n + 11, rv=n + 13, gb=n + 21, wb=n + 25,
                        wo=n + 29, ff=n + 33)

        def at_b(l):
            n = DEPTH * NPA + NPB * l
            return dict(q=n, k=n + 2, iq=n + 4, misc=n + 6, v=n + 7, ga=n + 9, wa=n + 13, gq=n + 15, gk=n + 17,
                        gv=n + 19, gb=n + 27, wb=n + 31, wo=n + 35, ff=n + 39)

        def bases(t, l):
            if t == "a":
                return 4 * FF1_GROUPS * l, 8 * FF1_GROUPS * l, 4 * FF1_GROUPS * l
            g1, g2 = FF1_GROUPS * DEPTH, FF2_GROUPS * l
            return 4 * (g1 + g2), 8 * (g1 + g2), 4 * g1 + 2 * g2

        def mask_b(b):
            if b == 3:
                return ROT[:, 0, :]
            o = 18 * S + (0, 128, 384)[b]
            return AR[:, :, :].rearrange("p a s -> p (a s)")[:, o:o + (b + 1) * P]

        def units_a(l):
            out = []
            for u in range(32):
                n, j, v = u // 8, (u % 8) // 2, u % 2
                k0, nk = max(n - 1, 0), min(n + 1, 2)
                h = slice(64 * v, 64 * v + 64)
                out.append(dict(id=("a", l), nk=nk * P, q=AR[h, j, n * P:(n + 1) * P], k=AR[h, 4, k0 * P:(k0 + nk) * P],
                                v=lambda kb, k0=k0, v=v: AR[:, 5, (k0 + kb) * P + 64 * v:(k0 + kb) * P + 64 * v + 64],
                                mask=CT[:, 1796 - nk * P:1796], weight=1.0, sink=2 * j + v,
                                ready=[("a", l, "v_read"), ("a", l, "roped", 4)],
                                o=AR[h, 14 + j, n * P:(n + 1) * P]))
            return out

        def units_b(l):
            out = []
            for u in range(32):
                b, j, v = u // 8, (u % 8) // 2, u % 2
                h = slice(64 * v, 64 * v + 64)
                out.append(dict(id=("b", l), nk=(b + 1) * P, q=AR[h, j, b * P:(b + 1) * P], k=AR[h, 4 + j, 0:(b + 1) * P],
                                v=lambda kb, j=j, v=v: AR[:, 14 + kb, (2 * j + v) * 64:(2 * j + v) * 64 + 64],
                                mask=mask_b(b), weight=-NEG, sink=None,
                                ready=[("b", l, "mask", b)] + [("read", "b", l, "av", p, m) for p in range(2) for m in range(2)],
                                o=AR[h, 8 + j, b * P:(b + 1) * P]))
            return out

        def up_panel(ff, g, per):
            return ff if isinstance(g, int) and g == 0 else ff + 2 + per * (g - 1)

        def down_panel(ff, g, per, groups):
            if isinstance(g, int) and g == groups - 1:
                return ff + 2 + per * (groups - 1)
            return ff + 4 + per * g

        @block.tensor
        def _(pe):
            T = Steps(pe, "pe", sems["pe"], marks, sems)
            pe.sem_inc(down_full, CREDIT)
            bank_reader = [None] * 8
            tile = [0]

            def split_products(ps, k, last, wh, wl, xh, xl):
                pe.matmul(ps, wh, xh, start=(k == 0), stop=False)
                pe.matmul(ps, wh, xl, start=False, stop=False)
                return pe.matmul(ps, wl, xh, start=False, stop=last)

            def gemm(n, kt, ms, xh, xl, ready, name):
                s = n % 2
                pe.wait_ge(lo_ready, n + 3)
                for m in range(ms):
                    b = tile[0] % 4
                    T.after(bank_reader[b], own=False)
                    for k in range(kt):
                        if m == 0:
                            T.after(ready(k), own=False)
                        c = (k * ms + m) * P
                        mm = split_products(PS[:, b, :], k, k == kt - 1, WH[:, s, c:c + P], WL[:, s, c:c + P],
                                            xh[:, k, :], xl[:, k, :])
                    T.done(mm, *name(m))
                    bank_reader[b] = ("read",) + name(m)
                    tile[0] += 1
                marks[("panel", n)] = marks[name(ms - 1)]

            def gemm_tok(n, ready, name):
                s = n % 2
                pe.wait_ge(lo_ready, n + 3)
                for t in range(NB):
                    b = tile[0] % 4
                    if t % 2 == 0:
                        T.after(bank_reader[b], own=False)
                    for k in range(KD):
                        if t == 0:
                            T.after(ready(k), own=False)
                        ps = PS[:, b, (t % 2) * 256:(t % 2) * 256 + 256]
                        xh, xl = XH[:, k, t * P:(t + 1) * P], XL[:, k, t * P:(t + 1) * P]
                        wh, wl = WH[:, s, k * 256:(k + 1) * 256], WL[:, s, k * 256:(k + 1) * 256]
                        pe.matmul(ps, xh, wh, start=(k == 0), stop=False)
                        pe.matmul(ps, xl, wh, start=False, stop=False)
                        mm = pe.matmul(ps, xh, wl, start=False, stop=(k == KD - 1))
                    if t % 2:
                        T.done(mm, *name(t // 2))
                        bank_reader[b] = ("read",) + name(t // 2)
                        tile[0] += 1
                marks[("panel", n)] = marks[name(1)]

            def column_sums(src, kt, bank, ready, after, name):
                T.after(*after, own=False)
                for k in range(kt):
                    T.after(ready(k), own=False)
                    mm = pe.matmul(PS[:, bank, :], CT[:, 128:256], src(k), start=(k == 0), stop=(k == kt - 1))
                    T.done(mm, *name, k)
                marks[name] = marks[name + (kt - 1,)]

            def swapped(src, perm, bank, after, name):
                T.after(*after, own=False)
                T.done(pe.matmul(PS[:, bank, :], perm, src, start=True, stop=True), *name)

            def attention(units, scores_name):
                def scores(u):
                    U = units[u]
                    T.after(*U["ready"], U["id"] + ("o_read", u - 2) if u >= 2 else None, own=False)
                    T.done(pe.matmul(PS[:, 4 + u % 2, 0:U["nk"]], U["q"], U["k"], start=True, stop=True),
                           *U["id"], "s", u)

                def transposes(u):
                    U = units[u]
                    T.after(U["id"] + ("p", u), U["id"] + ("pt_read", u - 2) if u >= 2 else None, own=False)
                    for kb in range(U["nk"] // P):
                        mm = pe.transpose(PS[:, 6 + u % 2, kb * P:(kb + 1) * P],
                                          TMP[:, u % 2, kb * P:(kb + 1) * P], CT[:, 0:128])
                    T.done(mm, *U["id"], "pt", u)

                def outputs(u):
                    U = units[u]
                    T.after(U["id"] + ("pt_read", u), U["id"] + ("s_read", u), own=False)
                    n = U["nk"] // P
                    for kb in range(n):
                        mm = pe.matmul(PS[0:64, 4 + u % 2, 0:P], U["v"](kb), TMP[:, 2 + u % 2, kb * P:(kb + 1) * P],
                                       start=(kb == 0), stop=(kb == n - 1))
                    T.done(mm, *U["id"], "o", u)

                for u in range(len(units) + 1):
                    if u < len(units):
                        scores(u)
                    if u >= 1:
                        transposes(u - 1)
                        outputs(u - 1)

            def mixer_gemms(l, w, t):
                for p in range(4):
                    gemm(w["gb"] + p, KD, 2, XH, XL, lambda k: None, lambda m: (t, l, "gb", 2 * p + m))
                for p in range(4):
                    gemm(w["wb"] + p, KD, 2, YH, YL, lambda k: (t, l, "r_lo", k), lambda m: (t, l, "wb", 2 * p + m))
                for p in range(4):
                    gemm(w["wo"] + p, KD, 2, XH, XL, lambda k: (t, l, "merged_lo", k),
                         lambda m: (t, l, "wo", 2 * p + m))

            def ffn(l, t, ff, groups, kt, base_t, base_d, base_h, h_ready):
                per = 2 + (2 if kt == 4 else 1)
                for b in range(8):
                    T.after(bank_reader[b], own=False)

                def up(g, s):
                    n = up_panel(ff, g, per)
                    slot = (up_panel(ff, s if isinstance(g, int) else s + 2, per)) % 2
                    for p in range(2):
                        pe.wait_ge(lo_ready, n + p + 3)
                        for m in range(2):
                            j = 2 * p + m
                            if not (isinstance(g, int) and g == 0 and l == 0):
                                pe.wait_ge(up_read, base_t + 4 * g + j - 3)
                            for k in range(KD):
                                if isinstance(g, int) and g == 0 and j == 0:
                                    T.after(h_ready(k), own=False)
                                c = (k * 2 + m) * P
                                sl = (slot + p) % 2
                                mm = split_products(PS[:, j, :], k, k == KD - 1, WH[:, sl, c:c + P],
                                                    WL[:, sl, c:c + P], XH[:, k, :], XL[:, k, :])
                            mm.then_inc(up_full, 1)

                def down(g, s):
                    n = down_panel(ff, g, per, groups)
                    slot = down_panel(ff, s if isinstance(g, int) else s + 2, per, groups if isinstance(g, int) else 99) % 2
                    pe.wait_ge(hid_lo, base_h + kt * (g + 1))
                    ms = 16 // kt
                    for p in range(kt * 8 // 16):
                        pe.wait_ge(lo_ready, n + p + 3)
                        for m in range(ms):
                            d = p * ms + m
                            pe.wait_ge(down_added, CREDIT + base_d + 8 * g + d - 3)
                            for k in range(kt):
                                c = (k * ms + m) * P
                                sl = (slot + p) % 2
                                mm = split_products(PS[:, 4 + d % 4, :], k, k == kt - 1, WH[:, sl, c:c + P],
                                                    WL[:, sl, c:c + P], YH[:, kt * (s % 2) + k, :],
                                                    YL[:, kt * (s % 2) + k, :])
                            mm.then_inc(down_full, 1)

                up(0, 0)
                trips = (groups - 1) // 2
                with pe.Fori(0, trips) as i:
                    up(2 * i + 1, 1)
                    down(2 * i, 0)
                    up(2 * i + 2, 2)
                    down(2 * i + 1, 1)
                for g in range(2 * trips, groups):
                    if g + 1 < groups:
                        up(g + 1, g + 1)
                    down(g, g)
                for b in range(8):
                    bank_reader[b] = (t, l, "ffn_out")
                done = CREDIT + base_d + 8 * groups
                marks[(t, l, "ffn_out")] = ("down_added", done)
                end = ff + per * groups
                marks[("panel", end - 1)] = ("down_full", done)
                marks[("panel", end - 2)] = ("down_full", done - (4 if kt == 4 else 8))

            for l in range(DEPTH):
                w, t = at_a(l), "a"
                if l == 0:
                    T.after("consts_a", own=False)
                column_sums(lambda k: TMP[:, k % 2, :], KD, 4, lambda k: (t, l, "sq", k), [bank_reader[4]], (t, l, "ms"))
                h_ready = lambda k: (t, l, "h_lo", k)
                for p in range(2):
                    gemm(w["q"] + p, KD, 2, XH, XL, h_ready, lambda m: (t, l, "q", 2 * p + m))
                gemm(w["kv"], KD, 2, XH, XL, h_ready, lambda m: (t, l, "q", 4 + m))
                for j in range(5):
                    swapped(AR[:, j, :], CT[:, 256:384], 4 + j % 2,
                            [("read", t, l, "q", j), (t, l, "roped", j - 2) if j > 1 else (t, l, "ms_read")],
                            (t, l, "swap", j))
                T.after(("read", t, l, "q", 5), own=False)
                for n in range(NB):
                    mm = pe.transpose(PS[:, 6, n * P:(n + 1) * P], AR[:, 18, n * P:(n + 1) * P], CT[:, 0:128])
                T.done(mm, t, l, "v_tok")
                for p in range(4):
                    gemm(w["rq"] + p, KD, 2, XH, XL, h_ready, lambda m: (t, l, "rqk", 2 * p + m))
                for j in range(8):
                    swapped(AR[:, 6 + j, :], CT[:, 384:512], 4 + j % 2,
                            [("read", t, l, "rqk", j), (t, l, "roped", 3 + j)], (t, l, "swap", 5 + j))
                T.after((t, l, "roped", 11), (t, l, "roped", 12), own=False)
                attention(units_a(l), t)
                for p in range(4):
                    gemm(w["ga"] + p, KD, 2, XH, XL, h_ready, lambda m: (t, l, "ga", 2 * p + m))
                for p in range(2):
                    gemm(w["wa"] + p, 4, 4, YH, YL, lambda k: (t, l, "ao_lo", k), lambda m: (t, l, "wa", 4 * p + m))
                gemm_tok(w["rv"], h_ready, lambda m: (t, l, "rv", 0, m))
                for h in range(RET_HEADS):
                    q, k, v = AR[:, 6 + h, :], AR[:, 10 + h, :], AR[:, 14 + 2 * (h % 2):16 + 2 * (h % 2), :].rearrange("p a (b e) -> p (a b) e", b=2)
                    T.after((t, l, "r_out_read", h - 1) if h else (t, l, "o_read", 31), own=False)
                    for c in range(NB):
                        mm = pe.matmul(PS[:, 4, c * P:(c + 1) * P], k[:, c * P:(c + 1) * P], q[:, c * P:(c + 1) * P],
                                       start=True, stop=True)
                    T.done(mm, t, l, "rs", h)
                    for c in range(NB):
                        mm = pe.transpose(PS[:, 5, c * P:(c + 1) * P], k[:, c * P:(c + 1) * P], CT[:, 0:128])
                    T.done(mm, t, l, "rkt", h)
                    gemm(w["rv"] + 2 * h + 1, KD, 2, XH, XL, h_ready, lambda m: (t, l, "rg", h, m))
                    T.after((t, l, "kz", h), ("read", t, l, "rv", h, 0), ("read", t, l, "rv", h, 1),
                            (t, l, "r_ms_read", h - 1) if h else (t, l, "pt_read", 31), own=False)
                    for c in range(NB - 1):
                        mm = pe.matmul(PS[:, 6 + c // 2, (c % 2) * 256:(c % 2) * 256 + 256], TMP[:, 1, c * P:(c + 1) * P],
                                       v[:, c, :], start=True, stop=True)
                    T.done(mm, t, l, "kv", h)
                    if h + 1 < RET_HEADS:
                        gemm_tok(w["rv"] + 2 * h + 2, h_ready, lambda m: (t, l, "rv", h + 1, m))
                    T.after((t, l, "rs_decayed", h), (t, l, "qx", h), (t, l, "state", h, 3), own=False)
                    for e in range(2):
                        for c in range(NB):
                            ps = PS[:, 4 + e, c * P:(c + 1) * P]
                            mm = pe.matmul(ps, v[:, c, e * P:(e + 1) * P], TMP[:, 0, c * P:(c + 1) * P],
                                           start=True, stop=(c == 0))
                            if c:
                                o = 4 * S + (c - 1) * 256 + e * P
                                mm = pe.matmul(ps, AR[:, o // S, o % S:o % S + P], TMP[:, 2, c * P:(c + 1) * P],
                                               start=False, stop=True)
                        T.done(mm, t, l, "r_out", h, e)
                    column_sums(lambda e: TMP[:, e, :], 2, 6, lambda e: (t, l, "r_sq", h, e), [], (t, l, "r_ms", h))
                bank_reader[4] = bank_reader[5] = (t, l, "r_out_read", 3)
                bank_reader[6] = (t, l, "r_ms_read", 3)
                bank_reader[7] = (t, l, "state", 3, 3)
                mixer_gemms(l, w, t)
                column_sums(lambda k: TMP[:, k % 2, :], KD, 6, lambda k: (t, l, "sq2", k), [bank_reader[6]], (t, l, "ms2"))
                bank_reader[6] = (t, l, "ms2_read")
                ffn(l, t, w["ff"], FF1_GROUPS, 4, *bases(t, l), lambda k: (t, l, "h2_lo", k))
            column_sums(lambda k: TMP[:, k % 2, :], KD, 4, lambda k: ("f", 0, "sq", k), [bank_reader[4]], ("f", 0, "ms"))
            bank_reader[4] = ("f", 0, "ms_read")

            for l in range(DEPTH):
                w, t = at_b(l), "b"
                T.after("consts_b", own=False)
                h_ready = lambda k: (t, l, "x_lo", k)
                for i, (n0, cnt) in enumerate(((w["q"], 2), (w["k"], 2), (w["iq"], 2), (w["misc"], 1))):
                    for p in range(cnt):
                        gemm(n0 + p, KD, 2, XH, XL, h_ready, lambda m: (t, l, "q", 4 * i + 2 * p + m))
                for b in range(4, 8):
                    T.after(bank_reader[b], own=False)
                for j in range(13):
                    swapped(AR[:, j, :], CT[:, 256:384], 4 + j % 2,
                            [("read", t, l, "q", j), (t, l, "rot_tables"), (t, l, "roped", j - 2) if j > 1 else None],
                            (t, l, "swap", j))
                T.after(("read", t, l, "q", 13), own=False)
                for n in range(NB):
                    mm = pe.transpose(PS[:, 6, n * P:(n + 1) * P], AR[:, 18, n * P:(n + 1) * P], CT[:, 0:128])
                T.done(mm, t, l, "iw")
                for b in range(1, NB):
                    for h in range(8):
                        u = 8 * (b - 1) + h
                        T.after((t, l, "dots_read", u - 2) if u >= 2 else (t, l, "roped", 12), own=False)
                        hp = 64 * (h % 2)
                        T.done(pe.matmul(PS[:, 4 + u % 2, 0:(b + 1) * P], AR[hp:hp + 64, 8 + h // 2, b * P:(b + 1) * P],
                                         AR[hp:hp + 64, 12, 0:(b + 1) * P], start=True, stop=True), t, l, "dots", u)
                for p in range(2):
                    gemm_tok(w["v"] + p, h_ready, lambda m: (t, l, "av", p, m))
                for p in range(4):
                    gemm(w["ga"] + p, KD, 2, XH, XL, h_ready, lambda m: (t, l, "ga", 2 * p + m))
                T.after((t, l, "dots_read", 22), (t, l, "dots_read", 23), (t, l, "iw_read"), own=False)
                attention(units_b(l), t)
                for p in range(2):
                    gemm(w["wa"] + p, 4, 4, YH, YL, lambda k: (t, l, "ao_lo", k), lambda m: (t, l, "wa", 4 * p + m))
                T.after((t, l, "glr"), ("w_gate", l), own=False)
                for n in range(NB):
                    T.after((t, l, "la", n - 2) if n >= 2 else (t, l, "o_read", 31), own=False)
                    T.done(pe.matmul(PS[:, 4 + n % 2, :], AR[0:32, 13, n * P:(n + 1) * P], WG[:, :],
                                     start=True, stop=True), t, l, "gate", n)
                for p in range(2):
                    gemm(w["gq"] + p, KD, 2, XH, XL, h_ready, lambda m: (t, l, "gq", 2 * p + m))
                for p in range(2):
                    gemm_tok(w["gk"] + p, h_ready, lambda m: (t, l, "gk", p, m))
                for n in range(NB):
                    T.after((t, l, "decay_read", n - 2) if n >= 2 else (t, l, "la", 3), own=False)
                    T.done(pe.matmul(PS[:, 4 + n % 2, :], CT[:, 384:512], AR[:, 8 + n, :], start=True, stop=True),
                           t, l, "decay", n)
                T.after((t, l, "pt_read", 31), own=False)
                for h in range(GLA_HEADS):
                    for n in range(NB):
                        mm = pe.matmul(PS[:, 6, h * 8 + 2 * n:h * 8 + 2 * n + 2], AR[:, 8 + n, h * P:(h + 1) * P],
                                       CT[:, 512:514], start=True, stop=True)
                T.done(mm, t, l, "totals")
                gemm_tok(w["gv"], h_ready, lambda m: (t, l, "gv", 0, m))
                for h in range(GLA_HEADS):
                    v = AR[:, 14 + 2 * (h % 2):16 + 2 * (h % 2), :].rearrange("p a (b e) -> p (a b) e", b=2)
                    T.after(("read", t, l, "gv", h, 0), ("read", t, l, "gv", h, 1), (t, l, "totals_read"),
                            (t, l, "kd", 3), own=False)

                    def kv(c):
                        hp = 64 * (c % 2)
                        if c % 2:
                            T.after()
                        else:
                            T.after((t, l, "state", h, c - 3) if c >= 4 else
                                    ((t, l, "o_mean_read" if c == 0 else "o_ms_read", h - 1) if h else None), own=False)
                        T.done(pe.matmul(PS[:, 4 + (c // 2) % 2, (c % 2) * 256:(c % 2) * 256 + 256],
                                         AR[hp:hp + 64, 4 + c // 2, h * P:(h + 1) * P],
                                         v[hp:hp + 64, c // 2, :], start=True, stop=True), t, l, "gkv", h, c)

                    kv(0)
                    kv(1)
                    for c in range(8):
                        if c % 2 == 0 and c + 2 < 8:
                            kv(c + 2)
                            kv(c + 3)
                        T.after((t, l, "state", h, c), (t, l, "o_out_read", h - 1) if h and c == 0 else None, own=False)
                        for e in range(2):
                            mm = pe.matmul(PS[:, 6 + e, c * 64:(c + 1) * 64],
                                           AR[:, 12, (c % 2) * 256 + e * P:(c % 2) * 256 + (e + 1) * P],
                                           AR[:, h, c * 64:(c + 1) * 64], start=True, stop=True)
                        T.done(mm, t, l, "g_out", h, c)
                    gemm(w["gv"] + 2 * h + 1, KD, 2, XH, XL, h_ready, lambda m: (t, l, "gr", h, m))
                    column_sums(lambda e: AR[:, 18 + e, :], 2, 4, lambda e: (t, l, "o_copied", h, e), [], (t, l, "o_mean", h))
                    if h + 1 < GLA_HEADS:
                        gemm_tok(w["gv"] + 2 * h + 2, h_ready, lambda m: (t, l, "gv", h + 1, m))
                    column_sums(lambda e: TMP[:, e, :], 2, 5, lambda e: (t, l, "o_sq", h, e), [], (t, l, "o_ms", h))
                bank_reader[4], bank_reader[5] = (t, l, "o_mean_read", 3), (t, l, "o_ms_read", 3)
                bank_reader[6] = bank_reader[7] = (t, l, "o_out_read", 3)
                mixer_gemms(l, w, t)
                for which in ("ln1", "ln2"):
                    if which == "ln2":
                        ffn(l, t, w["ff"], FF2_GROUPS, 2, *bases(t, l), lambda k: (t, l, "ln1_lo", k))
                    column_sums(lambda k: X[:, k, :], KD, 4, lambda k: (t, l, which + "_in", k), [bank_reader[4]],
                                (t, l, which + "_mean"))
                    column_sums(lambda k: TMP[:, k % 2, :], KD, 5, lambda k: (t, l, which + "_sq", k),
                                [bank_reader[5]], (t, l, which + "_ms"))
                    bank_reader[4] = (t, l, which + "_mean_read")
                    bank_reader[5] = (t, l, which + "_ms_read")


        @block.scalar
        def _(act):
            A = Steps(act, "act", sems["act"], marks, sems)

            def hi(c, k=0, i=0, used=None):
                if not k and c >= NPANELS:
                    return
                s = c % 2
                act.wait_ge(raw_full[s], 16 * (c // 2 + 1) + 8 * k * i)
                if used is not None:
                    act.wait_ge(*used)
                elif c >= 2:
                    who, n = marks.get(("panel", c - 2), ("pe", 1))
                    act.wait_ge(sems[who], n)
                act.activation(WH[:, s, :], RAW[:, s, :], ACT.Copy).then_inc(hi_ready, 1)

            def read(name, dst, func=ACT.Copy, *after, **kw):
                A.after(name, *after)
                b = kw.pop("bank")
                A.done(act.activation(dst, b, func, **kw), *(("read",) + name))

            tile = [0]

            def bank(cols=slice(0, S)):
                b = tile[0] % 4
                tile[0] += 1
                return PS[:, b, cols]

            def split_hi(dst, src, after, name):
                A.after(*after)
                A.done(act.activation(dst, src, ACT.Copy), *name)

            def squares(src, kt, dst, ready, used, name):
                for k in range(kt):
                    A.after(ready(k), used(k))
                    A.done(act.activation(dst(k), src(k), ACT.Square), *name, k)

            def root(ms, name, after):
                A.after(*after)
                A.done(act.activation(TMP[:, 3, :], TMP[:, 2, :], ACT.Sqrt), *name)

            def attention(units, l, t):
                def probabilities(u):
                    U, c = units[u], 8 * (u % 2)
                    A.after(U["id"] + ("negmax", u))
                    A.done(act.activation(TMP[:, u % 2, 0:U["nk"]], TMP[:, u % 2, 0:U["nk"]], ACT.Exp,
                                          bias=ST[:, c + 1:c + 2], scale=HD ** -0.5, accum_out=ST[:, c + 2:c + 3]),
                           *U["id"], "exp", u)
                    if U["sink"] is not None:
                        o = VA["sinks"] + U["sink"]
                        A.after()
                        A.done(act.activation(ST[:, c + 3:c + 4], VEC[:, l % 2, o:o + 1], ACT.Exp,
                                              bias=ST[:, c + 1:c + 2]), *U["id"], "exp", u)

                def evacuate(u):
                    U = units[u]
                    A.after(U["id"] + ("pt", u), U["id"] + ("o", u - 2) if u >= 2 else None)
                    A.done(act.activation(TMP[:, 2 + u % 2, 0:U["nk"]], PS[:, 6 + u % 2, 0:U["nk"]], ACT.Copy),
                           *U["id"], "pt_read", u)
                    A.after(U["id"] + ("o", u))
                    A.done(act.activation(U["o"], PS[0:64, 4 + u % 2, 0:P], ACT.Copy), *U["id"], "o_read", u)

                for u in range(len(units) + 1):
                    if u < len(units):
                        probabilities(u)
                    if u >= 1:
                        evacuate(u - 1)
                for j in range(4):
                    split_hi(YH[:, j, :], (AR[:, 14 + j, :] if t == "a" else AR[:, 8 + j, :]),
                             [], (t, l, "ao_hi", j))

            def skip_banks(n):
                tile[0] += n

            def mixer_gemms(l, w, t):
                for p in range(4):
                    hi(w["gb"] + p + 1)
                    for m in range(2):
                        read((t, l, "gb", 2 * p + m), SB[:, 2 * p + m, :], ACT.Sigmoid, (t, l, "arena_free"), bank=bank())
                if t == "b":
                    for k in range(KD):
                        A.after()
                        A.done(act.activation(X[:, k, :], X[:, k, :], ACT.Identity, scale=DN_ALPHA,
                                              bias=VEC[:, l % 2, VB["b_mix"] + k:VB["b_mix"] + k + 1]), t, l, "x_scaled", k)
                skip_banks(8)
                for p in range(4):
                    hi(w["wb"] + p + 1)
                    for m in range(2 * p, 2 * p + 2):
                        split_hi(XH[:, m, :], G[:, m, :], [(t, l, "merged", m)], (t, l, "merged_hi", m))
                skip_banks(8)
                for p in range(4):
                    hi(w["wo"] + p + 1)

            def ffn(l, t, ff, groups, kt, base_t, base_d, base_h):
                per = 2 + (2 if kt == 4 else 1)
                base_c = base_d - 8 * FF1_GROUPS * DEPTH if kt == 2 else 0
                base_c = base_c // 2
                downs = per - 2

                def up_used(g, p):
                    return up_full, base_t + 4 * g + 2 * (p + 1)

                def down_used(g, p):
                    return down_full, CREDIT + base_d + 8 * g + (8 // downs) * (p + 1)

                def hi_up(gc, gi, i, p):
                    g = gc + gi * i
                    if gi == 0 and gc == 1:
                        used = up_used(0, p)
                    elif downs == 2 or p == 1:
                        act.wait_ge(*up_used(g - 1, p))
                        used = down_used(g - 2, p if downs == 2 else 0)
                    else:
                        used = up_used(g - 1, 1)
                    hi(up_panel(ff, gc, per) + p, per * gi, i, used)

                def hi_down(gc, gi, i, p):
                    g = gc + gi * i
                    last = gi == 0 and gc == groups - 1
                    if downs == 2:
                        used = down_used(g - 1, p) if last else up_used(g + 1, p)
                    else:
                        used = up_used(g, 1) if last else up_used(g + 1, 0)
                    hi(down_panel(ff, gc, per, groups if gi == 0 else 99) + p, per * gi, i, used)

                def up(gc, gi, i, last=False):
                    g = gc + gi * i
                    t0 = base_t + 4 * g
                    buf = gc % 2
                    for p in range(2):
                        if p == 0:
                            if gi == 0 and gc == 0:
                                hi(ff + 1)
                            else:
                                hi_up(gc, gi, i, 1)
                        elif gi == 0 and gc == 0:
                            hi_up(1, 0, 0, 0)
                        else:
                            hi_down(gc - 1, gi, i, 0)
                        if kt == 2 and p == 1:
                            for m in range(2):
                                act.wait_ge(up_read, t0 + m + 1)
                                if not (gi == 0 and gc == 0):
                                    act.wait_ge(hid_ready, base_h + 2 * g + m - 1)
                                act.activation(AR[:, 4 + m, :], AR[:, m, :], ACT.Gelu_apprx_tanh).then_inc(gelu_done, 1)
                        for m in range(2):
                            j = 2 * p + m
                            act.wait_ge(up_full, t0 + j + 1)
                            if kt == 2:
                                if not (gi == 0 and gc == 0):
                                    if p == 0:
                                        act.wait_ge(gelu_done, base_c // 2 + 2 * g)
                                    else:
                                        act.wait_ge(hid_ready, base_h + 2 * g)
                                ch = 2 * g + m + (2 * FF2_GROUPS if p else 0)
                                tap, bias = VB["conv_w"] + 88 + ch, VB["conv_b"] + ch
                                act.activation(AR[:, j, :], PS[:, j, :], ACT.Identity, scale=VEC[:, l % 2, bass.ds(tap, 1)],
                                               bias=VEC[:, l % 2, bass.ds(bias, 1)]).then_inc(conv_begun, 1)
                            if kt == 4:
                                if not (gi == 0 and gc == 0 and base_t == 0):
                                    act.wait_ge(hid_ready, base_h + 4 * g + j - 3)
                                act.activation(AR[:, j, :], PS[:, j, :], ACT.Relu).then_inc(up_read, 1)
                        if kt == 4:
                            for m in range(2):
                                j = 2 * p + m
                                act.wait_ge(hid_ready, base_h + 4 * g + j + 1)
                                if not (gi == 0 and gc < 2):
                                    act.wait_ge(down_full, CREDIT + base_d + 8 * (g - 1))
                                act.activation(YH[:, 4 * buf + j, :], AR[:, 4 + j, :], ACT.Copy).then_inc(hid_hi, 1)
                    if kt == 2:
                        for m in range(2):
                            act.wait_ge(hid_ready, base_h + 2 * g + m + 1)
                            if not (gi == 0 and gc < 2):
                                act.wait_ge(down_full, CREDIT + base_d + 8 * (g - 1))
                            act.activation(YH[:, 2 * buf + m, :], AR[:, 6 + m, :], ACT.Copy).then_inc(hid_hi, 1)

                def down(gc, gi, i):
                    last = gi == 0 and gc == groups - 1
                    nxt_up = not (gi == 0 and gc >= groups - 2)
                    if downs == 2:
                        hi_down(gc, gi, i, 1)
                    if nxt_up:
                        hi_up(gc + 2, gi, i, 0)
                    elif not last:
                        hi_down(groups - 1, 0, 0, 0)
                    else:
                        hi(ff + per * groups)

                conv = up
                A.after()
                conv(0, 0, 0)
                trips = (groups - 1) // 2
                with act.Fori(0, trips) as i:
                    conv(1, 2, i)
                    down(0, 2, i)
                    conv(2, 2, i)
                    down(1, 2, i)
                for g in range(2 * trips, groups):
                    if g + 1 < groups:
                        conv(g + 1, 0, 0)
                    down(g, 0, 0)

            def norm(t, l, sfx, x_ready, gain, to_x=False):
                squares(lambda k: X[:, k, :], KD, lambda k: TMP[:, k % 2, :], lambda k: x_ready(k),
                        lambda k: (t, l, "ms" + sfx, k - 2) if k >= 2 else None, (t, l, "sq" + sfx))
                root(None, (t, l, "root" + sfx), [(t, l, "ms" + sfx + "_read")])
                for k in range(KD):
                    src = X[:, k, :] if to_x else TMP[:, k % 2, :]
                    hn = ("b", 0, "x_hi", k) if to_x else (t, l, "h" + sfx + "_hi", k)
                    split_hi(XH[:, k, :], src, [(t, l, "h" + sfx, k)], hn)

            hi(0)
            const_dma(act, X[:, :, :], x_in.rearrange("(k p) s -> p k s", p=P), "x_in")
            const_dma(act, CT[:, :], consts_in[0], "consts_a")
            const_dma(act, VEC[:, 0, :], vec_in[0], "vec0")
            const_dma(act, VEC[:, 1, :], vec_in[1], "vec1")
            for l in range(DEPTH):
                w, t = at_a(l), "a"
                if l:
                    A.after((t, l - 1, "roped", 12))
                const_dma(act, ROT[:, :, :], rot_in[0], ("rot", l, 0))
                norm(t, l, "", lambda k: "x_in" if l == 0 else (t, l - 1, "ffn_out"), None)
                for p in range(2):
                    hi(w["q"] + p + 1)
                    for m in range(2):
                        read((t, l, "q", 2 * p + m), AR[:, 2 * p + m, :], bank=bank())
                hi(w["kv"] + 1)
                read((t, l, "q", 4), AR[:, 4, :], bank=bank())
                read((t, l, "q", 5), AR[:, 18, :], bank=bank())
                A.after((t, l, "v_tok"))
                A.done(act.activation(AR[:, 5, :], PS[:, 6, :], ACT.Copy), t, l, "v_read")
                for p in range(4):
                    hi(w["rq"] + p + 1)
                    for m in range(2):
                        read((t, l, "rqk", 2 * p + m), AR[:, 6 + 2 * p + m, :], bank=bank())
                    if p == 0:
                        A.after((t, l, "roped", 4))
                        const_dma(act, ROT[:, :, :], rot_in[1], ("rot", l, 1))
                attention(units_a(l), l, t)
                for p in range(4):
                    hi(w["ga"] + p + 1)
                    for m in range(2):
                        read((t, l, "ga", 2 * p + m), G[:, 2 * p + m, :], ACT.Sigmoid, bank=bank())
                for p in range(2):
                    hi(w["wa"] + p + 1)
                skip_banks(8)

                def rv_read(h):
                    hi(w["rv"] + 2 * h + 1)
                    for m in range(2):
                        read((t, l, "rv", h, m), AR[:, 14 + 2 * (h % 2) + m, :], ACT.Copy, (t, l, "ao_lo", 3),
                             (t, l, "r_out", h - 2, 1) if h >= 2 else None, bank=bank())

                rv_read(0)
                for h in range(RET_HEADS):
                    A.after((t, l, "rkt", h), (t, l, "r_ms", h - 1) if h else (t, l, "o", 31))
                    z = CA["zeta"] + h
                    A.done(act.activation(TMP[:, 1, :], PS[:, 5, :], ACT.Copy, scale=CT[:, z:z + 1]), t, l, "kz", h)
                    hi(w["rv"] + 2 * h + 2)
                    for m in range(2):
                        read((t, l, "rg", h, m), AR[:, m, :], ACT.Silu, (t, l, "r_gated", h - 1, m) if h else None,
                             bank=bank())
                    if h + 1 < RET_HEADS:
                        rv_read(h + 1)
                    for e in range(2):
                        A.after((t, l, "r_out", h, 1))
                        A.done(act.activation(TMP[:, e, :], PS[:, 4 + e, :], ACT.Square), t, l, "r_sq", h, e)
                    for e in range(2):
                        A.after((t, l, "r_lo", 2 * h - 1) if h else None)
                        A.done(act.activation(AR[:, 18 + e, :], PS[:, 4 + e, :], ACT.Copy), t, l, "r_copied", h, e)
                    marks[(t, l, "r_out_read", h)] = ("act", A.n)
                    root(None, (t, l, "r_root", h), [(t, l, "r_ms_read", h)])
                    for e in range(2):
                        split_hi(YH[:, 2 * h + e, :], AR[:, 18 + e, :], [(t, l, "r_gated", h, e), (t, l, "wa", 7)],
                                 (t, l, "r_hi", 2 * h + e))
                marks[(t, l, "arena_free")] = marks.get((t, l, "r_gated", 3, 1), ("dve", 1))
                mixer_gemms(l, w, t)
                if l == DEPTH - 1:
                    const_dma(act, CT[:, 256:CW], consts_in[1, :, 256:CW], "consts_b")
                norm(t, l, "2", lambda k: ("read", t, l, "wo", k), None)
                ffn(l, t, w["ff"], FF1_GROUPS, 4, *bases(t, l))
                if l == 0:
                    const_dma(act, VEC[:, 0, :], vec_in[2], "vec2")
            norm("f", 0, "", lambda k: ("a", DEPTH - 1, "ffn_out"), None, to_x=True)
            const_dma(act, VEC[:, 1, :], vec_in[3], "vec3")

            for l in range(DEPTH):
                w, t = at_b(l), "b"
                pos = TMP[:, 3, :].bitcast(I32)
                A.after((t, l - 1, "ln2_ms_read") if l else None)
                const_dma(act, pos, pos_in, ("pos", l))
                const_dma(act, WG[:, :], wgate_in[l], ("w_gate", l))
                A.after((t, l, "angle"))
                A.done(act.activation(ROT[:, 1, :], TMP[:, 2, :], ACT.Sin))
                A.after()
                A.done(act.activation(TMP[:, 3, :], TMP[:, 2, :], ACT.Sin, scale=0.5), t, l, "sines")
                j = 0
                for n0, cnt in ((w["q"], 2), (w["k"], 2), (w["iq"], 2), (w["misc"], 1)):
                    for p in range(cnt):
                        hi(n0 + p + 1)
                        for m in range(2):
                            read((t, l, "q", j), AR[:, j if j < 13 else 18, :], bank=bank())
                            j += 1
                for u in range(24):
                    nk = (u // 8 + 2) * P
                    A.after((t, l, "dots", u), (t, l, "acc", u - 2) if u >= 2 else None)
                    A.done(act.activation(TMP[:, u % 2, 0:nk], PS[:, 4 + u % 2, 0:nk], ACT.Relu, scale=0.125),
                           t, l, "dots_read", u)

                def tok_read(n, name):
                    for p in range(2):
                        hi(n + p + 1)
                        for m in range(2):
                            u0 = (14 if name == "av" else 4) + 2 * m
                            A.after((t, l, name, p, m))
                            A.done(act.activation(AR[:, u0:u0 + 2, p * 256:(p + 1) * 256],
                                                  bank().rearrange("p (a b) -> p a b", a=2), ACT.Copy),
                                   "read", t, l, name, p, m)

                tok_read(w["v"], "av")
                for p in range(4):
                    hi(w["ga"] + p + 1)
                    for m in range(2):
                        read((t, l, "ga", 2 * p + m), G[:, 2 * p + m, :], ACT.Sigmoid, bank=bank())
                attention(units_b(l), l, t)
                for p in range(2):
                    hi(w["wa"] + p + 1)
                skip_banks(8)
                for n in range(NB):
                    A.after((t, l, "gate", n), (t, l, "la", n - 2) if n >= 2 else None)
                    A.done(act.activation(TMP[:, n % 2, :], PS[:, 4 + n % 2, :], ACT.Abs))
                    A.after()
                    A.done(act.activation(TMP[:, n % 2, :], TMP[:, n % 2, :], ACT.Exp, scale=-1.0))
                    A.after()
                    A.done(act.activation(TMP[:, n % 2, :], TMP[:, n % 2, :], ACT.Ln, bias=1.0), t, l, "soft", n)
                for p in range(2):
                    hi(w["gq"] + p + 1)
                    for m in range(2):
                        read((t, l, "gq", 2 * p + m), AR[:, 2 * p + m, :], bank=bank())
                tok_read(w["gk"], "gk")
                for n in range(NB):
                    A.after((t, l, "decay", n), (t, l, "kd", n - 2) if n >= 2 else (t, l, "la", 3))
                    A.done(act.activation(TMP[:, n % 2, :], PS[:, 4 + n % 2, :], ACT.Exp), t, l, "decay_read", n)
                A.after((t, l, "totals"))
                A.done(act.activation(ST[:, 64:96], PS[:, 6, 0:32], ACT.Exp), t, l, "totals_read")

                def gv_read(h):
                    hi(w["gv"] + 2 * h + 1)
                    for m in range(2):
                        read((t, l, "gv", h, m), AR[:, 14 + 2 * (h % 2) + m, :], ACT.Copy,
                             (t, l, "g_out", h - 2, 7) if h >= 2 else None, bank=bank())

                gv_read(0)
                for h in range(GLA_HEADS):
                    for e in range(2):
                        A.after((t, l, "g_out", h, 7), (t, l, "r_lo", 2 * h - 1) if h else None)
                        A.done(act.activation(AR[:, 18 + e, :], PS[:, 6 + e, :], ACT.Copy, scale=GLA_DK ** -0.5),
                               t, l, "o_copied", h, e)
                    marks[(t, l, "o_out_read", h)] = ("act", A.n)
                    hi(w["gv"] + 2 * h + 2)
                    for m in range(2):
                        read((t, l, "gr", h, m), AR[:, 8 + m, :], ACT.Silu, (t, l, "r_gated", h - 1, m) if h else None,
                             bank=bank())
                    for e in range(2):
                        A.after((t, l, "o_centered", h, e), (t, l, "kd", 3))
                        A.done(act.activation(TMP[:, e, :], AR[:, 18 + e, :], ACT.Square), t, l, "o_sq", h, e)
                    if h + 1 < GLA_HEADS:
                        gv_read(h + 1)
                    root(None, (t, l, "r_root", h), [(t, l, "o_ms_read", h)])
                    for e in range(2):
                        split_hi(YH[:, 2 * h + e, :], AR[:, 18 + e, :], [(t, l, "r_gated", h, e), (t, l, "wa", 7)],
                                 (t, l, "r_hi", 2 * h + e))
                marks[(t, l, "arena_free")] = marks.get((t, l, "r_gated", 3, 1), ("dve", 1))
                mixer_gemms(l, w, t)
                for which, gain in (("ln1", VB["ln1_g"]), ("ln2", VB["ln2_g"])):
                    squares(lambda k: X[:, k, :], KD, lambda k: TMP[:, k % 2, :], lambda k: (t, l, which + "_centered", k),
                            lambda k: (t, l, which + "_ms", k - 2) if k >= 2 else None, (t, l, which + "_sq"))
                    root(None, (t, l, which + "_root"), [(t, l, which + "_ms_read")])
                    for k in range(KD):
                        g = gain + k
                        A.after((t, l, which + "_scaled", k))
                        A.done(act.activation(X[:, k, :], X[:, k, :], ACT.Identity, scale=VEC[:, l % 2, g:g + 1],
                                              bias=VEC[:, l % 2, g + 8:g + 9]), t, l, which + "_x", k)
                        if which == "ln1":
                            split_hi(XH[:, k, :], X[:, k, :], [], (t, l, "ln1_hi", k))
                        elif l + 1 < DEPTH:
                            split_hi(XH[:, k, :], X[:, k, :], [], (t, l + 1, "x_hi", k))
                    if which == "ln1":
                        for k in range(KD):
                            A.after((t, l, "ln1_lo", k))
                            A.done(act.activation(X[:, k, :], X[:, k, :], ACT.Copy, scale=DN_ALPHA), t, l, "x2_scaled", k)
                        ffn(l, t, w["ff"], FF2_GROUPS, 2, *bases(t, l))
            marks["x_final"] = ("act", A.n)

        @block.vector
        def _(dve):
            V = Steps(dve, "dve", sems["dve"], marks, sems)
            dve.sem_inc(down_added, CREDIT)

            def lo(dst, src, high, after, name):
                V.after(*after)
                V.done(dve.tensor_tensor(dst, src, high.bitcast(F32), ALU.subtract), *name)

            def rope(x, ps, name, after):
                V.after(*after)
                V.done(dve.tensor_tensor(TMP[:, 2, :], ps, ROT[:, 1, :], ALU.mult))
                V.after()
                V.done(dve.tensor_tensor(x, x, ROT[:, 0, :], ALU.mult))
                V.after()
                V.done(dve.tensor_tensor(x, x, TMP[:, 2, :], ALU.add), *name)

            def mean_square(bank, n, eps, after, name):
                V.after(*after)
                V.done(dve.tensor_scalar(TMP[:, 2, :], PS[:, bank, :], 1.0 / n, eps, ALU.mult, ALU.add), *name)

            def inverse_root(after):
                V.after(*after)
                V.done(dve.reciprocal(TMP[:, 3, :], TMP[:, 3, :]))

            def norm(t, l, sfx, bank, gain, to_x=False, vec=()):
                mean_square(bank, D, EPS, [(t, l, "ms" + sfx, KD - 1)], (t, l, "ms" + sfx + "_read"))
                inverse_root([(t, l, "root" + sfx)])
                for k in range(KD):
                    dst = X[:, k, :] if to_x else TMP[:, k % 2, :]
                    hn = (lambda k: ("b", 0, "x_hi", k)) if to_x else (lambda k: (t, l, "h" + sfx + "_hi", k))
                    ln = (lambda k: ("b", 0, "x_lo", k)) if to_x else (lambda k: (t, l, "h" + sfx + "_lo", k))
                    V.after(hn(k - 2) if k >= 2 else None, *vec)
                    V.done(dve.scalar_tensor_tensor(dst, X[:, k, :], VEC[:, l % 2, gain + k:gain + k + 1] if not to_x else
                                                    VEC[:, 1, gain + k:gain + k + 1], TMP[:, 3, :], ALU.mult, ALU.mult),
                           t, l, "h" + sfx, k)
                    lo(XL[:, k, :], dst, XH[:, k, :], [hn(k)], ln(k))

            def attention(units, l, t):
                def maxima(u):
                    U, c = units[u], 8 * (u % 2)
                    s = TMP[:, u % 2, 0:U["nk"]]
                    V.after(U["id"] + ("s", u), U["id"] + ("pt", u - 2) if u >= 2 else None, (t, l, "mask", u // 8))
                    V.done(dve.scalar_tensor_tensor(s, U["mask"], U["weight"], PS[:, 4 + u % 2, 0:U["nk"]],
                                                    ALU.mult, ALU.add), *U["id"], "s_read", u)
                    V.after()
                    V.done(dve.tensor_reduce(ST[:, c:c + 1], s, AX, ALU.max))
                    V.after()
                    if U["sink"] is None:
                        V.done(dve.tensor_scalar(ST[:, c + 1:c + 2], ST[:, c:c + 1], -(HD ** -0.5), None, ALU.mult),
                               *U["id"], "negmax", u)
                    else:
                        k = 16 + U["sink"]
                        V.done(dve.tensor_scalar(ST[:, c + 1:c + 2], ST[:, c:c + 1], -(HD ** -0.5), ST[:, k:k + 1],
                                                 ALU.mult, ALU.min), *U["id"], "negmax", u)

                def normalise(u):
                    U, c = units[u], 8 * (u % 2)
                    s = TMP[:, u % 2, 0:U["nk"]]
                    V.after(U["id"] + ("exp", u))
                    if U["sink"] is not None:
                        V.done(dve.tensor_tensor(ST[:, c + 2:c + 3], ST[:, c + 2:c + 3], ST[:, c + 3:c + 4], ALU.add))
                        V.after()
                    V.done(dve.reciprocal(ST[:, c + 4:c + 5], ST[:, c + 2:c + 3]))
                    V.after()
                    V.done(dve.tensor_scalar(s, s, ST[:, c + 4:c + 5], None, ALU.mult), *U["id"], "p", u)

                for u in range(len(units) + 1):
                    if u < len(units):
                        maxima(u)
                    if u >= 1:
                        normalise(u - 1)
                for j in range(4):
                    lo(YL[:, j, :], AR[:, 14 + j, :] if t == "a" else AR[:, 8 + j, :], YH[:, j, :],
                       [(t, l, "ao_hi", j)], (t, l, "ao_lo", j))

            tile = [0]

            def bank():
                b = tile[0] % 4
                tile[0] += 1
                return PS[:, b, :]

            def branch_gate(l, t):
                for m in range(8):
                    V.after((t, l, "wa", m), ("read", t, l, "ga", m))
                    V.done(dve.tensor_tensor(G[:, m, :], G[:, m, :], bank(), ALU.mult), "read", t, l, "wa", m)

            def mixer_gemms(l, t):
                tile[0] += 8
                for m in range(8):
                    V.after((t, l, "wb", m), ("read", t, l, "gb", m))
                    V.done(dve.tensor_tensor(SB[:, m, :], SB[:, m, :], bank(), ALU.mult), "read", t, l, "wb", m)
                    V.after()
                    V.done(dve.tensor_tensor(G[:, m, :], G[:, m, :], SB[:, m, :], ALU.add), t, l, "merged", m)
                    lo(XL[:, m, :], G[:, m, :], XH[:, m, :], [(t, l, "merged_hi", m), (t, l, "gb", 7)],
                       (t, l, "merged_lo", m))
                for m in range(8):
                    V.after((t, l, "wo", m), (t, l, "x_scaled", m) if t == "b" else None)
                    V.done(dve.tensor_tensor(X[:, m, :], X[:, m, :], bank(), ALU.add), "read", t, l, "wo", m)
                    marks[(t, l, "ln1_in", m)] = ("dve", V.n)

            def ffn(l, t, groups, kt, base_t, base_d, base_h):
                base_c = (base_d - 8 * FF1_GROUPS * DEPTH) // 2 if kt == 2 else 0
                V.after(*[(t, l, "x2_scaled", k) for k in range(KD)] if kt == 2 else [])

                def up(gc, gi, i):
                    g = gc + gi * i
                    buf = gc % 2
                    first = gi == 0 and gc == 0
                    for p in range(2):
                        if kt == 2:
                            for m in range(2):
                                j = 2 * p + m
                                ch = 2 * g + m + (2 * FF2_GROUPS if p else 0)
                                for tap in (1, 2):
                                    n = S - tap
                                    wv = VEC[:, l % 2, bass.ds(VB["conv_w"] + 88 - 44 * tap + ch, 1)]
                                    if tap == 1:
                                        dve.wait_ge(conv_begun, base_c + 4 * g + j + 1)
                                    else:
                                        dve.wait_ge(tap_added, base_c + 4 * g + j + 1)
                                    ins = dve.scalar_tensor_tensor(AR[:, j, tap:S], PS[:, j, 0:n], wv, AR[:, j, tap:S],
                                                                   ALU.mult, ALU.add)
                                    ins.then_inc(tap_added if tap == 1 else up_read, 1)
                        if kt == 4:
                            for m in range(2):
                                j = 2 * p + m
                                dve.wait_ge(up_read, base_t + 4 * g + j + 1)
                                if not (first and base_h == 0):
                                    dve.wait_ge(hid_lo, base_h + 4 * g + j - 3)
                                dve.tensor_tensor(AR[:, 4 + j, :], AR[:, j, :], AR[:, j, :], ALU.mult)\
                                   .then_inc(hid_ready, 1)
                            for m in range(2):
                                j = 2 * p + m
                                dve.wait_ge(hid_hi, base_h + 4 * g + j + 1)
                                dve.tensor_tensor(YL[:, 4 * buf + j, :], AR[:, 4 + j, :], YH[:, 4 * buf + j, :].bitcast(F32),
                                                  ALU.subtract).then_inc(hid_lo, 1)
                    if kt == 2:
                        for m in range(2):
                            dve.wait_ge(gelu_done, base_c // 2 + 2 * g + m + 1)
                            dve.wait_ge(up_read, base_t + 4 * g + 3 + m)
                            if not first:
                                dve.wait_ge(hid_lo, base_h + 2 * g + m - 1)
                            dve.tensor_tensor(AR[:, 6 + m, :], AR[:, 4 + m, :], AR[:, 2 + m, :], ALU.mult)\
                               .then_inc(hid_ready, 1)
                        for m in range(2):
                            dve.wait_ge(hid_hi, base_h + 2 * g + m + 1)
                            dve.tensor_tensor(YL[:, 2 * buf + m, :], AR[:, 6 + m, :], YH[:, 2 * buf + m, :].bitcast(F32),
                                              ALU.subtract).then_inc(hid_lo, 1)

                def down(gc, gi, i):
                    g = gc + gi * i
                    for m in range(8):
                        dve.wait_ge(down_full, CREDIT + base_d + 8 * g + m + 1)
                        dve.wait_ge(down_added, CREDIT + base_d + 8 * g + m - 7)
                        dve.tensor_tensor(X[:, m, :], X[:, m, :], PS[:, 4 + m % 4, :], ALU.add).then_inc(down_added, 1)

                up(0, 0, 0)
                trips = (groups - 1) // 2
                with dve.Fori(0, trips) as i:
                    up(1, 2, i)
                    down(0, 2, i)
                    up(2, 2, i)
                    down(1, 2, i)
                for g in range(2 * trips, groups):
                    if g + 1 < groups:
                        up(g + 1, 0, 0)
                    down(g, 0, 0)
                dve.wait_ge(down_added, CREDIT + base_d + 8 * groups)

            for l in range(DEPTH):
                t = "a"
                V.after("vec%d" % l)
                o = VA["sinks"]
                V.done(dve.tensor_scalar(ST[:, 16:24], VEC[:, l % 2, o:o + 8], -1.0, None, ALU.mult))
                for b in range(4):
                    marks[(t, l, "mask", b)] = marks.get("consts_a", ("const", 16))
                norm(t, l, "", 4, VA["g_mix"])
                tile[0] += 6
                for j in range(5):
                    rope(AR[:, j, :], PS[:, 4 + j % 2, :], (t, l, "roped", j), [(t, l, "swap", j), ("rot", l, 0)])
                tile[0] += 8
                for j in range(8):
                    rope(AR[:, 6 + j, :], PS[:, 4 + j % 2, :], (t, l, "roped", 5 + j), [(t, l, "swap", 5 + j), ("rot", l, 1)])
                attention(units_a(l), l, t)
                tile[0] += 8
                branch_gate(l, t)
                for h in range(RET_HEADS):
                    dec, xi = CA["decay"] + h * P, CA["xi"] + h * P

                    def per_chunk(c0):
                        return CT[:, c0:c0 + P].unsqueeze(1).broadcast_to([P, NB, P])

                    def chunks(ap):
                        return ap.rearrange("p (c i) -> p c i", c=NB)

                    V.after((t, l, "rs", h), (t, l, "r_ms", h - 1) if h else (t, l, "o", 31))
                    V.done(dve.tensor_tensor(chunks(TMP[:, 0, :]), chunks(PS[:, 4, :]), per_chunk(dec), ALU.mult),
                           t, l, "rs_decayed", h)
                    V.after((t, l, "r_root", h - 1) if h else None)
                    V.done(dve.tensor_tensor(chunks(TMP[:, 2, :]), chunks(AR[:, 6 + h, :]), per_chunk(xi), ALU.mult),
                           t, l, "qx", h)
                    g_chunk = float(np.exp(np.log1p(-2.0 ** (-5.0 - h)) * P))
                    flat = AR[:, 4:6, :].rearrange("p a s -> p (a s)")
                    V.after((t, l, "kv", h))
                    V.done(dve.tensor_copy(flat[:, 0:256], PS[:, 6, 0:256]), t, l, "state", h, 1)
                    for c in (1, 2):
                        ps = PS[:, 6, 256:512] if c == 1 else PS[:, 7, 0:256]
                        V.after()
                        V.done(dve.scalar_tensor_tensor(flat[:, 256 * c:256 * c + 256], flat[:, 256 * c - 256:256 * c], g_chunk,
                                                        ps, ALU.mult, ALU.add), t, l, "state", h, c + 1)
                    mean_square(6, RET_V, EPS, [(t, l, "r_ms", h)], (t, l, "r_ms_read", h))
                    inverse_root([(t, l, "r_root", h)])
                    for e in range(2):
                        V.after((t, l, "r_copied", h, e))
                        V.done(dve.tensor_tensor(AR[:, 18 + e, :], AR[:, 18 + e, :], TMP[:, 3, :], ALU.mult))
                        V.after(("read", t, l, "rg", h, e))
                        V.done(dve.tensor_tensor(AR[:, 18 + e, :], AR[:, 18 + e, :], AR[:, e, :], ALU.mult),
                               t, l, "r_gated", h, e)
                    for e in range(2):
                        lo(YL[:, 2 * h + e, :], AR[:, 18 + e, :], YH[:, 2 * h + e, :], [(t, l, "r_hi", 2 * h + e)],
                           (t, l, "r_lo", 2 * h + e))
                tile[0] += 2 * RET_HEADS * 2
                mixer_gemms(l, t)
                norm(t, l, "2", 6, VA["g_mlp"])
                ffn(l, t, FF1_GROUPS, 4, *bases(t, l))
            norm("f", 0, "", 4, VB["g_final"], to_x=True)

            for l in range(DEPTH):
                t = "b"
                V.after(("pos", l), "consts_b", "vec2" if l == 0 else "vec3", (t, l - 1, "ln2_x", KD - 1) if l else None)
                V.done(dve.tensor_copy(TMP[:, 2, :], TMP[:, 3, :].bitcast(I32)))
                V.after()
                V.done(dve.tensor_scalar(TMP[:, 2, :], TMP[:, 2, :], CT[:, 514:515], None, ALU.mult))
                V.after()
                V.done(dve.tensor_scalar(TMP[:, 3, :], TMP[:, 2, :], 1.0 / (2 * np.pi), 12582912.0, ALU.mult, ALU.add))
                V.after()
                V.done(dve.tensor_scalar(TMP[:, 3, :], TMP[:, 3, :], 12582912.0, None, ALU.subtract))
                for part in (6.28125, 2 * np.pi - 6.28125):
                    V.after()
                    V.done(dve.scalar_tensor_tensor(TMP[:, 2, :], TMP[:, 3, :], -part, TMP[:, 2, :], ALU.mult, ALU.add))
                V.after()
                V.done(dve.tensor_scalar(TMP[:, 2, :], TMP[:, 2, :], -3.1415925, 3.1415925, ALU.max, ALU.min), t, l, "angle")
                V.after((t, l, "sines"))
                V.done(dve.tensor_scalar(ROT[:, 1, :], ROT[:, 1, :], CT[:, 515:516], None, ALU.mult))
                V.after()
                V.done(dve.tensor_tensor(TMP[:, 3, :], TMP[:, 3, :], TMP[:, 3, :], ALU.mult))
                V.after()
                V.done(dve.tensor_scalar(ROT[:, 0, :], TMP[:, 3, :], -2.0, 1.0, ALU.mult, ALU.add), t, l, "rot_tables")
                for j in range(13):
                    rope(AR[:, j, :], PS[:, 4 + j % 2, :], (t, l, "roped", j), [(t, l, "swap", j)])
                tile[0] += 14
                iw = ST[:, 32:64].rearrange("p (n h) -> p n h", n=NB)
                V.after((t, l, "iw"))
                V.done(dve.tensor_scalar(iw, PS[:, 6, :].rearrange("p (n c) -> p n c", n=NB)[:, :, 32:40], 8 ** -0.5, None,
                                         ALU.mult), t, l, "iw_read")
                V.after()
                V.done(dve.memset(AR[0:32, 13, :], 1.0))
                V.after()
                V.done(dve.tensor_copy(AR[0:16, 13, :], AR[0:16, 18, :]), t, l, "glr")
                V.after()
                m0 = mask_b(0)
                V.done(dve.memset(m0, 0.0))
                V.after()
                V.done(dve.memset(m0[0:64, 64:128], -1.0), t, l, "mask", 0)
                for b in range(1, NB):
                    sc = mask_b(b)
                    for h in range(8):
                        u = 8 * (b - 1) + h
                        src = TMP[:, u % 2, 0:(b + 1) * P]
                        V.after((t, l, "dots_read", u))
                        wcol = ST[:, 32 + 8 * b + h:33 + 8 * b + h]
                        if h == 0:
                            V.done(dve.tensor_scalar(sc, src, wcol, None, ALU.mult), t, l, "acc", u)
                        else:
                            V.done(dve.scalar_tensor_tensor(sc, src, wcol, sc, ALU.mult, ALU.add), t, l, "acc", u)
                    V.after()
                    V.done(dve.memset(sc[0:64, b * P + 64:(b + 1) * P], NEG))
                for b in range(1, NB):
                    sc, other, best = mask_b(b), TMP[:, 3, 0:(b + 1) * P], ST[:, 24:32]
                    for r in range(TOPK // 8):
                        src, dst = (sc, other) if r % 2 == 0 else (other, sc)
                        V.after()
                        V.done(dve.max(best, src))
                        V.after()
                        V.done(dve.match_replace(dst, best, src, TAKEN))
                    V.after()
                    V.done(dve.tensor_scalar(sc, sc, TAKEN, 1.0, ALU.is_equal, ALU.subtract), t, l, "mask", b)
                tile[0] += 4 + 8
                attention(units_b(l), l, t)
                branch_gate(l, t)
                for n in range(NB):
                    V.after((t, l, "soft", n), (t, l, "ao_hi", 3))
                    V.done(dve.scalar_tensor_tensor(AR[:, 8 + n, :], PS[:, 4 + n % 2, :], 0.0, TMP[:, n % 2, :],
                                                    ALU.min, ALU.subtract), t, l, "la", n)
                for n in range(NB):
                    V.after((t, l, "decay_read", n), *[("read", t, l, "gk", p, n // 2) for p in range(2)])
                    V.done(dve.tensor_tensor(AR[:, 4 + n, :], AR[:, 4 + n, :], TMP[:, n % 2, :], ALU.mult), t, l, "kd", n)
                tile[0] += 4 + 4
                for h in range(GLA_HEADS):
                    for c in range(8):
                        ps = PS[:, 4 + (c // 2) % 2, (c % 2) * 256:(c % 2) * 256 + 256]
                        new, old = AR[:, 12, (c % 2) * 256:(c % 2) * 256 + 256], AR[:, 12, ((c + 1) % 2) * 256:((c + 1) % 2) * 256 + 256]
                        V.after((t, l, "gkv", h, c | 1), (t, l, "totals_read"),
                                (t, l, "g_out", h, c - 2) if c >= 2 else ((t, l, "g_out", h - 1, c + 6) if h else None))
                        if c == 0:
                            V.done(dve.tensor_copy(new, ps), t, l, "state", h, c)
                        else:
                            V.done(dve.scalar_tensor_tensor(new, old, ST[:, 64 + 8 * h + c:65 + 8 * h + c], ps,
                                                            ALU.mult, ALU.add), t, l, "state", h, c)
                    for e in range(2):
                        V.after((t, l, "o_mean", h), (t, l, "o_copied", h, e))
                        V.done(dve.scalar_tensor_tensor(AR[:, 18 + e, :], PS[:, 4, :], -1.0 / GLA_DV, AR[:, 18 + e, :],
                                                        ALU.mult, ALU.add), t, l, "o_centered", h, e)
                    marks[(t, l, "o_mean_read", h)] = ("dve", V.n)
                    mean_square(5, GLA_DV, LN_EPS, [(t, l, "o_ms", h)], (t, l, "o_ms_read", h))
                    inverse_root([(t, l, "r_root", h)])
                    for e in range(2):
                        g = VB["gla_g"] + 2 * h + e
                        V.after((t, l, "o_sq", h, e))
                        V.done(dve.scalar_tensor_tensor(AR[:, 18 + e, :], AR[:, 18 + e, :], VEC[:, l % 2, g:g + 1],
                                                        TMP[:, 3, :], ALU.mult, ALU.mult))
                        V.after(("read", t, l, "gr", h, e))
                        V.done(dve.tensor_tensor(AR[:, 18 + e, :], AR[:, 18 + e, :], AR[:, 8 + e, :], ALU.mult),
                               t, l, "r_gated", h, e)
                    for e in range(2):
                        lo(YL[:, 2 * h + e, :], AR[:, 18 + e, :], YH[:, 2 * h + e, :], [(t, l, "r_hi", 2 * h + e)],
                           (t, l, "r_lo", 2 * h + e))
                tile[0] += 2 * GLA_HEADS * 2
                mixer_gemms(l, t)
                for which in ("ln1", "ln2"):
                    if which == "ln2":
                        ffn(l, t, FF2_GROUPS, 2, *bases(t, l))
                        for k in range(KD):
                            marks[(t, l, "ln2_in", k)] = marks.get((t, l, "ffn_out"), ("dve", 1))
                    for k in range(KD):
                        V.after((t, l, which + "_mean"))
                        V.done(dve.scalar_tensor_tensor(X[:, k, :], PS[:, 4, :], -1.0 / D, X[:, k, :], ALU.mult, ALU.add),
                               t, l, which + "_centered", k)
                    marks[(t, l, which + "_mean_read")] = ("dve", V.n)
                    mean_square(5, D, LN_EPS, [(t, l, which + "_ms")], (t, l, which + "_ms_read"))
                    inverse_root([(t, l, which + "_root")])
                    for k in range(KD):
                        V.after((t, l, which + "_sq", k))
                        V.done(dve.tensor_tensor(X[:, k, :], X[:, k, :], TMP[:, 3, :], ALU.mult), t, l, which + "_scaled", k)
                    for k in range(KD):
                        if which == "ln1":
                            lo(XL[:, k, :], X[:, k, :], XH[:, k, :], [(t, l, "ln1_hi", k)], (t, l, "ln1_lo", k))
                        elif l + 1 < DEPTH:
                            lo(XL[:, k, :], X[:, k, :], XH[:, k, :], [(t, l + 1, "x_hi", k)], (t, l + 1, "x_lo", k))


def kernel(**inputs):
    import concourse.bacc as bacc
    from concourse.bass_utils import run_bass_kernel_spmd

    i = {k: np.asarray(v) for k, v in inputs.items()}
    consts, rot = _constants()
    wgate = np.zeros((DEPTH, 32, S), np.float32)
    for l in range(DEPTH):
        wgate[l, 0:GLA_RANK] = i["gla_w_gate_2"][l]
        wgate[l, GLA_RANK] = i["gla_b_gate_2"][l]
    arrays = {
        "stream": _stream(i), "x_t": np.ascontiguousarray(i["x"][0].T), "consts": consts, "rot": rot,
        "vectors": _vectors(i), "w_gate_in": wgate,
        "pos": np.ascontiguousarray(np.broadcast_to(i["positions_2"].astype(np.int32), (P, S))),
    }

    def build(marks):
        nc = bacc.Bacc("TRN2", target_bir_lowering=False, num_devices=1)
        args = [nc.dram_tensor(n, a.shape, mybir.dt.from_np(a.dtype), kind="ExternalInput").ap() for n, a in arrays.items()]
        args.append(nc.dram_tensor("y_t", (D, S), F32, kind="ExternalOutput").ap())
        program(nc, *args, marks)
        return nc

    marks = {}
    build(marks)
    marks["complete"] = True
    nc = build(marks)
    r = run_bass_kernel_spmd(nc, [arrays], core_ids=[0])
    return np.ascontiguousarray(r.results[0]["y_t"].T)[None]
```

```python
from contextlib import ExitStack

import numpy as np

import concourse.bass as bass
from concourse import mybir

F32 = mybir.dt.float32
F32R = mybir.dt.float32r
I32 = mybir.dt.int32
ALU = mybir.AluOpType
ACT = mybir.ActivationFunctionType
AX = mybir.AxisListType.X

P = 128
D = 1024
S = 512
DEPTH = 2
KD = D // P
NB = S // P
EPS = 1e-6
LN_EPS = 1e-5
NEG = -1.0e30
TAKEN = -3.0e38
PANEL = 2048

HD = 64
WINDOW = 128
RET_HEADS, RET_QK, RET_V = 4, 128, 256
D_FF = 4 * D
FF1_GROUPS = 8
TOPK = min(256, S // 4)
GLA_HEADS, GLA_DK, GLA_DV, GLA_RANK, GLA_TAU = 4, 128, 256, 16, 16.0
D_FF2 = 2816
FF2_GROUPS = D_FF2 // (2 * P)
DN_ALPHA = (2.0 * DEPTH) ** 0.25

NPA = 33 + 4 * FF1_GROUPS
NPB = 39 + 3 * FF2_GROUPS
NPANELS = DEPTH * (NPA + NPB)
CREDIT = 8


def _panel(rows):
    kt = rows.shape[0] // P
    return rows.reshape(kt, P, rows.shape[1]).transpose(1, 0, 2).reshape(P, -1)


def _cols(w, n=256):
    return [_panel(w[:, c:c + n]) for c in range(0, w.shape[1], n)]


def _stream(i):
    out = []
    for l in range(DEPTH):
        w = i["w_in"][l]
        q, k, v, rq, rk, rv, rg, ga, gb = np.split(w, [512, 640, 768, 1280, 1792, 2816, 3840, 4864], axis=1)
        q = q.reshape(D, 2, 4, HD).transpose(0, 2, 1, 3).reshape(D, 512)
        wa = i["w_a"][l].reshape(2, 4, HD, D).transpose(1, 0, 2, 3).reshape(512, D)
        qp = _cols(q)
        out += [qp[0], _panel(np.concatenate([k, v], 1)), qp[1]] + _cols(rq) + _cols(rk) + _cols(ga)
        out += _cols(wa, 512)
        rvp, rgp = _cols(rv), _cols(rg)
        for h in range(RET_HEADS):
            out += [rvp[h], rgp[h]]
        out += _cols(gb) + _cols(i["w_b"][l]) + _cols(i["w_out"][l])
        up = _cols(i["w_up"][l])
        down = [p for g in range(FF1_GROUPS) for p in _cols(i["w_down"][l][g * 512:(g + 1) * 512], 512)]
        out += up[0:2]
        for g in range(FF1_GROUPS):
            out += up[2 * g + 2:2 * g + 4] + down[2 * g:2 * g + 2]
    for l in range(DEPTH):
        w = i["w_in_2"][l]
        aq, ak, av, iq, ik, iw, gq, gk, gv, glr, gr, ga, gb = np.split(
            w, [512, 1024, 1536, 2048, 2112, 2120, 2632, 3144, 4168, 4184, 5208, 6232], axis=1)
        z = np.zeros((D, 1), np.float32)
        misc = np.concatenate([ik, ik, glr, np.repeat(z, 16, 1), iw, np.repeat(z, 88, 1)], axis=1)
        out += _cols(aq) + _cols(ak) + _cols(iq) + [_panel(misc)] + _cols(av) + _cols(ga)
        out += _cols(gq) + _cols(i["p_attn_2"][l], 512) + _cols(gk)
        gvp, grp = _cols(gv), _cols(gr)
        for h in range(GLA_HEADS):
            out += [gvp[h], grp[h]]
        out += _cols(gb) + _cols(i["p_gla_2"][l]) + _cols(i["w_mix_out_2"][l])
        up, down = i["w_up_2"][l], i["w_down_2"][l]
        a, b = _cols(up[:, :D_FF2]), _cols(up[:, D_FF2:])
        dn = [_panel(down[g * 256:(g + 1) * 256]) for g in range(FF2_GROUPS)]
        out += [a[0], b[0]]
        for g in range(FF2_GROUPS):
            if g + 1 < FF2_GROUPS:
                out += [a[g + 1], b[g + 1]]
            out += [dn[g]]
    assert len(out) == NPANELS
    return np.stack(out)


def _tiles(v):
    return v.reshape(-1, P).T


VA = dict(g_mix=0, g_mlp=8, sinks=16)
VB = dict(gla_g=0, b_mix=8, ln1_g=16, ln1_b=24, ln2_g=32, ln2_b=40, conv_b=48, conv_w=92, g_final=224)
VW = 232


def _vectors(i):
    out = np.zeros((2 * DEPTH, P, VW), np.float32)
    for l in range(DEPTH):
        a, b = out[l], out[DEPTH + l]
        a[:, 0:8] = _tiles(i["g_mix"][l])
        a[:, 8:16] = _tiles(i["g_mlp"][l])
        a[:, 16:24] = np.broadcast_to(i["sinks"][l].reshape(2, 4).T.reshape(1, 8), (P, 8))
        a[:, 224:232] = b[:, 224:232] = _tiles(i["g_final"])
        for name, at in (("gla_norm_g_2", 0), ("b_mix_out_2", 8), ("ln1_g_2", 16), ("ln1_b_2", 24),
                         ("ln2_g_2", 32), ("ln2_b_2", 40), ("conv_b_2", 48)):
            t = _tiles(i[name][l])
            b[:, at:at + t.shape[1]] = t
        for c in range(3):
            b[:, 92 + 44 * c:92 + 44 * (c + 1)] = _tiles(i["conv_w_2"][l, c])
    return out


CA = dict(ident=0, ones=128, perm_a=256, perm_r=384, decay=512, xi=1024, zeta=1536, mask=1540)
CB = dict(ident=0, ones=128, perm_b=256, later=384, total=512, inv=514)
CW = 1796


def _swap(pairs):
    m = np.zeros((P, P), np.float32)
    for to, of in pairs:
        m[of, to] = 1.0
    return m


def _constants():
    f = np.float32
    a, b = np.zeros((P, CW), f), np.zeros((P, CW), f)
    for c in (a, b):
        c[:, 0:128] = np.eye(P)
        c[:, 128:256] = 1.0
    half = HD // 2
    a[:, 256:384] = _swap([(r, (r // HD) * HD + (r % HD + half) % HD) for r in range(P)])
    a[:, 384:512] = _swap([(r, r ^ 1) for r in range(P)])
    idx = np.arange(P)
    scale = RET_QK ** -0.5
    for h in range(RET_HEADS):
        lg = np.log1p(-2.0 ** (-5.0 - h))
        rel = idx[None, :] - idx[:, None]
        a[:, 512 + h * P:512 + (h + 1) * P] = np.where(rel >= 0, np.exp(lg * np.maximum(rel, 0)), 0.0) * scale
        a[:, 1024 + h * P:1024 + (h + 1) * P] = np.exp(lg * (idx + 1.0))[None, :]
        a[:, 1536 + h] = np.exp(lg * (P - 1.0 - idx)) * scale
    a[:, 1540:1668] = np.where(idx[None, :] > idx[:, None], 0.0, NEG)
    a[:, 1668:1796] = np.where(idx[None, :] <= idx[:, None], 0.0, NEG)
    b[:, 256:384] = _swap([(r, r // 64 * 64 + (r % 64 + 8) % 16) if r % 64 < 16 else (r, r) for r in range(P)])
    t = np.arange(P)
    b[:, 384:512] = ((t[:, None] > t[None, :]) & (t[:, None] // 64 == t[None, :] // 64)) / GLA_TAU
    b[:, 512:514] = (t[:, None] // 64 == np.arange(2)[None, :]) / GLA_TAU
    inv = np.power(f(500000.0), -np.arange(8, dtype=f) * f(2.0) / f(16.0)).astype(f)
    b[:, 514] = [inv[r % 64 % 8] if r % 64 < 16 else 0.0 for r in range(P)]
    b[:, 515] = [(-1.0 if r % 64 < 8 else 1.0) for r in range(P)]
    rot = np.zeros((2, P, 2, S), f)
    pos = np.arange(S, dtype=f)
    inv = np.power(f(10000.0), -np.arange(half, dtype=f) / f(half)).astype(f)
    ang = (pos[None, :] * inv[np.arange(P) % half][:, None]).astype(f).astype(np.float64)
    sign = np.where(np.arange(P) % HD < half, -1.0, 1.0)[:, None]
    rot[0, :, 0], rot[0, :, 1] = np.cos(ang), np.sin(ang) * sign
    theta = (f(1.0) / np.power(f(10000.0), np.linspace(0.0, 1.0, RET_QK // 2, dtype=f))).astype(f)
    ang = (pos[None, :] * theta[np.arange(P) // 2][:, None]).astype(f).astype(np.float64)
    sign = np.where(np.arange(P) % 2 == 0, -1.0, 1.0)[:, None]
    rot[1, :, 0], rot[1, :, 1] = np.cos(ang), np.sin(ang) * sign
    return np.stack([a, b]), rot


class Steps:

    def __init__(self, eng, name, sem, marks, sems):
        self.eng, self.name, self.sem, self.marks, self.sems = eng, name, sem, marks, sems
        self.n = 0

    def after(self, *names, own=True):
        need = {}
        for name in names:
            if name is None or (name not in self.marks and not self.marks.get("complete")):
                continue
            who, n = self.marks[name]
            need[who] = max(need.get(who, 0), n)
        if own:
            need[self.name] = self.n
        for who, n in need.items():
            if n > 0:
                self.eng.wait_ge(self.sems[who], n)

    def done(self, instruction, *name):
        instruction.then_inc(self.sem, 1)
        self.n += 1
        if name:
            self.marks[name if len(name) > 1 else name[0]] = (self.name, self.n)


def program(nc, stream, x_in, consts_in, rot_in, vec_in, wgate_in, pos_in, out, marks):
    ctx = ExitStack()
    with ctx:
        def sb(name, shape, dt=F32):
            return ctx.enter_context(nc.sbuf_tensor(name, shape, dt))

        def sem(name):
            return ctx.enter_context(nc.semaphore(name))

        X = sb("x", [P, KD, S])
        XH, XL = sb("x_hi", [P, KD, S], F32R), sb("x_lo", [P, KD, S], F32R)
        with nc.sbuf_tensor("scratch", [P, 2 * KD, S], F32) as scratch:
            YSCR = scratch
        YH, YL = sb("y_hi", [P, KD, S], F32R), sb("y_lo", [P, KD, S], F32R)
        WH, WL = sb("w_hi", [P, 2, PANEL], F32R), sb("w_lo", [P, 2, PANEL], F32R)
        RAW = sb("w_raw", [P, 2, PANEL])
        AR = sb("arena", [P, 28, S])
        TMP = sb("tmp", [P, 4, S])
        CT = sb("ct", [P, CW])
        ROT = sb("rotary", [P, 2, S])
        VEC = sb("vec", [P, 2, VW])
        ST = sb("stats", [P, 96])
        WG = sb("w_gate", [32, S])
        PS = ctx.enter_context(nc.psum_tensor("ps", [P, 8, S], F32))

        raw_full = [sem("raw_full0"), sem("raw_full1")]
        hi_ready, lo_ready = sem("hi_ready"), sem("lo_ready")
        const_loaded, stored = sem("const_loaded"), sem("stored")
        up_full, down_full, down_added = sem("up_full"), sem("down_full"), sem("down_added")
        sems = dict(pe=sem("pe_done"), act=sem("act_done"), dve=sem("dve_done"), const=const_loaded,
                    down_full=down_full, down_added=down_added)
        up_read, hid_ready, hid_hi, hid_lo = sem("up_read"), sem("hid_ready"), sem("hid_hi"), sem("hid_lo")
        conv_begun, tap_added, gelu_done = sem("conv_begun"), sem("tap_added"), sem("gelu_done")
        block = ctx.enter_context(nc.Block())

        def unit(a, n=1):
            return AR[:, a:a + n, :]

        G = unit(20, 8)
        SB = unit(0, 8)
        n_consts = [0]

        def const_dma(eng, dst, src, name):
            if n_consts[0]:
                eng.wait_ge(const_loaded, 16 * n_consts[0])
            eng.dma_start(dst, src).then_inc(const_loaded, 16)
            n_consts[0] += 1
            marks[name] = ("const", 16 * n_consts[0])

        @block.sync
        def _(sp):
            with sp.Fori(0, NPANELS // 2) as i:
                for s in range(2):
                    sp.wait_ge(lo_ready, 2 * i + s + 1)
                    sp.dma_start(RAW[:, s, :], stream[bass.ds(2 * i + s, 1), :, :].rearrange("o p n -> p (o n)"))\
                        .then_inc(raw_full[s], 16)
            sp.wait_ge(sems["act"], marks.get("x_final", ("act", 1))[1])
            sp.dma_start(out.rearrange("(k p) s -> p k s", p=P), X[:, :, :]).then_inc(stored, 16)
            sp.wait_ge(stored, 16)

        @block.gpsimd
        def _(pool):
            pool.sem_inc(lo_ready, 2)
            with pool.Fori(0, NPANELS // 2) as i:
                for s in range(2):
                    pool.wait_ge(hi_ready, 2 * i + s + 1)
                    nc.gpsimd.tensor_tensor(WL[:, s, :], RAW[:, s, :], WH[:, s, :].bitcast(F32), ALU.subtract)\
                        .then_inc(lo_ready, 1)

        def at_a(l):
            n = NPA * l
            return dict(q=n, kv=n + 1, rq=n + 3, rk=n + 5, ga=n + 7, wa=n + 11, rv=n + 13, gb=n + 21, wb=n + 25,
                        wo=n + 29, ff=n + 33)

        def at_b(l):
            n = DEPTH * NPA + NPB * l
            return dict(q=n, k=n + 2, iq=n + 4, misc=n + 6, v=n + 7, ga=n + 9, gq=n + 13, wa=n + 15, gk=n + 17,
                        gv=n + 19, gb=n + 27, wb=n + 31, wo=n + 35, ff=n + 39)

        def bases(t, l):
            if t == "a":
                return 4 * FF1_GROUPS * l, 8 * FF1_GROUPS * l, 4 * FF1_GROUPS * l
            g1, g2 = FF1_GROUPS * DEPTH, FF2_GROUPS * l
            return 4 * (g1 + g2), 8 * (g1 + g2), 4 * g1 + 2 * g2

        def mask_b(b):
            if b == 3:
                return ROT[:, 0, :]
            o = 18 * S + (0, 128, 384)[b]
            return AR[:, :, :].rearrange("p a s -> p (a s)")[:, o:o + (b + 1) * P]

        def pairs_a(l):
            out = []
            for i in range(16):
                n, j = i // 4, i % 4
                k0, nk = max(n - 1, 0), min(n + 1, 2)
                out.append(dict(nk=nk * P, q=AR[:, j, n * P:(n + 1) * P], k=AR[:, 4, k0 * P:(k0 + nk) * P],
                                v=lambda kb, k0=k0: AR[:, 5, (k0 + kb) * P:(k0 + kb + 1) * P],
                                mask=CT[:, 1796 - nk * P:1796], weight=1.0, sink=2 * j,
                                ready=[("a", l, "v_read"), ("a", l, "roped", 4)],
                                o=AR[:, 14 + j, n * P:(n + 1) * P]))
            return out

        def pairs_b(l):
            out = []
            for i in range(16):
                b, j = i // 4, i % 4
                out.append(dict(nk=(b + 1) * P, q=AR[:, j, b * P:(b + 1) * P], k=AR[:, 4 + j, 0:(b + 1) * P],
                                v=lambda kb, j=j: AR[:, 14 + kb, 2 * j * 64:(2 * j + 2) * 64],
                                mask=mask_b(b), weight=-NEG, sink=None,
                                ready=[("b", l, "mask", b)] + [("read", "b", l, "av", p, m) for p in range(2) for m in range(2)],
                                o=AR[:, 8 + j, b * P:(b + 1) * P]))
            return out

        def probs(i, nk):
            return TMP[:, 2 * (i % 2):2 * (i % 2) + 2, 0:nk]

        def probs_t(i, nk):
            a = 4 + 2 * (i % 2)
            return YSCR[:, a:a + 2, 0:nk]

        def run(work, n=1):
            for _ in range(n):
                next(work, None)

        def bank_of(*name):
            return PS[:, marks.get(("bank",) + name, 0), :]

        def up_panel(ff, g, per):
            return ff if isinstance(g, int) and g == 0 else ff + 2 + per * (g - 1)

        def down_panel(ff, g, per, groups):
            if isinstance(g, int) and g == groups - 1:
                return ff + 2 + per * (groups - 1)
            return ff + 4 + per * g

        @block.tensor
        def _(pe):
            T = Steps(pe, "pe", sems["pe"], marks, sems)
            pe.sem_inc(down_full, CREDIT)
            bank_reader = [None] * 8
            tile = [0]
            ring = [4]

            def next_bank(name):
                b = tile[0] % ring[0]
                tile[0] += 1
                marks[("bank",) + name] = b
                return b

            def split_products(ps, k, last, wh, wl, xh, xl):
                pe.matmul(ps, wh, xh, start=(k == 0), stop=False)
                pe.matmul(ps, wh, xl, start=False, stop=False)
                return pe.matmul(ps, wl, xh, start=False, stop=last)

            def gemm_tiles(n, kt, ms, xh, xl, ready, name):
                s = n % 2
                pe.wait_ge(lo_ready, n + 3)
                for m in range(ms):
                    b = next_bank(name(m))
                    T.after(bank_reader[b], own=False)
                    for k in range(kt):
                        if m == 0:
                            T.after(ready(k), own=False)
                        c = (k * ms + m) * P
                        mm = split_products(PS[:, b, :], k, k == kt - 1, WH[:, s, c:c + P], WL[:, s, c:c + P],
                                            xh[:, k, :], xl[:, k, :])
                    T.done(mm, *name(m))
                    bank_reader[b] = ("read",) + name(m)
                    if m == ms - 1:
                        marks[("panel", n)] = marks[name(m)]
                    yield

            def gemm(*args):
                for _ in gemm_tiles(*args):
                    pass

            def gemm_first(n, kt, ms, xh, xl, ready, name):
                s = n % 2
                pe.wait_ge(lo_ready, n + 3)
                banks = [next_bank(name(m)) for m in range(ms)]
                for b in banks:
                    T.after(bank_reader[b], own=False)
                for k in range(kt):
                    T.after(ready(k), own=False)
                    for m in range(ms):
                        c = (k * ms + m) * P
                        mm = split_products(PS[:, banks[m], :], k, k == kt - 1, WH[:, s, c:c + P], WL[:, s, c:c + P],
                                            xh[:, k, :], xl[:, k, :])
                        if k == kt - 1:
                            T.done(mm, *name(m))
                            bank_reader[banks[m]] = ("read",) + name(m)
                marks[("panel", n)] = marks[name(ms - 1)]

            def gemm_tok(*args):
                for _ in tok_tiles(*args):
                    pass

            def tok_tiles(n, ready, name):
                s = n % 2
                pe.wait_ge(lo_ready, n + 3)
                for t in range(NB):
                    if t % 2 == 0:
                        b = next_bank(name(t // 2))
                        T.after(bank_reader[b], own=False)
                    for k in range(KD):
                        if t == 0:
                            T.after(ready(k), own=False)
                        ps = PS[:, b, (t % 2) * 256:(t % 2) * 256 + 256]
                        xh, xl = XH[:, k, t * P:(t + 1) * P], XL[:, k, t * P:(t + 1) * P]
                        wh, wl = WH[:, s, k * 256:(k + 1) * 256], WL[:, s, k * 256:(k + 1) * 256]
                        pe.matmul(ps, xh, wh, start=(k == 0), stop=False)
                        pe.matmul(ps, xl, wh, start=False, stop=False)
                        mm = pe.matmul(ps, xh, wl, start=False, stop=(k == KD - 1))
                    if t % 2:
                        T.done(mm, *name(t // 2))
                        bank_reader[b] = ("read",) + name(t // 2)
                        if t == NB - 1:
                            marks[("panel", n)] = marks[name(1)]
                        yield

            def tok_pair(n, name, ready, t, l):
                for p in range(2):
                    yield from tok_tiles(n + p, ready, lambda m: (t, l, name, p, m))

            def column_sums(src, kt, bank, ready, after, name):
                T.after(*after, own=False)
                for k in range(kt):
                    T.after(ready(k), own=False)
                    mm = pe.matmul(PS[:, bank, :], CT[:, 128:256], src(k), start=(k == 0), stop=(k == kt - 1))
                    T.done(mm, *name, k)
                marks[name] = marks[name + (kt - 1,)]

            def swapped(src, perm, bank, after, name):
                T.after(*after, own=False)
                T.done(pe.matmul(PS[:, bank, :], perm, src, start=True, stop=True), *name)

            def attention(pairs, l, t, fillers, steps):
                ring[0] = 2

                def scores(i):
                    U, nk = pairs[i], pairs[i]["nk"]
                    for v in range(2):
                        h = slice(64 * v, 64 * v + 64)
                        T.after(*U["ready"], (t, l, "s_read", i - 1) if i else bank_reader[4 + v], own=False)
                        mm = pe.matmul(PS[:, 4 + v, 0:nk], U["q"][h], U["k"][h], start=True, stop=True)
                    T.done(mm, t, l, "s", i)

                def transposes(i):
                    nk = pairs[i]["nk"]
                    T.after((t, l, "p", i), *[(t, l, "pt_read", i - 1)] if i else bank_reader[6:8], own=False)
                    for v in range(2):
                        for c in range(0, nk, P):
                            mm = pe.transpose(PS[:, 6 + v, c:c + P], probs(i, nk)[:, v, c:c + P], CT[:, 0:128])
                    T.done(mm, t, l, "pt", i)

                def outputs(i):
                    U, n = pairs[i], pairs[i]["nk"] // P
                    T.after((t, l, "pt_read", i), (t, l, "o_read", i - 1) if i else bank_reader[2], own=False)
                    for kb in range(n):
                        mm = pe.matmul(PS[:, 2, 0:2 * P], U["v"](kb), probs_t(i, n * P)[:, :, kb * P:(kb + 1) * P],
                                       start=(kb == 0), stop=(kb == n - 1))
                    T.done(mm, t, l, "o", i)

                scores(0)
                for i in range(16):
                    if i < 15:
                        scores(i + 1)
                    transposes(i)
                    run(fillers)
                    outputs(i)
                    run(steps)
                for _ in fillers:
                    pass
                bank_reader[2] = (t, l, "o_read", 15)
                bank_reader[4] = bank_reader[5] = (t, l, "s_read", 15)
                bank_reader[6] = bank_reader[7] = (t, l, "pt_read", 15)
                ring[0] = 4

            def mixer_gemms(l, w, t):
                for p in range(4):
                    gemm(w["gb"] + p, KD, 2, XH, XL, lambda k: None, lambda m: (t, l, "gb", 2 * p + m))
                for p in range(4):
                    (gemm if p else gemm_first)(w["wb"] + p, KD, 2, YH, YL, lambda k: (t, l, "r_lo", k), lambda m: (t, l, "wb", 2 * p + m))
                for p in range(4):
                    (gemm if p else gemm_first)(w["wo"] + p, KD, 2, XH, XL, lambda k: (t, l, "merged_lo", k),
                         lambda m: (t, l, "wo", 2 * p + m))

            def ffn(l, t, ff, groups, kt, base_t, base_d, base_h, h_ready):
                per = 2 + (2 if kt == 4 else 1)
                for b in range(8):
                    T.after(bank_reader[b], own=False)

                def up(g, s):
                    n = up_panel(ff, g, per)
                    slot = (up_panel(ff, s if isinstance(g, int) else s + 2, per)) % 2
                    for p in range(2):
                        pe.wait_ge(lo_ready, n + p + 3)
                        for m in range(2):
                            j = 2 * p + m
                            if not (isinstance(g, int) and g == 0 and l == 0):
                                pe.wait_ge(up_read, base_t + 4 * g + j - 3)
                            for k in range(KD):
                                if isinstance(g, int) and g == 0 and j == 0:
                                    T.after(h_ready(k), own=False)
                                c = (k * 2 + m) * P
                                sl = (slot + p) % 2
                                mm = split_products(PS[:, j, :], k, k == KD - 1, WH[:, sl, c:c + P],
                                                    WL[:, sl, c:c + P], XH[:, k, :], XL[:, k, :])
                            mm.then_inc(up_full, 1)

                def down(g, s):
                    n = down_panel(ff, g, per, groups)
                    slot = down_panel(ff, s if isinstance(g, int) else s + 2, per, groups if isinstance(g, int) else 99) % 2
                    pe.wait_ge(hid_lo, base_h + kt * (g + 1))
                    ms = 16 // kt
                    for p in range(kt * 8 // 16):
                        pe.wait_ge(lo_ready, n + p + 3)
                        for m in range(ms):
                            d = p * ms + m
                            pe.wait_ge(down_added, CREDIT + base_d + 8 * g + d - 3)
                            for k in range(kt):
                                c = (k * ms + m) * P
                                sl = (slot + p) % 2
                                mm = split_products(PS[:, 4 + d % 4, :], k, k == kt - 1, WH[:, sl, c:c + P],
                                                    WL[:, sl, c:c + P], YH[:, kt * (s % 2) + k, :],
                                                    YL[:, kt * (s % 2) + k, :])
                            mm.then_inc(down_full, 1)

                up(0, 0)
                trips = (groups - 1) // 2
                with pe.Fori(0, trips) as i:
                    up(2 * i + 1, 1)
                    down(2 * i, 0)
                    up(2 * i + 2, 2)
                    down(2 * i + 1, 1)
                for g in range(2 * trips, groups):
                    if g + 1 < groups:
                        up(g + 1, g + 1)
                    down(g, g)
                for b in range(8):
                    bank_reader[b] = (t, l, "ffn_out")
                done = CREDIT + base_d + 8 * groups
                marks[(t, l, "ffn_out")] = ("down_added", done)
                end = ff + per * groups
                marks[("panel", end - 1)] = ("down_full", done)
                marks[("panel", end - 2)] = ("down_full", done - (4 if kt == 4 else 8))

            for l in range(DEPTH):
                w, t = at_a(l), "a"
                if l == 0:
                    T.after("consts_a", own=False)
                column_sums(lambda k: TMP[:, k % 2, :], KD, 4, lambda k: (t, l, "sq", k), [bank_reader[4]], (t, l, "ms"))
                h_ready = lambda k: (t, l, "h_lo", k)
                before = {4: ("roped", 0), 2: ("roped", 4), 3: ("roped", 1)}

                def swap_a(j):
                    swapped(AR[:, j, :], CT[:, 256:384], 4 + j % 2,
                            [("read", t, l, "q", j), (t, l, "ms_read") if j < 2 else (t, l) + before[j]],
                            (t, l, "swap", j))

                gemm_first(w["q"], KD, 2, XH, XL, h_ready, lambda m: (t, l, "q", m))
                gemm(w["kv"], KD, 2, XH, XL, h_ready, lambda m: (t, l, "q", 4 + m))
                swap_a(0)
                swap_a(1)
                gemm(w["q"] + 2, KD, 2, XH, XL, h_ready, lambda m: (t, l, "q", 2 + m))
                swap_a(4)
                T.after(("read", t, l, "q", 5), bank_reader[6], own=False)
                for n in range(NB):
                    mm = pe.transpose(PS[:, 6, n * P:(n + 1) * P], AR[:, 18, n * P:(n + 1) * P], CT[:, 0:128])
                T.done(mm, t, l, "v_tok")

                def retention_tiles(p):
                    return gemm_tiles(w["rq"] + p, KD, 2, XH, XL, h_ready, lambda m: (t, l, "rqk", 2 * p + m))

                for _ in retention_tiles(0):
                    pass
                swap_a(2)
                swap_a(3)
                bank_reader[4], bank_reader[5], bank_reader[6] = (t, l, "roped", 2), (t, l, "roped", 3), (t, l, "v_read")

                def fillers():
                    for p in range(1, 4):
                        yield from retention_tiles(p)
                    for p in range(4):
                        yield from gemm_tiles(w["ga"] + p, KD, 2, XH, XL, h_ready, lambda m: (t, l, "ga", 2 * p + m))

                def retention_swaps():
                    for j in range(8):
                        swapped(AR[:, 6 + j, :], CT[:, 384:512], 3,
                                [("read", t, l, "rqk", j), (t, l, "roped", 4 + j) if j else bank_reader[3]],
                                (t, l, "swap", 5 + j))
                        yield

                attention(pairs_a(l), l, t, fillers(), retention_swaps())
                bank_reader[3] = (t, l, "roped", 12)
                for p in range(2):
                    (gemm if p else gemm_first)(w["wa"] + p, 4, 4, YH, YL, lambda k: (t, l, "ao_lo", k),
                                                lambda m: (t, l, "wa", 4 * p + m))
                gemm_tok(w["rv"], h_ready, lambda m: (t, l, "rv", 0, m))
                for h in range(RET_HEADS):
                    q, k, v = AR[:, 6 + h, :], AR[:, 10 + h, :], AR[:, 14 + 2 * (h % 2):16 + 2 * (h % 2), :].rearrange("p a (b e) -> p (a b) e", b=2)
                    T.after((t, l, "r_out_read", h - 1) if h else (t, l, "s_read", 15), own=False)
                    for c in range(NB):
                        mm = pe.matmul(PS[:, 4, c * P:(c + 1) * P], k[:, c * P:(c + 1) * P], q[:, c * P:(c + 1) * P],
                                       start=True, stop=True)
                    T.done(mm, t, l, "rs", h)
                    for c in range(NB):
                        mm = pe.transpose(PS[:, 5, c * P:(c + 1) * P], k[:, c * P:(c + 1) * P], CT[:, 0:128])
                    T.done(mm, t, l, "rkt", h)
                    gemm(w["rv"] + 2 * h + 1, KD, 2, XH, XL, h_ready, lambda m: (t, l, "rg", h, m))
                    T.after((t, l, "kz", h), ("read", t, l, "rv", h, 0), ("read", t, l, "rv", h, 1),
                            (t, l, "r_ms_read", h - 1) if h else (t, l, "pt_read", 15), own=False)
                    for c in range(NB - 1):
                        mm = pe.matmul(PS[:, 6 + c // 2, (c % 2) * 256:(c % 2) * 256 + 256], TMP[:, 1, c * P:(c + 1) * P],
                                       v[:, c, :], start=True, stop=True)
                    T.done(mm, t, l, "kv", h)
                    if h + 1 < RET_HEADS:
                        gemm_tok(w["rv"] + 2 * h + 2, h_ready, lambda m: (t, l, "rv", h + 1, m))
                    T.after((t, l, "rs_decayed", h), (t, l, "qx", h), (t, l, "state", h, 3), own=False)
                    for e in range(2):
                        for c in range(NB):
                            ps = PS[:, 4 + e, c * P:(c + 1) * P]
                            mm = pe.matmul(ps, v[:, c, e * P:(e + 1) * P], TMP[:, 0, c * P:(c + 1) * P],
                                           start=True, stop=(c == 0))
                            if c:
                                o = 4 * S + (c - 1) * 256 + e * P
                                mm = pe.matmul(ps, AR[:, o // S, o % S:o % S + P], TMP[:, 2, c * P:(c + 1) * P],
                                               start=False, stop=True)
                        T.done(mm, t, l, "r_out", h, e)
                    column_sums(lambda e: TMP[:, e, :], 2, 6, lambda e: (t, l, "r_sq", h, e), [], (t, l, "r_ms", h))
                bank_reader[4] = bank_reader[5] = (t, l, "r_out_read", 3)
                bank_reader[6] = (t, l, "r_ms_read", 3)
                bank_reader[7] = (t, l, "state", 3, 3)
                mixer_gemms(l, w, t)
                column_sums(lambda k: TMP[:, k % 2, :], KD, 6, lambda k: (t, l, "sq2", k), [bank_reader[6]], (t, l, "ms2"))
                bank_reader[6] = (t, l, "ms2_read")
                ffn(l, t, w["ff"], FF1_GROUPS, 4, *bases(t, l), lambda k: (t, l, "h2_lo", k))
            column_sums(lambda k: TMP[:, k % 2, :], KD, 4, lambda k: ("f", 0, "sq", k), [bank_reader[4]], ("f", 0, "ms"))
            bank_reader[4] = ("f", 0, "ms_read")

            for l in range(DEPTH):
                w, t = at_b(l), "b"
                T.after("consts_b", own=False)
                h_ready = lambda k: (t, l, "x_lo", k)
                def swap_b(j):
                    swapped(AR[:, j, :], CT[:, 256:384], 4 + j % 2,
                            [("read", t, l, "q", j), (t, l, "rot_tables"), (t, l, "roped", j - 2) if j > 1 else bank_reader[4 + j]],
                            (t, l, "swap", j))

                for i in range(7):
                    (gemm if i else gemm_first)(w["q"] + i, KD, 2, XH, XL, h_ready, lambda m: (t, l, "q", 2 * i + m))
                    if i:
                        swap_b(2 * i - 2)
                        swap_b(2 * i - 1)
                fillers = tok_pair(w["v"], "av", h_ready, t, l)
                run(fillers)
                swap_b(12)
                T.after(("read", t, l, "q", 13), bank_reader[6], own=False)
                for n in range(NB):
                    mm = pe.transpose(PS[:, 6, n * P:(n + 1) * P], AR[:, 18, n * P:(n + 1) * P], CT[:, 0:128])
                T.done(mm, t, l, "iw")
                run(fillers)
                for i in range(12):
                    b, j, bank = 1 + i // 4, i % 4, 4 + 2 * (i % 2)
                    T.after((t, l, "dots_read", i - 2) if i >= 2 else (t, l, "roped", 12), (t, l, "iw_read"),
                            bank_reader[7], own=False)
                    for v in range(2):
                        h = slice(64 * v, 64 * v + 64)
                        mm = pe.matmul(PS[:, bank + v, 0:(b + 1) * P], AR[h, 8 + j, b * P:(b + 1) * P],
                                       AR[h, 12, 0:(b + 1) * P], start=True, stop=True)
                    T.done(mm, t, l, "dots", i)
                    if i in (3, 7):
                        run(fillers)
                bank_reader[4] = bank_reader[5] = (t, l, "dots_read", 10)
                bank_reader[6] = bank_reader[7] = (t, l, "dots_read", 11)

                def fillers():
                    yield
                    for p in range(4):
                        yield from gemm_tiles(w["ga"] + p, KD, 2, XH, XL, h_ready, lambda m: (t, l, "ga", 2 * p + m))
                    for p in range(2):
                        yield from gemm_tiles(w["gq"] + p, KD, 2, XH, XL, h_ready, lambda m: (t, l, "gq", 2 * p + m))

                attention(pairs_b(l), l, t, fillers(), iter(()))
                for p in range(2):
                    (gemm if p else gemm_first)(w["wa"] + p, 4, 4, YH, YL, lambda k: (t, l, "ao_lo", k),
                                                lambda m: (t, l, "wa", 4 * p + m))
                T.after((t, l, "glr"), ("w_gate", l), own=False)
                for n in range(NB):
                    T.after((t, l, "la", n - 2) if n >= 2 else (t, l, "s_read", 15), own=False)
                    T.done(pe.matmul(PS[:, 4 + n % 2, :], AR[0:32, 13, n * P:(n + 1) * P], WG[:, :],
                                     start=True, stop=True), t, l, "gate", n)
                for p in range(2):
                    gemm_tok(w["gk"] + p, h_ready, lambda m: (t, l, "gk", p, m))
                for n in range(NB):
                    T.after((t, l, "decay_read", n - 2) if n >= 2 else (t, l, "la", 3), own=False)
                    T.done(pe.matmul(PS[:, 4 + n % 2, :], CT[:, 384:512], AR[:, 8 + n, :], start=True, stop=True),
                           t, l, "decay", n)
                T.after((t, l, "pt_read", 15), own=False)
                for h in range(GLA_HEADS):
                    for n in range(NB):
                        mm = pe.matmul(PS[:, 6, h * 8 + 2 * n:h * 8 + 2 * n + 2], AR[:, 8 + n, h * P:(h + 1) * P],
                                       CT[:, 512:514], start=True, stop=True)
                T.done(mm, t, l, "totals")
                gemm_tok(w["gv"], h_ready, lambda m: (t, l, "gv", 0, m))
                for h in range(GLA_HEADS):
                    v = AR[:, 14 + 2 * (h % 2):16 + 2 * (h % 2), :].rearrange("p a (b e) -> p (a b) e", b=2)
                    T.after(("read", t, l, "gv", h, 0), ("read", t, l, "gv", h, 1), (t, l, "totals_read"),
                            (t, l, "kd", 3), own=False)

                    def kv(c):
                        hp = 64 * (c % 2)
                        if c % 2:
                            T.after()
                        else:
                            T.after((t, l, "state", h, c - 3) if c >= 4 else
                                    ((t, l, "o_mean_read" if c == 0 else "o_ms_read", h - 1) if h else None), own=False)
                        T.done(pe.matmul(PS[:, 4 + (c // 2) % 2, (c % 2) * 256:(c % 2) * 256 + 256],
                                         AR[hp:hp + 64, 4 + c // 2, h * P:(h + 1) * P],
                                         v[hp:hp + 64, c // 2, :], start=True, stop=True), t, l, "gkv", h, c)

                    kv(0)
                    kv(1)
                    for c in range(8):
                        if c % 2 == 0 and c + 2 < 8:
                            kv(c + 2)
                            kv(c + 3)
                        T.after((t, l, "state", h, c), (t, l, "o_out_read", h - 1) if h and c == 0 else None, own=False)
                        for e in range(2):
                            mm = pe.matmul(PS[:, 6 + e, c * 64:(c + 1) * 64],
                                           AR[:, 12, (c % 2) * 256 + e * P:(c % 2) * 256 + (e + 1) * P],
                                           YSCR[:, KD + 4 + h, c * 64:(c + 1) * 64], start=True, stop=True)
                        T.done(mm, t, l, "g_out", h, c)
                    gemm(w["gv"] + 2 * h + 1, KD, 2, XH, XL, h_ready, lambda m: (t, l, "gr", h, m))
                    column_sums(lambda e: AR[:, 18 + e, :], 2, 4, lambda e: (t, l, "o_copied", h, e), [], (t, l, "o_mean", h))
                    if h + 1 < GLA_HEADS:
                        gemm_tok(w["gv"] + 2 * h + 2, h_ready, lambda m: (t, l, "gv", h + 1, m))
                    column_sums(lambda e: TMP[:, e, :], 2, 5, lambda e: (t, l, "o_sq", h, e), [], (t, l, "o_ms", h))
                bank_reader[4], bank_reader[5] = (t, l, "o_mean_read", 3), (t, l, "o_ms_read", 3)
                bank_reader[6] = bank_reader[7] = (t, l, "o_out_read", 3)
                mixer_gemms(l, w, t)
                for which in ("ln1", "ln2"):
                    if which == "ln2":
                        ffn(l, t, w["ff"], FF2_GROUPS, 2, *bases(t, l), lambda k: (t, l, "ln1_lo", k))
                    column_sums(lambda k: X[:, k, :], KD, 4, lambda k: (t, l, which + "_in", k), [bank_reader[4]],
                                (t, l, which + "_mean"))
                    column_sums(lambda k: TMP[:, k % 2, :], KD, 5, lambda k: (t, l, which + "_sq", k),
                                [bank_reader[5]], (t, l, which + "_ms"))
                    bank_reader[4] = (t, l, which + "_mean_read")
                    bank_reader[5] = (t, l, which + "_ms_read")


        @block.scalar
        def _(act):
            A = Steps(act, "act", sems["act"], marks, sems)

            def hi(c, k=0, i=0, used=None):
                if not k and c >= NPANELS:
                    return
                s = c % 2
                act.wait_ge(raw_full[s], 16 * (c // 2 + 1) + 8 * k * i)
                if used is not None:
                    act.wait_ge(*used)
                elif c >= 2:
                    who, n = marks.get(("panel", c - 2), ("pe", 1))
                    act.wait_ge(sems[who], n)
                act.activation(WH[:, s, :], RAW[:, s, :], ACT.Copy).then_inc(hi_ready, 1)

            def read(name, dst, func=ACT.Copy, *after, **kw):
                A.after(name, *after)
                A.done(act.activation(dst, bank_of(*name), func, **kw), *(("read",) + name))

            def split_hi(dst, src, after, name):
                A.after(*after)
                A.done(act.activation(dst, src, ACT.Copy), *name)

            def squares(src, kt, dst, ready, used, name):
                for k in range(kt):
                    A.after(ready(k), used(k))
                    A.done(act.activation(dst(k), src(k), ACT.Square), *name, k)

            def root(ms, name, after):
                A.after(*after)
                A.done(act.activation(TMP[:, 3, :], TMP[:, 2, :], ACT.Sqrt), *name)

            def attention(pairs, l, t, fillers):
                def exponentials(i):
                    U, c, pr = pairs[i], 8 * (i % 2), probs(i, pairs[i]["nk"])
                    A.after((t, l, "negmax", i))
                    for v in range(2):
                        if v:
                            A.after()
                        A.done(act.activation(pr[:, v, :], pr[:, v, :], ACT.Exp, bias=ST[:, c + 2 + v:c + 3 + v],
                                              scale=HD ** -0.5, accum_out=ST[:, c + 4 + v:c + 5 + v]), t, l, "exp", i)
                    if U["sink"] is not None:
                        A.after()
                        A.done(act.activation(ST[:, c + 6:c + 8], ST[:, c + 6:c + 8], ACT.Exp), t, l, "exp", i)

                def read_transposes(i):
                    nk = pairs[i]["nk"]
                    A.after((t, l, "pt", i), (t, l, "o", i - 2) if i >= 2 else None)
                    A.done(act.activation(probs_t(i, nk), PS[:, 6:8, 0:nk], ACT.Copy), t, l, "pt_read", i)

                def read_outputs(i):
                    A.after((t, l, "o", i))
                    for v in range(2):
                        if v:
                            A.after()
                        h = slice(64 * v, 64 * v + 64)
                        A.done(act.activation(pairs[i]["o"][h], PS[h, 2, v * P:(v + 1) * P], ACT.Copy), t, l, "o_read", i)

                exponentials(0)
                for i in range(16):
                    read_transposes(i)
                    if i < 15:
                        exponentials(i + 1)
                    run(fillers)
                    read_outputs(i)
                    if i >= 12:
                        j = i - 12
                        split_hi(YH[:, j, :], (AR[:, 14 + j, :] if t == "a" else AR[:, 8 + j, :]), [], (t, l, "ao_hi", j))
                for _ in fillers:
                    pass

            def mixer_gemms(l, w, t):
                for p in range(4):
                    hi(w["gb"] + p + 1)
                    for m in range(2):
                        read((t, l, "gb", 2 * p + m), SB[:, 2 * p + m, :], ACT.Sigmoid, (t, l, "arena_free"))
                if t == "b":
                    for k in range(KD):
                        A.after()
                        A.done(act.activation(X[:, k, :], X[:, k, :], ACT.Identity, scale=DN_ALPHA,
                                              bias=VEC[:, l % 2, VB["b_mix"] + k:VB["b_mix"] + k + 1]), t, l, "x_scaled", k)
                for p in range(4):
                    hi(w["wb"] + p + 1)
                    for m in range(2 * p, 2 * p + 2):
                        split_hi(XH[:, m, :], G[:, m, :], [(t, l, "merged", m)], (t, l, "merged_hi", m))
                for p in range(4):
                    hi(w["wo"] + p + 1)

            def ffn(l, t, ff, groups, kt, base_t, base_d, base_h):
                per = 2 + (2 if kt == 4 else 1)
                base_c = base_d - 8 * FF1_GROUPS * DEPTH if kt == 2 else 0
                base_c = base_c // 2
                downs = per - 2

                def up_used(g, p):
                    return up_full, base_t + 4 * g + 2 * (p + 1)

                def down_used(g, p):
                    return down_full, CREDIT + base_d + 8 * g + (8 // downs) * (p + 1)

                def hi_up(gc, gi, i, p):
                    g = gc + gi * i
                    if gi == 0 and gc == 1:
                        used = up_used(0, p)
                    elif downs == 2 or p == 1:
                        act.wait_ge(*up_used(g - 1, p))
                        used = down_used(g - 2, p if downs == 2 else 0)
                    else:
                        used = up_used(g - 1, 1)
                    hi(up_panel(ff, gc, per) + p, per * gi, i, used)

                def hi_down(gc, gi, i, p):
                    g = gc + gi * i
                    last = gi == 0 and gc == groups - 1
                    if downs == 2:
                        used = down_used(g - 1, p) if last else up_used(g + 1, p)
                    else:
                        used = up_used(g, 1) if last else up_used(g + 1, 0)
                    hi(down_panel(ff, gc, per, groups if gi == 0 else 99) + p, per * gi, i, used)

                def up(gc, gi, i, last=False):
                    g = gc + gi * i
                    t0 = base_t + 4 * g
                    buf = gc % 2
                    for p in range(2):
                        if p == 0:
                            if gi == 0 and gc == 0:
                                hi(ff + 1)
                            else:
                                hi_up(gc, gi, i, 1)
                        elif gi == 0 and gc == 0:
                            hi_up(1, 0, 0, 0)
                        else:
                            hi_down(gc - 1, gi, i, 0)
                        if kt == 2 and p == 1:
                            for m in range(2):
                                act.wait_ge(up_read, t0 + m + 1)
                                if not (gi == 0 and gc == 0):
                                    act.wait_ge(hid_ready, base_h + 2 * g + m - 1)
                                act.activation(AR[:, 4 + m, :], AR[:, m, :], ACT.Gelu_apprx_tanh).then_inc(gelu_done, 1)
                        for m in range(2):
                            j = 2 * p + m
                            act.wait_ge(up_full, t0 + j + 1)
                            if kt == 2:
                                if not (gi == 0 and gc == 0):
                                    if p == 0:
                                        act.wait_ge(gelu_done, base_c // 2 + 2 * g)
                                    else:
                                        act.wait_ge(hid_ready, base_h + 2 * g)
                                ch = 2 * g + m + (2 * FF2_GROUPS if p else 0)
                                tap, bias = VB["conv_w"] + 88 + ch, VB["conv_b"] + ch
                                act.activation(AR[:, j, :], PS[:, j, :], ACT.Identity, scale=VEC[:, l % 2, bass.ds(tap, 1)],
                                               bias=VEC[:, l % 2, bass.ds(bias, 1)]).then_inc(conv_begun, 1)
                            if kt == 4:
                                if not (gi == 0 and gc == 0 and base_t == 0):
                                    act.wait_ge(hid_ready, base_h + 4 * g + j - 3)
                                act.activation(AR[:, j, :], PS[:, j, :], ACT.Relu).then_inc(up_read, 1)
                        if kt == 4:
                            for m in range(2):
                                j = 2 * p + m
                                act.wait_ge(hid_ready, base_h + 4 * g + j + 1)
                                if not (gi == 0 and gc < 2):
                                    act.wait_ge(down_full, CREDIT + base_d + 8 * (g - 1))
                                act.activation(YH[:, 4 * buf + j, :], AR[:, 4 + j, :], ACT.Copy).then_inc(hid_hi, 1)
                    if kt == 2:
                        for m in range(2):
                            act.wait_ge(hid_ready, base_h + 2 * g + m + 1)
                            if not (gi == 0 and gc < 2):
                                act.wait_ge(down_full, CREDIT + base_d + 8 * (g - 1))
                            act.activation(YH[:, 2 * buf + m, :], AR[:, 6 + m, :], ACT.Copy).then_inc(hid_hi, 1)

                def down(gc, gi, i):
                    last = gi == 0 and gc == groups - 1
                    nxt_up = not (gi == 0 and gc >= groups - 2)
                    if downs == 2:
                        hi_down(gc, gi, i, 1)
                    if nxt_up:
                        hi_up(gc + 2, gi, i, 0)
                    elif not last:
                        hi_down(groups - 1, 0, 0, 0)
                    else:
                        hi(ff + per * groups)

                conv = up
                A.after()
                conv(0, 0, 0)
                trips = (groups - 1) // 2
                with act.Fori(0, trips) as i:
                    conv(1, 2, i)
                    down(0, 2, i)
                    conv(2, 2, i)
                    down(1, 2, i)
                for g in range(2 * trips, groups):
                    if g + 1 < groups:
                        conv(g + 1, 0, 0)
                    down(g, 0, 0)

            def norm(t, l, sfx, x_ready, gain, to_x=False):
                squares(lambda k: X[:, k, :], KD, lambda k: TMP[:, k % 2, :], lambda k: x_ready(k),
                        lambda k: (t, l, "ms" + sfx, k - 2) if k >= 2 else None, (t, l, "sq" + sfx))
                root(None, (t, l, "root" + sfx), [(t, l, "ms" + sfx + "_read")])
                for k in range(KD):
                    src = X[:, k, :] if to_x else TMP[:, k % 2, :]
                    hn = ("b", 0, "x_hi", k) if to_x else (t, l, "h" + sfx + "_hi", k)
                    split_hi(XH[:, k, :], src, [(t, l, "h" + sfx, k)], hn)

            hi(0)
            const_dma(act, X[:, :, :], x_in.rearrange("(k p) s -> p k s", p=P), "x_in")
            const_dma(act, CT[:, :], consts_in[0], "consts_a")
            const_dma(act, VEC[:, 0, :], vec_in[0], "vec0")
            const_dma(act, VEC[:, 1, :], vec_in[1], "vec1")
            for l in range(DEPTH):
                w, t = at_a(l), "a"
                if l:
                    A.after((t, l - 1, "roped", 12))
                const_dma(act, ROT[:, :, :], rot_in[0], ("rot", l, 0))
                norm(t, l, "", lambda k: "x_in" if l == 0 else (t, l - 1, "ffn_out"), None)
                hi(w["q"] + 1)
                for m in range(2):
                    read((t, l, "q", m), AR[:, m, :])
                hi(w["kv"] + 1)
                read((t, l, "q", 4), AR[:, 4, :])
                read((t, l, "q", 5), AR[:, 18, :])
                hi(w["q"] + 3)
                for m in range(2, 4):
                    read((t, l, "q", m), AR[:, m, :])
                A.after((t, l, "v_tok"))
                A.done(act.activation(AR[:, 5, :], PS[:, 6, :], ACT.Copy), t, l, "v_read")

                def retention_reads(p):
                    hi(w["rq"] + p + 1)
                    for m in range(2):
                        read((t, l, "rqk", 2 * p + m), AR[:, 6 + 2 * p + m, :])
                        yield

                def filler_reads():
                    for p in range(1, 4):
                        yield from retention_reads(p)
                    for p in range(4):
                        hi(w["ga"] + p + 1)
                        for m in range(2):
                            read((t, l, "ga", 2 * p + m), G[:, 2 * p + m, :], ACT.Sigmoid)
                            yield

                for _ in retention_reads(0):
                    pass
                A.after((t, l, "roped", 3))
                const_dma(act, ROT[:, :, :], rot_in[1], ("rot", l, 1))
                attention(pairs_a(l), l, t, filler_reads())
                for p in range(2):
                    hi(w["wa"] + p + 1)

                def rv_read(h):
                    hi(w["rv"] + 2 * h + 1)
                    for m in range(2):
                        read((t, l, "rv", h, m), AR[:, 14 + 2 * (h % 2) + m, :], ACT.Copy, (t, l, "ao_lo", 3),
                             (t, l, "r_out", h - 2, 1) if h >= 2 else None)

                rv_read(0)
                for h in range(RET_HEADS):
                    A.after((t, l, "rkt", h), (t, l, "r_ms", h - 1) if h else (t, l, "pt", 15))
                    z = CA["zeta"] + h
                    A.done(act.activation(TMP[:, 1, :], PS[:, 5, :], ACT.Copy, scale=CT[:, z:z + 1]), t, l, "kz", h)
                    hi(w["rv"] + 2 * h + 2)
                    for m in range(2):
                        read((t, l, "rg", h, m), AR[:, m, :], ACT.Silu, (t, l, "r_gated", h - 1, m) if h else None)
                    if h + 1 < RET_HEADS:
                        rv_read(h + 1)
                    for e in range(2):
                        A.after((t, l, "r_out", h, 1))
                        A.done(act.activation(TMP[:, e, :], PS[:, 4 + e, :], ACT.Square), t, l, "r_sq", h, e)
                    for e in range(2):
                        A.after((t, l, "r_lo", 2 * h - 1) if h else None)
                        A.done(act.activation(AR[:, 18 + e, :], PS[:, 4 + e, :], ACT.Copy), t, l, "r_copied", h, e)
                    marks[(t, l, "r_out_read", h)] = ("act", A.n)
                    root(None, (t, l, "r_root", h), [(t, l, "r_ms_read", h)])
                    for e in range(2):
                        split_hi(YH[:, 2 * h + e, :], AR[:, 18 + e, :], [(t, l, "r_gated", h, e), (t, l, "wa", 7)],
                                 (t, l, "r_hi", 2 * h + e))
                marks[(t, l, "arena_free")] = marks.get((t, l, "r_gated", 3, 1), ("dve", 1))
                mixer_gemms(l, w, t)
                if l == DEPTH - 1:
                    const_dma(act, CT[:, 256:CW], consts_in[1, :, 256:CW], "consts_b")
                norm(t, l, "2", lambda k: ("read", t, l, "wo", k), None)
                ffn(l, t, w["ff"], FF1_GROUPS, 4, *bases(t, l))
                if l == 0:
                    const_dma(act, VEC[:, 0, :], vec_in[2], "vec2")
            norm("f", 0, "", lambda k: ("a", DEPTH - 1, "ffn_out"), None, to_x=True)
            const_dma(act, VEC[:, 1, :], vec_in[3], "vec3")

            for l in range(DEPTH):
                w, t = at_b(l), "b"
                pos = TMP[:, 3, :].bitcast(I32)
                A.after((t, l - 1, "ln2_ms_read") if l else None)
                const_dma(act, pos, pos_in, ("pos", l))
                const_dma(act, WG[:, :], wgate_in[l], ("w_gate", l))
                A.after((t, l, "angle"))
                A.done(act.activation(ROT[:, 1, :], TMP[:, 2, :], ACT.Sin))
                A.after()
                A.done(act.activation(TMP[:, 3, :], TMP[:, 2, :], ACT.Sin, scale=0.5), t, l, "sines")
                j = 0
                for i in range(7):
                    hi(w["q"] + i + 1)
                    for m in range(2):
                        read((t, l, "q", j), AR[:, j if j < 13 else 18, :])
                        j += 1

                def tok_reads(n, name):
                    for p in range(2):
                        hi(n + p + 1)
                        for m in range(2):
                            u0 = (14 if name == "av" else 4) + 2 * m
                            A.after((t, l, name, p, m))
                            A.done(act.activation(AR[:, u0:u0 + 2, p * 256:(p + 1) * 256],
                                                  bank_of(t, l, name, p, m).rearrange("p (a b) -> p a b", a=2), ACT.Copy),
                                   "read", t, l, name, p, m)
                            yield

                fillers = tok_reads(w["v"], "av")
                run(fillers, 2)
                for i in range(12):
                    nk = (i // 4 + 2) * P
                    A.after((t, l, "dots", i), (t, l, "acc", 2 * (i - 2) + 1) if i >= 2 else None)
                    A.done(act.activation(probs(i, nk), PS[:, 4 + 2 * (i % 2):6 + 2 * (i % 2), 0:nk], ACT.Relu, scale=0.125),
                           t, l, "dots_read", i)
                    if i in (3, 7):
                        run(fillers)

                def filler_reads():
                    yield
                    for p in range(4):
                        hi(w["ga"] + p + 1)
                        for m in range(2):
                            read((t, l, "ga", 2 * p + m), G[:, 2 * p + m, :], ACT.Sigmoid)
                            yield
                    for p in range(2):
                        hi(w["gq"] + p + 1)
                        for m in range(2):
                            read((t, l, "gq", 2 * p + m), YSCR[:, KD + 4 + 2 * p + m, :])
                            yield

                attention(pairs_b(l), l, t, filler_reads())
                for p in range(2):
                    hi(w["wa"] + p + 1)
                for n in range(NB):
                    A.after((t, l, "gate", n), (t, l, "la", n - 2) if n >= 2 else None)
                    A.done(act.activation(TMP[:, n % 2, :], PS[:, 4 + n % 2, :], ACT.Abs))
                    A.after()
                    A.done(act.activation(TMP[:, n % 2, :], TMP[:, n % 2, :], ACT.Exp, scale=-1.0))
                    A.after()
                    A.done(act.activation(TMP[:, n % 2, :], TMP[:, n % 2, :], ACT.Ln, bias=1.0), t, l, "soft", n)
                for _ in tok_reads(w["gk"], "gk"):
                    pass
                for n in range(NB):
                    A.after((t, l, "decay", n), (t, l, "kd", n - 2) if n >= 2 else (t, l, "la", 3))
                    A.done(act.activation(TMP[:, n % 2, :], PS[:, 4 + n % 2, :], ACT.Exp), t, l, "decay_read", n)
                A.after((t, l, "totals"))
                A.done(act.activation(ST[:, 64:96], PS[:, 6, 0:32], ACT.Exp), t, l, "totals_read")

                def gv_read(h):
                    hi(w["gv"] + 2 * h + 1)
                    for m in range(2):
                        read((t, l, "gv", h, m), AR[:, 14 + 2 * (h % 2) + m, :], ACT.Copy,
                             (t, l, "g_out", h - 2, 7) if h >= 2 else None)

                gv_read(0)
                for h in range(GLA_HEADS):
                    for e in range(2):
                        A.after((t, l, "g_out", h, 7), (t, l, "r_lo", 2 * h - 1) if h else None)
                        A.done(act.activation(AR[:, 18 + e, :], PS[:, 6 + e, :], ACT.Copy, scale=GLA_DK ** -0.5),
                               t, l, "o_copied", h, e)
                    marks[(t, l, "o_out_read", h)] = ("act", A.n)
                    hi(w["gv"] + 2 * h + 2)
                    for m in range(2):
                        read((t, l, "gr", h, m), AR[:, 8 + m, :], ACT.Silu, (t, l, "r_gated", h - 1, m) if h else None)
                    for e in range(2):
                        A.after((t, l, "o_centered", h, e), (t, l, "kd", 3))
                        A.done(act.activation(TMP[:, e, :], AR[:, 18 + e, :], ACT.Square), t, l, "o_sq", h, e)
                    if h + 1 < GLA_HEADS:
                        gv_read(h + 1)
                    root(None, (t, l, "r_root", h), [(t, l, "o_ms_read", h)])
                    for e in range(2):
                        split_hi(YH[:, 2 * h + e, :], AR[:, 18 + e, :], [(t, l, "r_gated", h, e), (t, l, "wa", 7)],
                                 (t, l, "r_hi", 2 * h + e))
                marks[(t, l, "arena_free")] = marks.get((t, l, "r_gated", 3, 1), ("dve", 1))
                mixer_gemms(l, w, t)
                for which, gain in (("ln1", VB["ln1_g"]), ("ln2", VB["ln2_g"])):
                    squares(lambda k: X[:, k, :], KD, lambda k: TMP[:, k % 2, :], lambda k: (t, l, which + "_centered", k),
                            lambda k: (t, l, which + "_ms", k - 2) if k >= 2 else None, (t, l, which + "_sq"))
                    root(None, (t, l, which + "_root"), [(t, l, which + "_ms_read")])
                    for k in range(KD):
                        g = gain + k
                        A.after((t, l, which + "_scaled", k))
                        A.done(act.activation(X[:, k, :], X[:, k, :], ACT.Identity, scale=VEC[:, l % 2, g:g + 1],
                                              bias=VEC[:, l % 2, g + 8:g + 9]), t, l, which + "_x", k)
                        if which == "ln1":
                            split_hi(XH[:, k, :], X[:, k, :], [], (t, l, "ln1_hi", k))
                        elif l + 1 < DEPTH:
                            split_hi(XH[:, k, :], X[:, k, :], [], (t, l + 1, "x_hi", k))
                    if which == "ln1":
                        for k in range(KD):
                            A.after((t, l, "ln1_lo", k))
                            A.done(act.activation(X[:, k, :], X[:, k, :], ACT.Copy, scale=DN_ALPHA), t, l, "x2_scaled", k)
                        ffn(l, t, w["ff"], FF2_GROUPS, 2, *bases(t, l))
            marks["x_final"] = ("act", A.n)

        @block.vector
        def _(dve):
            V = Steps(dve, "dve", sems["dve"], marks, sems)
            dve.sem_inc(down_added, CREDIT)

            def lo(dst, src, high, after, name):
                V.after(*after)
                V.done(dve.tensor_tensor(dst, src, high.bitcast(F32), ALU.subtract), *name)

            def rope(x, ps, name, after, part=TMP[:, 2, :]):
                V.after(*after)
                V.done(dve.tensor_tensor(part, ps, ROT[:, 1, :], ALU.mult))
                V.after()
                V.done(dve.tensor_tensor(x, x, ROT[:, 0, :], ALU.mult))
                V.after()
                V.done(dve.tensor_tensor(x, x, part, ALU.add), *name)

            def mean_square(bank, n, eps, after, name):
                V.after(*after)
                V.done(dve.tensor_scalar(TMP[:, 2, :], PS[:, bank, :], 1.0 / n, eps, ALU.mult, ALU.add), *name)

            def inverse_root(after):
                V.after(*after)
                V.done(dve.reciprocal(TMP[:, 3, :], TMP[:, 3, :]))

            def norm(t, l, sfx, bank, gain, to_x=False, vec=()):
                mean_square(bank, D, EPS, [(t, l, "ms" + sfx, KD - 1)], (t, l, "ms" + sfx + "_read"))
                inverse_root([(t, l, "root" + sfx)])
                for k in range(KD):
                    dst = X[:, k, :] if to_x else TMP[:, k % 2, :]
                    hn = (lambda k: ("b", 0, "x_hi", k)) if to_x else (lambda k: (t, l, "h" + sfx + "_hi", k))
                    ln = (lambda k: ("b", 0, "x_lo", k)) if to_x else (lambda k: (t, l, "h" + sfx + "_lo", k))
                    V.after(hn(k - 2) if k >= 2 else None, *vec)
                    V.done(dve.scalar_tensor_tensor(dst, X[:, k, :], VEC[:, l % 2, gain + k:gain + k + 1] if not to_x else
                                                    VEC[:, 1, gain + k:gain + k + 1], TMP[:, 3, :], ALU.mult, ALU.mult),
                           t, l, "h" + sfx, k)
                    lo(XL[:, k, :], dst, XH[:, k, :], [hn(k)], ln(k))

            def attention(pairs, l, t, steps, per_pair):
                def maxima(i):
                    U, c, nk = pairs[i], 8 * (i % 2), pairs[i]["nk"]
                    pr = probs(i, nk)
                    V.after((t, l, "s", i), (t, l, "pt", i - 2) if i >= 2 else None, (t, l, "mask", i // 4))
                    V.done(dve.scalar_tensor_tensor(pr, U["mask"].unsqueeze(1).broadcast_to([P, 2, nk]), U["weight"],
                                                    PS[:, 4:6, 0:nk], ALU.mult, ALU.add), t, l, "s_read", i)
                    V.after()
                    V.done(dve.tensor_reduce(ST[:, c:c + 2], pr, AX, ALU.max))
                    V.after()
                    if U["sink"] is None:
                        V.done(dve.tensor_scalar(ST[:, c + 2:c + 4], ST[:, c:c + 2], -(HD ** -0.5), None, ALU.mult),
                               t, l, "negmax", i)
                    else:
                        sinks = ST[:, 16 + U["sink"]:18 + U["sink"]]
                        V.done(dve.scalar_tensor_tensor(ST[:, c + 2:c + 4], ST[:, c:c + 2], -(HD ** -0.5), sinks,
                                                        ALU.mult, ALU.min))
                        V.after()
                        V.done(dve.tensor_tensor(ST[:, c + 6:c + 8], ST[:, c + 2:c + 4], sinks, ALU.subtract),
                               t, l, "negmax", i)

                def normalise(i):
                    U, c, nk = pairs[i], 8 * (i % 2), pairs[i]["nk"]
                    pr = probs(i, nk)
                    V.after((t, l, "exp", i))
                    if U["sink"] is not None:
                        V.done(dve.tensor_tensor(ST[:, c + 4:c + 6], ST[:, c + 4:c + 6], ST[:, c + 6:c + 8], ALU.add))
                        V.after()
                    V.done(dve.reciprocal(ST[:, c:c + 2], ST[:, c + 4:c + 6]))
                    V.after()
                    V.done(dve.tensor_tensor(pr, pr, ST[:, c:c + 2].unsqueeze(2).broadcast_to([P, 2, nk]), ALU.mult),
                           t, l, "p", i)

                for i in range(16):
                    maxima(i)
                    if per_pair > 1:
                        run(steps, per_pair)
                    normalise(i)
                    if per_pair == 1 and i:
                        run(steps)
                for j in range(4):
                    lo(YL[:, j, :], AR[:, 14 + j, :] if t == "a" else AR[:, 8 + j, :], YH[:, j, :],
                       [(t, l, "ao_hi", j)], (t, l, "ao_lo", j))

            def branch_gate(l, t):
                for m in range(8):
                    V.after((t, l, "wa", m), ("read", t, l, "ga", m))
                    V.done(dve.tensor_tensor(G[:, m, :], G[:, m, :], bank_of(t, l, "wa", m), ALU.mult),
                           "read", t, l, "wa", m)

            def mixer_gemms(l, t):
                for m in range(8):
                    V.after((t, l, "wb", m), ("read", t, l, "gb", m))
                    V.done(dve.tensor_tensor(SB[:, m, :], SB[:, m, :], bank_of(t, l, "wb", m), ALU.mult),
                           "read", t, l, "wb", m)
                    V.after()
                    V.done(dve.tensor_tensor(G[:, m, :], G[:, m, :], SB[:, m, :], ALU.add), t, l, "merged", m)
                    lo(XL[:, m, :], G[:, m, :], XH[:, m, :], [(t, l, "merged_hi", m), (t, l, "gb", 7)],
                       (t, l, "merged_lo", m))
                for m in range(8):
                    V.after((t, l, "wo", m), (t, l, "x_scaled", m) if t == "b" else None)
                    V.done(dve.tensor_tensor(X[:, m, :], X[:, m, :], bank_of(t, l, "wo", m), ALU.add),
                           "read", t, l, "wo", m)
                    marks[(t, l, "ln1_in", m)] = ("dve", V.n)

            def ffn(l, t, groups, kt, base_t, base_d, base_h):
                base_c = (base_d - 8 * FF1_GROUPS * DEPTH) // 2 if kt == 2 else 0
                V.after(*[(t, l, "x2_scaled", k) for k in range(KD)] if kt == 2 else [])

                def up(gc, gi, i):
                    g = gc + gi * i
                    buf = gc % 2
                    first = gi == 0 and gc == 0
                    for p in range(2):
                        if kt == 2:
                            for m in range(2):
                                j = 2 * p + m
                                ch = 2 * g + m + (2 * FF2_GROUPS if p else 0)
                                for tap in (1, 2):
                                    n = S - tap
                                    wv = VEC[:, l % 2, bass.ds(VB["conv_w"] + 88 - 44 * tap + ch, 1)]
                                    if tap == 1:
                                        dve.wait_ge(conv_begun, base_c + 4 * g + j + 1)
                                    else:
                                        dve.wait_ge(tap_added, base_c + 4 * g + j + 1)
                                    ins = dve.scalar_tensor_tensor(AR[:, j, tap:S], PS[:, j, 0:n], wv, AR[:, j, tap:S],
                                                                   ALU.mult, ALU.add)
                                    ins.then_inc(tap_added if tap == 1 else up_read, 1)
                        if kt == 4:
                            for m in range(2):
                                j = 2 * p + m
                                dve.wait_ge(up_read, base_t + 4 * g + j + 1)
                                if not (first and base_h == 0):
                                    dve.wait_ge(hid_lo, base_h + 4 * g + j - 3)
                                dve.tensor_tensor(AR[:, 4 + j, :], AR[:, j, :], AR[:, j, :], ALU.mult)\
                                   .then_inc(hid_ready, 1)
                            for m in range(2):
                                j = 2 * p + m
                                dve.wait_ge(hid_hi, base_h + 4 * g + j + 1)
                                dve.tensor_tensor(YL[:, 4 * buf + j, :], AR[:, 4 + j, :], YH[:, 4 * buf + j, :].bitcast(F32),
                                                  ALU.subtract).then_inc(hid_lo, 1)
                    if kt == 2:
                        for m in range(2):
                            dve.wait_ge(gelu_done, base_c // 2 + 2 * g + m + 1)
                            dve.wait_ge(up_read, base_t + 4 * g + 3 + m)
                            if not first:
                                dve.wait_ge(hid_lo, base_h + 2 * g + m - 1)
                            dve.tensor_tensor(AR[:, 6 + m, :], AR[:, 4 + m, :], AR[:, 2 + m, :], ALU.mult)\
                               .then_inc(hid_ready, 1)
                        for m in range(2):
                            dve.wait_ge(hid_hi, base_h + 2 * g + m + 1)
                            dve.tensor_tensor(YL[:, 2 * buf + m, :], AR[:, 6 + m, :], YH[:, 2 * buf + m, :].bitcast(F32),
                                              ALU.subtract).then_inc(hid_lo, 1)

                def down(gc, gi, i):
                    g = gc + gi * i
                    for m in range(8):
                        dve.wait_ge(down_full, CREDIT + base_d + 8 * g + m + 1)
                        dve.wait_ge(down_added, CREDIT + base_d + 8 * g + m - 7)
                        dve.tensor_tensor(X[:, m, :], X[:, m, :], PS[:, 4 + m % 4, :], ALU.add).then_inc(down_added, 1)

                up(0, 0, 0)
                trips = (groups - 1) // 2
                with dve.Fori(0, trips) as i:
                    up(1, 2, i)
                    down(0, 2, i)
                    up(2, 2, i)
                    down(1, 2, i)
                for g in range(2 * trips, groups):
                    if g + 1 < groups:
                        up(g + 1, 0, 0)
                    down(g, 0, 0)
                dve.wait_ge(down_added, CREDIT + base_d + 8 * groups)

            for l in range(DEPTH):
                t = "a"
                V.after("vec%d" % l)
                o = VA["sinks"]
                V.done(dve.tensor_scalar(ST[:, 16:24], VEC[:, l % 2, o:o + 8], -1.0, None, ALU.mult))
                for b in range(4):
                    marks[(t, l, "mask", b)] = marks.get("consts_a", ("const", 16))
                norm(t, l, "", 4, VA["g_mix"])
                for j in (0, 1, 4, 2, 3):
                    rope(AR[:, j, :], PS[:, 4 + j % 2, :], (t, l, "roped", j), [(t, l, "swap", j), ("rot", l, 0)])

                def retention_ropes():
                    for j in range(8):
                        rope(AR[:, 6 + j, :], PS[:, 3, :], (t, l, "roped", 5 + j), [(t, l, "swap", 5 + j), ("rot", l, 1)],
                             YSCR[:, KD + 7, :])
                        yield

                attention(pairs_a(l), l, t, retention_ropes(), 1)
                branch_gate(l, t)
                for h in range(RET_HEADS):
                    dec, xi = CA["decay"] + h * P, CA["xi"] + h * P

                    def per_chunk(c0):
                        return CT[:, c0:c0 + P].unsqueeze(1).broadcast_to([P, NB, P])

                    def chunks(ap):
                        return ap.rearrange("p (c i) -> p c i", c=NB)

                    V.after((t, l, "rs", h), (t, l, "r_ms", h - 1) if h else (t, l, "pt", 15))
                    V.done(dve.tensor_tensor(chunks(TMP[:, 0, :]), chunks(PS[:, 4, :]), per_chunk(dec), ALU.mult),
                           t, l, "rs_decayed", h)
                    V.after((t, l, "r_root", h - 1) if h else None)
                    V.done(dve.tensor_tensor(chunks(TMP[:, 2, :]), chunks(AR[:, 6 + h, :]), per_chunk(xi), ALU.mult),
                           t, l, "qx", h)
                    g_chunk = float(np.exp(np.log1p(-2.0 ** (-5.0 - h)) * P))
                    flat = AR[:, 4:6, :].rearrange("p a s -> p (a s)")
                    V.after((t, l, "kv", h))
                    V.done(dve.tensor_copy(flat[:, 0:256], PS[:, 6, 0:256]), t, l, "state", h, 1)
                    for c in (1, 2):
                        ps = PS[:, 6, 256:512] if c == 1 else PS[:, 7, 0:256]
                        V.after()
                        V.done(dve.scalar_tensor_tensor(flat[:, 256 * c:256 * c + 256], flat[:, 256 * c - 256:256 * c], g_chunk,
                                                        ps, ALU.mult, ALU.add), t, l, "state", h, c + 1)
                    mean_square(6, RET_V, EPS, [(t, l, "r_ms", h)], (t, l, "r_ms_read", h))
                    inverse_root([(t, l, "r_root", h)])
                    for e in range(2):
                        V.after((t, l, "r_copied", h, e))
                        V.done(dve.tensor_tensor(AR[:, 18 + e, :], AR[:, 18 + e, :], TMP[:, 3, :], ALU.mult))
                        V.after(("read", t, l, "rg", h, e))
                        V.done(dve.tensor_tensor(AR[:, 18 + e, :], AR[:, 18 + e, :], AR[:, e, :], ALU.mult),
                               t, l, "r_gated", h, e)
                    for e in range(2):
                        lo(YL[:, 2 * h + e, :], AR[:, 18 + e, :], YH[:, 2 * h + e, :], [(t, l, "r_hi", 2 * h + e)],
                           (t, l, "r_lo", 2 * h + e))
                mixer_gemms(l, t)
                norm(t, l, "2", 6, VA["g_mlp"])
                ffn(l, t, FF1_GROUPS, 4, *bases(t, l))
            norm("f", 0, "", 4, VB["g_final"], to_x=True)

            for l in range(DEPTH):
                t = "b"
                V.after(("pos", l), "consts_b", "vec2" if l == 0 else "vec3", (t, l - 1, "ln2_x", KD - 1) if l else None)
                V.done(dve.tensor_copy(TMP[:, 2, :], TMP[:, 3, :].bitcast(I32)))
                V.after()
                V.done(dve.tensor_scalar(TMP[:, 2, :], TMP[:, 2, :], CT[:, 514:515], None, ALU.mult))
                V.after()
                V.done(dve.tensor_scalar(TMP[:, 3, :], TMP[:, 2, :], 1.0 / (2 * np.pi), 12582912.0, ALU.mult, ALU.add))
                V.after()
                V.done(dve.tensor_scalar(TMP[:, 3, :], TMP[:, 3, :], 12582912.0, None, ALU.subtract))
                for part in (6.28125, 2 * np.pi - 6.28125):
                    V.after()
                    V.done(dve.scalar_tensor_tensor(TMP[:, 2, :], TMP[:, 3, :], -part, TMP[:, 2, :], ALU.mult, ALU.add))
                V.after()
                V.done(dve.tensor_scalar(TMP[:, 2, :], TMP[:, 2, :], -3.1415925, 3.1415925, ALU.max, ALU.min), t, l, "angle")
                V.after((t, l, "sines"))
                V.done(dve.tensor_scalar(ROT[:, 1, :], ROT[:, 1, :], CT[:, 515:516], None, ALU.mult))
                V.after()
                V.done(dve.tensor_tensor(TMP[:, 3, :], TMP[:, 3, :], TMP[:, 3, :], ALU.mult))
                V.after()
                V.done(dve.tensor_scalar(ROT[:, 0, :], TMP[:, 3, :], -2.0, 1.0, ALU.mult, ALU.add), t, l, "rot_tables")
                for j in range(13):
                    rope(AR[:, j, :], PS[:, 4 + j % 2, :], (t, l, "roped", j), [(t, l, "swap", j)])
                iw = ST[:, 32:64].rearrange("p (n h) -> p n h", n=NB)
                V.after((t, l, "iw"))
                V.done(dve.tensor_scalar(iw, PS[:, 6, :].rearrange("p (n c) -> p n c", n=NB)[:, :, 32:40], 8 ** -0.5, None,
                                         ALU.mult), t, l, "iw_read")
                V.after()
                V.done(dve.memset(AR[0:32, 13, :], 1.0))
                V.after()
                V.done(dve.tensor_copy(AR[0:16, 13, :], AR[0:16, 18, :]), t, l, "glr")
                V.after()
                m0 = mask_b(0)
                V.done(dve.memset(m0, 0.0))
                V.after()
                V.done(dve.memset(m0[0:64, 64:128], -1.0), t, l, "mask", 0)
                for b in range(1, NB):
                    sc = mask_b(b)
                    for h in range(8):
                        u = 8 * (b - 1) + h
                        src = probs(u // 2, (b + 1) * P)[:, u % 2, :]
                        V.after((t, l, "dots_read", u // 2))
                        wcol = ST[:, 32 + 8 * b + h:33 + 8 * b + h]
                        if h == 0:
                            V.done(dve.tensor_scalar(sc, src, wcol, None, ALU.mult), t, l, "acc", u)
                        else:
                            V.done(dve.scalar_tensor_tensor(sc, src, wcol, sc, ALU.mult, ALU.add), t, l, "acc", u)
                    V.after()
                    V.done(dve.memset(sc[0:64, b * P + 64:(b + 1) * P], NEG))

                def top_k():
                    for b in range(1, NB):
                        sc, other, best = mask_b(b), AR[:, 12, 0:(b + 1) * P], ST[:, 24:32]
                        for r in range(TOPK // 8):
                            src, dst = (sc, other) if r % 2 == 0 else (other, sc)
                            V.after((t, l, "dots", 11))
                            V.done(dve.max(best, src))
                            V.after()
                            V.done(dve.match_replace(dst, best, src, TAKEN))
                            if r == TOPK // 8 - 1:
                                V.after()
                                V.done(dve.tensor_scalar(sc, sc, TAKEN, 1.0, ALU.is_equal, ALU.subtract), t, l, "mask", b)
                            yield

                attention(pairs_b(l), l, t, top_k(), TOPK // 8 // 4)
                branch_gate(l, t)
                for n in range(NB):
                    V.after((t, l, "soft", n), (t, l, "ao_hi", 3))
                    V.done(dve.scalar_tensor_tensor(AR[:, 8 + n, :], PS[:, 4 + n % 2, :], 0.0, TMP[:, n % 2, :],
                                                    ALU.min, ALU.subtract), t, l, "la", n)
                for n in range(NB):
                    V.after((t, l, "decay_read", n), *[("read", t, l, "gk", p, n // 2) for p in range(2)])
                    V.done(dve.tensor_tensor(AR[:, 4 + n, :], AR[:, 4 + n, :], TMP[:, n % 2, :], ALU.mult), t, l, "kd", n)
                for h in range(GLA_HEADS):
                    for c in range(8):
                        ps = PS[:, 4 + (c // 2) % 2, (c % 2) * 256:(c % 2) * 256 + 256]
                        new, old = AR[:, 12, (c % 2) * 256:(c % 2) * 256 + 256], AR[:, 12, ((c + 1) % 2) * 256:((c + 1) % 2) * 256 + 256]
                        V.after((t, l, "gkv", h, c | 1), (t, l, "totals_read"),
                                (t, l, "g_out", h, c - 2) if c >= 2 else ((t, l, "g_out", h - 1, c + 6) if h else None))
                        if c == 0:
                            V.done(dve.tensor_copy(new, ps), t, l, "state", h, c)
                        else:
                            V.done(dve.scalar_tensor_tensor(new, old, ST[:, 64 + 8 * h + c:65 + 8 * h + c], ps,
                                                            ALU.mult, ALU.add), t, l, "state", h, c)
                    for e in range(2):
                        V.after((t, l, "o_mean", h), (t, l, "o_copied", h, e))
                        V.done(dve.scalar_tensor_tensor(AR[:, 18 + e, :], PS[:, 4, :], -1.0 / GLA_DV, AR[:, 18 + e, :],
                                                        ALU.mult, ALU.add), t, l, "o_centered", h, e)
                    marks[(t, l, "o_mean_read", h)] = ("dve", V.n)
                    mean_square(5, GLA_DV, LN_EPS, [(t, l, "o_ms", h)], (t, l, "o_ms_read", h))
                    inverse_root([(t, l, "r_root", h)])
                    for e in range(2):
                        g = VB["gla_g"] + 2 * h + e
                        V.after((t, l, "o_sq", h, e))
                        V.done(dve.scalar_tensor_tensor(AR[:, 18 + e, :], AR[:, 18 + e, :], VEC[:, l % 2, g:g + 1],
                                                        TMP[:, 3, :], ALU.mult, ALU.mult))
                        V.after(("read", t, l, "gr", h, e))
                        V.done(dve.tensor_tensor(AR[:, 18 + e, :], AR[:, 18 + e, :], AR[:, 8 + e, :], ALU.mult),
                               t, l, "r_gated", h, e)
                    for e in range(2):
                        lo(YL[:, 2 * h + e, :], AR[:, 18 + e, :], YH[:, 2 * h + e, :], [(t, l, "r_hi", 2 * h + e)],
                           (t, l, "r_lo", 2 * h + e))
                mixer_gemms(l, t)
                for which in ("ln1", "ln2"):
                    if which == "ln2":
                        ffn(l, t, FF2_GROUPS, 2, *bases(t, l))
                        for k in range(KD):
                            marks[(t, l, "ln2_in", k)] = marks.get((t, l, "ffn_out"), ("dve", 1))
                    for k in range(KD):
                        V.after((t, l, which + "_mean"))
                        V.done(dve.scalar_tensor_tensor(X[:, k, :], PS[:, 4, :], -1.0 / D, X[:, k, :], ALU.mult, ALU.add),
                               t, l, which + "_centered", k)
                    marks[(t, l, which + "_mean_read")] = ("dve", V.n)
                    mean_square(5, D, LN_EPS, [(t, l, which + "_ms")], (t, l, which + "_ms_read"))
                    inverse_root([(t, l, which + "_root")])
                    for k in range(KD):
                        V.after((t, l, which + "_sq", k))
                        V.done(dve.tensor_tensor(X[:, k, :], X[:, k, :], TMP[:, 3, :], ALU.mult), t, l, which + "_scaled", k)
                    for k in range(KD):
                        if which == "ln1":
                            lo(XL[:, k, :], X[:, k, :], XH[:, k, :], [(t, l, "ln1_hi", k)], (t, l, "ln1_lo", k))
                        elif l + 1 < DEPTH:
                            lo(XL[:, k, :], X[:, k, :], XH[:, k, :], [(t, l + 1, "x_hi", k)], (t, l + 1, "x_lo", k))


def kernel(**inputs):
    import concourse.bacc as bacc
    from concourse.bass_utils import run_bass_kernel_spmd

    i = {k: np.asarray(v) for k, v in inputs.items()}
    consts, rot = _constants()
    wgate = np.zeros((DEPTH, 32, S), np.float32)
    for l in range(DEPTH):
        wgate[l, 0:GLA_RANK] = i["gla_w_gate_2"][l]
        wgate[l, GLA_RANK] = i["gla_b_gate_2"][l]
    arrays = {
        "stream": _stream(i), "x_t": np.ascontiguousarray(i["x"][0].T), "consts": consts, "rot": rot,
        "vectors": _vectors(i), "w_gate_in": wgate,
        "pos": np.ascontiguousarray(np.broadcast_to(i["positions_2"].astype(np.int32), (P, S))),
    }

    def build(marks):
        nc = bacc.Bacc("TRN2", target_bir_lowering=False, num_devices=1)
        args = [nc.dram_tensor(n, a.shape, mybir.dt.from_np(a.dtype), kind="ExternalInput").ap() for n, a in arrays.items()]
        args.append(nc.dram_tensor("y_t", (D, S), F32, kind="ExternalOutput").ap())
        program(nc, *args, marks)
        return nc

    marks = {}
    build(marks)
    marks["complete"] = True
    nc = build(marks)
    r = run_bass_kernel_spmd(nc, [arrays], core_ids=[0])
    return np.ascontiguousarray(r.results[0]["y_t"].T)[None]
```

```python
from contextlib import ExitStack

import numpy as np

import concourse.bass as bass
from concourse import mybir

F32 = mybir.dt.float32
F32R = mybir.dt.float32r
I32 = mybir.dt.int32
ALU = mybir.AluOpType
ACT = mybir.ActivationFunctionType
AX = mybir.AxisListType.X

P = 128
D = 1024
S = 512
DEPTH = 2
KD = D // P
NB = S // P
EPS = 1e-6
LN_EPS = 1e-5
NEG = -1.0e30
TAKEN = -3.0e38
PANEL = 2048

HD = 64
WINDOW = 128
RET_HEADS, RET_QK, RET_V = 4, 128, 256
D_FF = 4 * D
FF1_GROUPS = 8
TOPK = min(256, S // 4)
GLA_HEADS, GLA_DK, GLA_DV, GLA_RANK, GLA_TAU = 4, 128, 256, 16, 16.0
D_FF2 = 2816
FF2_GROUPS = D_FF2 // (2 * P)
DN_ALPHA = (2.0 * DEPTH) ** 0.25

NPA = 33 + 4 * FF1_GROUPS
NPB = 39 + 3 * FF2_GROUPS
NPANELS = DEPTH * (NPA + NPB)
CREDIT = 8


def _panel(rows):
    kt = rows.shape[0] // P
    return rows.reshape(kt, P, rows.shape[1]).transpose(1, 0, 2).reshape(P, -1)


def _cols(w, n=256):
    return [_panel(w[:, c:c + n]) for c in range(0, w.shape[1], n)]


def _stream(i):
    out = []
    for l in range(DEPTH):
        w = i["w_in"][l]
        q, k, v, rq, rk, rv, rg, ga, gb = np.split(w, [512, 640, 768, 1280, 1792, 2816, 3840, 4864], axis=1)
        q = q.reshape(D, 2, 4, HD).transpose(0, 2, 1, 3).reshape(D, 512)
        wa = i["w_a"][l].reshape(2, 4, HD, D).transpose(1, 0, 2, 3).reshape(512, D)
        qp = _cols(q)
        out += [qp[0], _panel(np.concatenate([k, v], 1)), qp[1]] + _cols(rq) + _cols(rk) + _cols(ga)
        out += _cols(wa, 512)
        rvp, rgp = _cols(rv), _cols(rg)
        for h in range(RET_HEADS):
            out += [rvp[h], rgp[h]]
        out += _cols(gb) + _cols(i["w_b"][l]) + _cols(i["w_out"][l])
        up = _cols(i["w_up"][l])
        down = [p for g in range(FF1_GROUPS) for p in _cols(i["w_down"][l][g * 512:(g + 1) * 512], 512)]
        out += up[0:2]
        for g in range(FF1_GROUPS):
            out += up[2 * g + 2:2 * g + 4] + down[2 * g:2 * g + 2]
    for l in range(DEPTH):
        w = i["w_in_2"][l]
        aq, ak, av, iq, ik, iw, gq, gk, gv, glr, gr, ga, gb = np.split(
            w, [512, 1024, 1536, 2048, 2112, 2120, 2632, 3144, 4168, 4184, 5208, 6232], axis=1)
        z = np.zeros((D, 1), np.float32)
        misc = np.concatenate([ik, ik, glr, np.repeat(z, 16, 1), iw, np.repeat(z, 88, 1)], axis=1)
        out += _cols(aq) + _cols(ak) + _cols(iq) + [_panel(misc)] + _cols(av) + _cols(ga)
        out += _cols(gq) + _cols(i["p_attn_2"][l], 512) + _cols(gk)
        gvp, grp = _cols(gv), _cols(gr)
        for h in range(GLA_HEADS):
            out += [gvp[h], grp[h]]
        out += _cols(gb) + _cols(i["p_gla_2"][l]) + _cols(i["w_mix_out_2"][l])
        up, down = i["w_up_2"][l], i["w_down_2"][l]
        a, b = _cols(up[:, :D_FF2]), _cols(up[:, D_FF2:])
        dn = [_panel(down[g * 256:(g + 1) * 256]) for g in range(FF2_GROUPS)]
        out += [a[0], b[0]]
        for g in range(FF2_GROUPS):
            if g + 1 < FF2_GROUPS:
                out += [a[g + 1], b[g + 1]]
            out += [dn[g]]
    assert len(out) == NPANELS
    return np.stack(out)


def _tiles(v):
    return v.reshape(-1, P).T


VA = dict(g_mix=0, g_mlp=8, sinks=16)
VB = dict(gla_g=0, b_mix=8, ln1_g=16, ln1_b=24, ln2_g=32, ln2_b=40, conv_b=48, conv_w=92, g_final=224)
VW = 232


def _vectors(i):
    out = np.zeros((2 * DEPTH, P, VW), np.float32)
    for l in range(DEPTH):
        a, b = out[l], out[DEPTH + l]
        a[:, 0:8] = _tiles(i["g_mix"][l])
        a[:, 8:16] = _tiles(i["g_mlp"][l])
        a[:, 16:24] = np.broadcast_to(i["sinks"][l].reshape(2, 4).T.reshape(1, 8), (P, 8))
        a[:, 224:232] = b[:, 224:232] = _tiles(i["g_final"])
        for name, at in (("gla_norm_g_2", 0), ("b_mix_out_2", 8), ("ln1_g_2", 16), ("ln1_b_2", 24),
                         ("ln2_g_2", 32), ("ln2_b_2", 40), ("conv_b_2", 48)):
            t = _tiles(i[name][l])
            b[:, at:at + t.shape[1]] = t
        for c in range(3):
            b[:, 92 + 44 * c:92 + 44 * (c + 1)] = _tiles(i["conv_w_2"][l, c])
    return out


CA = dict(ident=0, ones=128, perm_a=256, perm_r=384, decay=512, xi=1024, zeta=1536, mask=1540)
CB = dict(ident=0, ones=128, perm_b=256, later=384, total=512, inv=514)
CW = 1796


def _swap(pairs):
    m = np.zeros((P, P), np.float32)
    for to, of in pairs:
        m[of, to] = 1.0
    return m


def _constants():
    f = np.float32
    a, b = np.zeros((P, CW), f), np.zeros((P, CW), f)
    for c in (a, b):
        c[:, 0:128] = np.eye(P)
        c[:, 128:256] = 1.0
    half = HD // 2
    a[:, 256:384] = _swap([(r, (r // HD) * HD + (r % HD + half) % HD) for r in range(P)])
    a[:, 384:512] = _swap([(r, r ^ 1) for r in range(P)])
    idx = np.arange(P)
    scale = RET_QK ** -0.5
    for h in range(RET_HEADS):
        lg = np.log1p(-2.0 ** (-5.0 - h))
        rel = idx[None, :] - idx[:, None]
        a[:, 512 + h * P:512 + (h + 1) * P] = np.where(rel >= 0, np.exp(lg * np.maximum(rel, 0)), 0.0) * scale
        a[:, 1024 + h * P:1024 + (h + 1) * P] = np.exp(lg * (idx + 1.0))[None, :]
        a[:, 1536 + h] = np.exp(lg * (P - 1.0 - idx)) * scale
    a[:, 1540:1668] = np.where(idx[None, :] > idx[:, None], 0.0, NEG)
    a[:, 1668:1796] = np.where(idx[None, :] <= idx[:, None], 0.0, NEG)
    b[:, 256:384] = _swap([(r, r // 64 * 64 + (r % 64 + 8) % 16) if r % 64 < 16 else (r, r) for r in range(P)])
    t = np.arange(P)
    b[:, 384:512] = ((t[:, None] > t[None, :]) & (t[:, None] // 64 == t[None, :] // 64)) / GLA_TAU
    b[:, 512:514] = (t[:, None] // 64 == np.arange(2)[None, :]) / GLA_TAU
    inv = np.power(f(500000.0), -np.arange(8, dtype=f) * f(2.0) / f(16.0)).astype(f)
    b[:, 514] = [inv[r % 64 % 8] if r % 64 < 16 else 0.0 for r in range(P)]
    b[:, 515] = [(-1.0 if r % 64 < 8 else 1.0) for r in range(P)]
    rot = np.zeros((2, P, 2, S), f)
    pos = np.arange(S, dtype=f)
    inv = np.power(f(10000.0), -np.arange(half, dtype=f) / f(half)).astype(f)
    ang = (pos[None, :] * inv[np.arange(P) % half][:, None]).astype(f).astype(np.float64)
    sign = np.where(np.arange(P) % HD < half, -1.0, 1.0)[:, None]
    rot[0, :, 0], rot[0, :, 1] = np.cos(ang), np.sin(ang) * sign
    theta = (f(1.0) / np.power(f(10000.0), np.linspace(0.0, 1.0, RET_QK // 2, dtype=f))).astype(f)
    ang = (pos[None, :] * theta[np.arange(P) // 2][:, None]).astype(f).astype(np.float64)
    sign = np.where(np.arange(P) % 2 == 0, -1.0, 1.0)[:, None]
    rot[1, :, 0], rot[1, :, 1] = np.cos(ang), np.sin(ang) * sign
    return np.stack([a, b]), rot


class Steps:

    def __init__(self, eng, name, sem, marks, sems):
        self.eng, self.name, self.sem, self.marks, self.sems = eng, name, sem, marks, sems
        self.n = 0

    def after(self, *names, own=True):
        need = {}
        for name in names:
            if name is None or (name not in self.marks and not self.marks.get("complete")):
                continue
            who, n = self.marks[name]
            need[who] = max(need.get(who, 0), n)
        if own:
            need[self.name] = self.n
        for who, n in need.items():
            if n > 0:
                self.eng.wait_ge(self.sems[who], n)

    def done(self, instruction, *name):
        instruction.then_inc(self.sem, 1)
        self.n += 1
        if name:
            self.marks[name if len(name) > 1 else name[0]] = (self.name, self.n)


def program(nc, stream, x_in, consts_in, rot_in, vec_in, wgate_in, pos_in, out, marks):
    ctx = ExitStack()
    with ctx:
        def sb(name, shape, dt=F32):
            return ctx.enter_context(nc.sbuf_tensor(name, shape, dt))

        def sem(name):
            return ctx.enter_context(nc.semaphore(name))

        X = sb("x", [P, KD, S])
        XH, XL = sb("x_hi", [P, KD, S], F32R), sb("x_lo", [P, KD, S], F32R)
        with nc.sbuf_tensor("scratch", [P, 2 * KD, S], F32) as scratch:
            YSCR = scratch
        YH, YL = sb("y_hi", [P, KD, S], F32R), sb("y_lo", [P, KD, S], F32R)
        WH, WL = sb("w_hi", [P, 2, PANEL], F32R), sb("w_lo", [P, 2, PANEL], F32R)
        RAW = sb("w_raw", [P, 2, PANEL])
        AR = sb("arena", [P, 28, S])
        TMP = sb("tmp", [P, 4, S])
        CT = sb("ct", [P, CW])
        ROT = sb("rotary", [P, 2, S])
        VEC = sb("vec", [P, 2, VW])
        ST = sb("stats", [P, 108])
        WG = sb("w_gate", [32, S])
        PS = ctx.enter_context(nc.psum_tensor("ps", [P, 8, S], F32))

        raw_full = [sem("raw_full0"), sem("raw_full1")]
        hi_ready, lo_ready = sem("hi_ready"), sem("lo_ready")
        const_loaded, stored = sem("const_loaded"), sem("stored")
        x_loaded = [sem("x_loaded%d" % c) for c in range(4)]
        up_full, down_full, down_added = sem("up_full"), sem("down_full"), sem("down_added")
        sems = dict(pe=sem("pe_done"), act=sem("act_done"), dve=sem("dve_done"), const=const_loaded,
                    down_full=down_full, down_added=down_added, x0=x_loaded[0], x1=x_loaded[1], x2=x_loaded[2],
                    x3=x_loaded[3])
        up_read, hid_ready, hid_hi, hid_lo = sem("up_read"), sem("hid_ready"), sem("hid_hi"), sem("hid_lo")
        conv_begun, tap_added, gelu_done = sem("conv_begun"), sem("tap_added"), sem("gelu_done")
        block = ctx.enter_context(nc.Block())

        def unit(a, n=1):
            return AR[:, a:a + n, :]

        G = unit(20, 8)
        SB = unit(0, 8)
        n_consts = [0]

        def const_dma(eng, dst, src, name):
            if n_consts[0]:
                eng.wait_ge(const_loaded, 16 * n_consts[0])
            eng.dma_start(dst, src).then_inc(const_loaded, 16)
            n_consts[0] += 1
            marks[name] = ("const", 16 * n_consts[0])

        @block.sync
        def _(sp):
            for c in range(4):
                k = slice(2 * c, 2 * c + 2)
                sp.dma_start(X[:, k, :], x_in.rearrange("(k p) s -> p k s", p=P)[:, k, :]).then_inc(x_loaded[c], 16)
                marks[("x_in", c)] = ("x%d" % c, 16)
            sp.wait_ge(x_loaded[2], 16)
            with sp.Fori(0, NPANELS // 2) as i:
                for s in range(2):
                    sp.wait_ge(lo_ready, 2 * i + s + 1)
                    sp.dma_start(RAW[:, s, :], stream[bass.ds(2 * i + s, 1), :, :].rearrange("o p n -> p (o n)"))\
                        .then_inc(raw_full[s], 16)
            for k in range(KD):
                sp.wait_ge(sems["act"], marks.get(("b", DEPTH - 1, "ln2_x", k), ("act", 1))[1])
                sp.dma_start(out.rearrange("(k p) s -> p k s", p=P)[:, k, :], X[:, k, :]).then_inc(stored, 16)
            sp.wait_ge(stored, 16 * KD)

        @block.gpsimd
        def _(pool):
            pool.sem_inc(lo_ready, 2)
            with pool.Fori(0, NPANELS // 2) as i:
                for s in range(2):
                    pool.wait_ge(hi_ready, 2 * i + s + 1)
                    nc.gpsimd.tensor_tensor(WL[:, s, :], RAW[:, s, :], WH[:, s, :].bitcast(F32), ALU.subtract)\
                        .then_inc(lo_ready, 1)

        def at_a(l):
            n = NPA * l
            return dict(q=n, kv=n + 1, rq=n + 3, rk=n + 5, ga=n + 7, wa=n + 11, rv=n + 13, gb=n + 21, wb=n + 25,
                        wo=n + 29, ff=n + 33)

        def at_b(l):
            n = DEPTH * NPA + NPB * l
            return dict(q=n, k=n + 2, iq=n + 4, misc=n + 6, v=n + 7, ga=n + 9, gq=n + 13, wa=n + 15, gk=n + 17,
                        gv=n + 19, gb=n + 27, wb=n + 31, wo=n + 35, ff=n + 39)

        def bases(t, l):
            if t == "a":
                return 4 * FF1_GROUPS * l, 8 * FF1_GROUPS * l, 4 * FF1_GROUPS * l
            g1, g2 = FF1_GROUPS * DEPTH, FF2_GROUPS * l
            return 4 * (g1 + g2), 8 * (g1 + g2), 4 * g1 + 2 * g2

        def mask_b(b):
            if b == 3:
                return ROT[:, 0, :]
            o = 18 * S + (0, 128, 384)[b]
            return AR[:, :, :].rearrange("p a s -> p (a s)")[:, o:o + (b + 1) * P]

        def pairs_a(l):
            out = []
            for i in range(16):
                n, j = i // 4, i % 4
                k0, nk = max(n - 1, 0), min(n + 1, 2)
                out.append(dict(nk=nk * P, q=AR[:, j, n * P:(n + 1) * P], k=AR[:, 4, k0 * P:(k0 + nk) * P],
                                v=lambda kb, k0=k0: AR[:, 5, (k0 + kb) * P:(k0 + kb + 1) * P],
                                mask=CT[:, 1796 - nk * P:1796], weight=1.0, sink=2 * j,
                                ready=[("a", l, "v_read"), ("a", l, "roped", 4)],
                                o=AR[:, 14 + j, n * P:(n + 1) * P]))
            return out

        def pairs_b(l):
            out = []
            for i in range(16):
                b, j = i // 4, i % 4
                out.append(dict(nk=(b + 1) * P, q=AR[:, j, b * P:(b + 1) * P], k=AR[:, 4 + j, 0:(b + 1) * P],
                                v=lambda kb, j=j: AR[:, 14 + kb, 2 * j * 64:(2 * j + 2) * 64],
                                mask=mask_b(b), weight=-NEG, sink=None,
                                ready=[("b", l, "mask", b)] + [("read", "b", l, "av", p, m) for p in range(2) for m in range(2)],
                                o=AR[:, 8 + j, b * P:(b + 1) * P]))
            return out

        def probs(i, nk):
            return TMP[:, 2 * (i % 2):2 * (i % 2) + 2, 0:nk]

        def probs_t(i, nk):
            a = 4 + 2 * (i % 2)
            return YSCR[:, a:a + 2, 0:nk]

        def run(work, n=1):
            for _ in range(n):
                next(work, None)

        def next_rot(l, t):
            return {("a", DEPTH - 1): 0}.get((t, l), l + 1 if t == "b" and l + 1 < DEPTH else None)

        def rg_unit(h, e):
            return AR[:, (6 + 4 * e if h % 2 else e), :]

        def bank_of(*name):
            return PS[:, marks.get(("bank",) + name, 0), :]

        def up_panel(ff, g, per):
            return ff if isinstance(g, int) and g == 0 else ff + 2 + per * (g - 1)

        def down_panel(ff, g, per, groups):
            if isinstance(g, int) and g == groups - 1:
                return ff + 2 + per * (groups - 1)
            return ff + 4 + per * g

        @block.tensor
        def _(pe):
            T = Steps(pe, "pe", sems["pe"], marks, sems)
            pe.sem_inc(down_full, CREDIT)
            bank_reader = [None] * 8
            tile = [0]
            ring = [4]

            def next_bank(name):
                b = tile[0] % ring[0]
                tile[0] += 1
                marks[("bank",) + name] = b
                return b

            def split_products(ps, k, last, wh, wl, xh, xl):
                pe.matmul(ps, wh, xh, start=(k == 0), stop=False)
                pe.matmul(ps, wh, xl, start=False, stop=False)
                return pe.matmul(ps, wl, xh, start=False, stop=last)

            def gemm_tiles(n, kt, ms, xh, xl, ready, name):
                s = n % 2
                pe.wait_ge(lo_ready, n + 3)
                for m in range(ms):
                    b = next_bank(name(m))
                    T.after(bank_reader[b], own=False)
                    for k in range(kt):
                        if m == 0:
                            T.after(ready(k), own=False)
                        c = (k * ms + m) * P
                        mm = split_products(PS[:, b, :], k, k == kt - 1, WH[:, s, c:c + P], WL[:, s, c:c + P],
                                            xh[:, k, :], xl[:, k, :])
                    T.done(mm, *name(m))
                    bank_reader[b] = ("read",) + name(m)
                    if m == ms - 1:
                        marks[("panel", n)] = marks[name(m)]
                    yield

            def gemm(*args):
                for _ in gemm_tiles(*args):
                    pass

            def gemm_first(n, kt, ms, xh, xl, ready, name):
                s = n % 2
                pe.wait_ge(lo_ready, n + 3)
                banks = [next_bank(name(m)) for m in range(ms)]
                for b in banks:
                    T.after(bank_reader[b], own=False)
                for k in range(kt):
                    T.after(ready(k), own=False)
                    for m in range(ms):
                        c = (k * ms + m) * P
                        mm = split_products(PS[:, banks[m], :], k, k == kt - 1, WH[:, s, c:c + P], WL[:, s, c:c + P],
                                            xh[:, k, :], xl[:, k, :])
                        if k == kt - 1:
                            T.done(mm, *name(m))
                            bank_reader[banks[m]] = ("read",) + name(m)
                marks[("panel", n)] = marks[name(ms - 1)]

            def gemm_tok(*args):
                for _ in tok_tiles(*args):
                    pass

            def tok_tiles(n, ready, name):
                s = n % 2
                pe.wait_ge(lo_ready, n + 3)
                for t in range(NB):
                    if t % 2 == 0:
                        b = next_bank(name(t // 2))
                        T.after(bank_reader[b], own=False)
                    for k in range(KD):
                        if t == 0:
                            T.after(ready(k), own=False)
                        ps = PS[:, b, (t % 2) * 256:(t % 2) * 256 + 256]
                        xh, xl = XH[:, k, t * P:(t + 1) * P], XL[:, k, t * P:(t + 1) * P]
                        wh, wl = WH[:, s, k * 256:(k + 1) * 256], WL[:, s, k * 256:(k + 1) * 256]
                        pe.matmul(ps, xh, wh, start=(k == 0), stop=False)
                        pe.matmul(ps, xl, wh, start=False, stop=False)
                        mm = pe.matmul(ps, xh, wl, start=False, stop=(k == KD - 1))
                    if t % 2:
                        T.done(mm, *name(t // 2))
                        bank_reader[b] = ("read",) + name(t // 2)
                        if t == NB - 1:
                            marks[("panel", n)] = marks[name(1)]
                        yield

            def tok_pair(n, name, ready, t, l):
                for p in range(2):
                    yield from tok_tiles(n + p, ready, lambda m: (t, l, name, p, m))

            def column_sums(src, kt, bank, ready, after, name):
                T.after(*after, own=False)
                for k in range(kt):
                    T.after(ready(k), own=False)
                    mm = pe.matmul(PS[:, bank, :], CT[:, 128:256], src(k), start=(k == 0), stop=(k == kt - 1))
                    T.done(mm, *name, k)
                marks[name] = marks[name + (kt - 1,)]

            def token_sums(acc, bank, ready, name):
                T.after(ready, bank_reader[bank], own=False)
                for c in range(NB):
                    mm = pe.matmul(PS[:, bank, c:c + 1], acc[:, c * P:(c + 1) * P], CT[:, 128:129], start=True, stop=True)
                T.done(mm, *name)

            def keep_clock(bank, n):
                T.after(bank_reader[bank], own=False)
                for _ in range(2 * n):
                    pe.matmul(PS[:, bank, 0:2 * P], CT[:, 128:256], CT[:, 0:256], start=True, stop=True)

            def spread(bank, ready, name):
                T.after(ready, bank_reader[bank], own=False)
                T.done(pe.matmul(PS[:, bank, :], CT[:, 128:256], TMP[:, 3, :], start=True, stop=True), *name)

            def inverse_deviation(bank, t, l, which):
                token_sums(TMP[:, 2, :], bank, (t, l, which + "_acc", KD - 1), (t, l, which + "_ms"))
                bank_reader[bank] = (t, l, which + "_root")
                keep_clock(bank + 1, 1)
                spread(bank + 1, (t, l, which + "_diagonal"), (t, l, which + "_spread"))
                bank_reader[bank + 1] = (t, l, which + "_scaled", KD - 1)
                keep_clock(bank, 2)

            def swapped(src, perm, bank, after, name):
                T.after(*after, own=False)
                T.done(pe.matmul(PS[:, bank, :], perm, src, start=True, stop=True), *name)

            def attention(pairs, l, t, fillers, steps):
                ring[0] = 2

                def scores(i):
                    U, nk = pairs[i], pairs[i]["nk"]
                    for v in range(2):
                        h = slice(64 * v, 64 * v + 64)
                        T.after(*U["ready"], (t, l, "s_read", i - 1) if i else bank_reader[4 + v], own=False)
                        mm = pe.matmul(PS[:, 4 + v, 0:nk], U["q"][h], U["k"][h], start=True, stop=True)
                    T.done(mm, t, l, "s", i)

                def transposes(i):
                    nk = pairs[i]["nk"]
                    T.after((t, l, "p", i), *[(t, l, "pt_read", i - 1)] if i else bank_reader[6:8], own=False)
                    for v in range(2):
                        for c in range(0, nk, P):
                            mm = pe.transpose(PS[:, 6 + v, c:c + P], probs(i, nk)[:, v, c:c + P], CT[:, 0:128])
                    T.done(mm, t, l, "pt", i)

                def outputs(i):
                    U, n = pairs[i], pairs[i]["nk"] // P
                    T.after((t, l, "pt_read", i), (t, l, "o_read", i - 1) if i else bank_reader[2], own=False)
                    for kb in range(n):
                        mm = pe.matmul(PS[:, 2, 0:2 * P], U["v"](kb), probs_t(i, n * P)[:, :, kb * P:(kb + 1) * P],
                                       start=(kb == 0), stop=(kb == n - 1))
                    T.done(mm, t, l, "o", i)

                scores(0)
                for i in range(16):
                    if i < 15:
                        scores(i + 1)
                    transposes(i)
                    run(fillers)
                    outputs(i)
                    run(steps)
                for _ in fillers:
                    pass
                bank_reader[2] = (t, l, "o_read", 15)
                bank_reader[4] = bank_reader[5] = (t, l, "s_read", 15)
                bank_reader[6] = bank_reader[7] = (t, l, "pt_read", 15)
                ring[0] = 4

            def gate_tiles(l, w, t):
                for p in range(4):
                    yield from gemm_tiles(w["gb"] + p, KD, 2, XH, XL, lambda k: None, lambda m: (t, l, "gb", 2 * p + m))

            def mixer_gemms(l, w, t, gates):
                for _ in gates:
                    pass
                for p in range(4):
                    (gemm if p else gemm_first)(w["wb"] + p, KD, 2, YH, YL, lambda k: (t, l, "r_lo", k), lambda m: (t, l, "wb", 2 * p + m))
                for p in range(4):
                    (gemm if p else gemm_first)(w["wo"] + p, KD, 2, XH, XL, lambda k: (t, l, "merged_lo", k),
                         lambda m: (t, l, "wo", 2 * p + m))

            def ffn(l, t, ff, groups, kt, base_t, base_d, base_h, h_ready):
                per = 2 + (2 if kt == 4 else 1)
                for b in range(4):
                    T.after(bank_reader[b], own=False)

                def up(g, s):
                    n = up_panel(ff, g, per)
                    slot = (up_panel(ff, s if isinstance(g, int) else s + 2, per)) % 2
                    for p in range(2):
                        pe.wait_ge(lo_ready, n + p + 3)
                        if isinstance(g, int) and g == 0 and p == 0:
                            if l or t == "b":
                                pe.wait_ge(up_read, base_t)
                            for k in range(KD):
                                T.after(h_ready(k), own=False)
                                for m in range(2):
                                    c = (k * 2 + m) * P
                                    mm = split_products(PS[:, m, :], k, k == KD - 1, WH[:, slot, c:c + P],
                                                        WL[:, slot, c:c + P], XH[:, k, :], XL[:, k, :])
                                    if k == KD - 1:
                                        mm.then_inc(up_full, 1)
                            continue
                        for m in range(2):
                            j = 2 * p + m
                            if not (isinstance(g, int) and g == 0 and l == 0):
                                pe.wait_ge(up_read, base_t + 4 * g + j - 3)
                            for k in range(KD):
                                c = (k * 2 + m) * P
                                sl = (slot + p) % 2
                                mm = split_products(PS[:, j, :], k, k == KD - 1, WH[:, sl, c:c + P],
                                                    WL[:, sl, c:c + P], XH[:, k, :], XL[:, k, :])
                            mm.then_inc(up_full, 1)

                def down(g, s):
                    n = down_panel(ff, g, per, groups)
                    slot = down_panel(ff, s if isinstance(g, int) else s + 2, per, groups if isinstance(g, int) else 99) % 2
                    pe.wait_ge(hid_lo, base_h + kt * (g + 1))
                    ms = 16 // kt
                    for p in range(kt * 8 // 16):
                        pe.wait_ge(lo_ready, n + p + 3)
                        for m in range(ms):
                            d = p * ms + m
                            pe.wait_ge(down_added, CREDIT + base_d + 8 * g + d - 3)
                            for k in range(kt):
                                c = (k * ms + m) * P
                                sl = (slot + p) % 2
                                mm = split_products(PS[:, 4 + d % 4, :], k, k == kt - 1, WH[:, sl, c:c + P],
                                                    WL[:, sl, c:c + P], YH[:, kt * (s % 2) + k, :],
                                                    YL[:, kt * (s % 2) + k, :])
                            mm.then_inc(down_full, 1)

                up(0, 0)
                for b in range(4, 8):
                    T.after(bank_reader[b], own=False)
                trips = (groups - 1) // 2
                with pe.Fori(0, trips) as i:
                    up(2 * i + 1, 1)
                    down(2 * i, 0)
                    up(2 * i + 2, 2)
                    down(2 * i + 1, 1)
                for g in range(2 * trips, groups):
                    if g + 1 < groups:
                        up(g + 1, g + 1)
                    down(g, g)
                for b in range(8):
                    bank_reader[b] = (t, l, "ffn_out")
                done = CREDIT + base_d + 8 * groups
                marks[(t, l, "ffn_out")] = ("down_added", done)
                for k in range(KD):
                    marks[(t, l, "ffn_out", k)] = ("down_added", done - KD + 1 + k)
                end = ff + per * groups
                marks[("panel", end - 1)] = ("down_full", done)
                marks[("panel", end - 2)] = ("down_full", done - (4 if kt == 4 else 8))

            for l in range(DEPTH):
                w, t = at_a(l), "a"
                if l == 0:
                    T.after("ident_ones", own=False)
                inverse_deviation(4, t, l, "n1")
                h_ready = lambda k: (t, l, "h_lo", k)
                before = {4: ("roped", 0), 2: ("roped", 4), 3: ("roped", 1)}

                def swap_a(j):
                    swapped(AR[:, j, :], CT[:, 256:384], 4 + j % 2,
                            [("read", t, l, "q", j), (t, l, "n1_scaled", KD - 1) if j < 2 else (t, l) + before[j]],
                            (t, l, "swap", j))

                gemm_first(w["q"], KD, 2, XH, XL, h_ready, lambda m: (t, l, "q", m))
                gemm(w["kv"], KD, 2, XH, XL, h_ready, lambda m: (t, l, "q", 4 + m))
                T.after("consts_a", own=False)
                swap_a(0)
                swap_a(1)
                gemm(w["q"] + 2, KD, 2, XH, XL, h_ready, lambda m: (t, l, "q", 2 + m))
                swap_a(4)
                T.after(("read", t, l, "q", 5), bank_reader[6], own=False)
                for n in range(NB):
                    mm = pe.transpose(PS[:, 6, n * P:(n + 1) * P], AR[:, 18, n * P:(n + 1) * P], CT[:, 0:128])
                T.done(mm, t, l, "v_tok")

                def retention_tiles(p):
                    return gemm_tiles(w["rq"] + p, KD, 2, XH, XL, h_ready, lambda m: (t, l, "rqk", 2 * p + m))

                for _ in retention_tiles(0):
                    pass
                swap_a(2)
                swap_a(3)
                bank_reader[4], bank_reader[5], bank_reader[6] = (t, l, "roped", 2), (t, l, "roped", 3), (t, l, "v_read")

                def fillers():
                    for p in range(1, 4):
                        yield from retention_tiles(p)
                    for p in range(4):
                        yield from gemm_tiles(w["ga"] + p, KD, 2, XH, XL, h_ready, lambda m: (t, l, "ga", 2 * p + m))

                def retention_swaps():
                    for j in range(8):
                        swapped(AR[:, 6 + j, :], CT[:, 384:512], 3,
                                [("read", t, l, "rqk", j), (t, l, "roped", 4 + j) if j else bank_reader[3]],
                                (t, l, "swap", 5 + j))
                        yield

                attention(pairs_a(l), l, t, fillers(), retention_swaps())
                bank_reader[3] = (t, l, "roped", 12)
                for p in range(2):
                    (gemm if p else gemm_first)(w["wa"] + p, 4, 4, YH, YL, lambda k: (t, l, "ao_lo", k),
                                                lambda m: (t, l, "wa", 4 * p + m))
                gemm_tok(w["rv"], h_ready, lambda m: (t, l, "rv", 0, m))
                ring[0] = 2
                gates = gate_tiles(l, w, t)

                def fillers():
                    for h in range(RET_HEADS):
                        yield from gemm_tiles(w["rv"] + 2 * h + 1, KD, 2, XH, XL, h_ready, lambda m: (t, l, "rg", h, m))
                        if h + 1 < RET_HEADS:
                            yield from tok_tiles(w["rv"] + 2 * h + 2, h_ready, lambda m: (t, l, "rv", h + 1, m))
                    yield from gates

                def retention_squares(h):
                    column_sums(lambda e: AR[:, 2 + e, :], 2, 3, lambda e: (t, l, "r_sq", h, e),
                                [(t, l, "r_ms_read", h - 1) if h else bank_reader[3]], (t, l, "r_ms", h))

                fill = fillers()
                for h in range(RET_HEADS):
                    q, k, v = AR[:, 6 + h, :], AR[:, 10 + h, :], AR[:, 14 + 2 * (h % 2):16 + 2 * (h % 2), :].rearrange("p a (b e) -> p (a b) e", b=2)
                    run(fill)
                    T.after((t, l, "r_out_read", h - 1) if h else (t, l, "s_read", 15), own=False)
                    for c in range(NB):
                        mm = pe.matmul(PS[:, 4, c * P:(c + 1) * P], k[:, c * P:(c + 1) * P], q[:, c * P:(c + 1) * P],
                                       start=True, stop=True)
                    T.done(mm, t, l, "rs", h)
                    for c in range(NB):
                        mm = pe.transpose(PS[:, 5, c * P:(c + 1) * P], k[:, c * P:(c + 1) * P], CT[:, 0:128])
                    T.done(mm, t, l, "rkt", h)
                    if h:
                        retention_squares(h - 1)
                    run(fill)
                    T.after((t, l, "kz", h), ("read", t, l, "rv", h, 0), ("read", t, l, "rv", h, 1),
                            (t, l, "state", h - 1, 3) if h else (t, l, "pt_read", 15), own=False)
                    for c in range(NB - 1):
                        mm = pe.matmul(PS[:, 6 + c // 2, (c % 2) * 256:(c % 2) * 256 + 256], TMP[:, 1, c * P:(c + 1) * P],
                                       v[:, c, :], start=True, stop=True)
                    T.done(mm, t, l, "kv", h)
                    run(fill, 2 if h + 1 < RET_HEADS else 1)
                    T.after((t, l, "rs_decayed", h), (t, l, "qx", h), (t, l, "state", h, 3), own=False)
                    for e in range(2):
                        for c in range(NB):
                            ps = PS[:, 4 + e, c * P:(c + 1) * P]
                            mm = pe.matmul(ps, v[:, c, e * P:(e + 1) * P], TMP[:, 0, c * P:(c + 1) * P],
                                           start=True, stop=(c == 0))
                            if c:
                                o = 4 * S + (c - 1) * 256 + e * P
                                mm = pe.matmul(ps, AR[:, o // S, o % S:o % S + P], TMP[:, 2, c * P:(c + 1) * P],
                                               start=False, stop=True)
                        T.done(mm, t, l, "r_out", h, e)
                run(fill)
                retention_squares(RET_HEADS - 1)
                bank_reader[3] = (t, l, "r_ms_read", 3)
                bank_reader[4] = bank_reader[5] = (t, l, "r_out_read", 3)
                bank_reader[6] = bank_reader[7] = (t, l, "state", 3, 3)
                mixer_gemms(l, w, t, gates)
                ring[0] = 4
                inverse_deviation(6, t, l, "n2")
                ffn(l, t, w["ff"], FF1_GROUPS, 4, *bases(t, l), lambda k: (t, l, "h2_lo", k))
            inverse_deviation(4, "f", 0, "n1")

            for l in range(DEPTH):
                w, t = at_b(l), "b"
                T.after("consts_b", own=False)
                h_ready = lambda k: (t, l, "x_lo", k)
                def swap_b(j):
                    swapped(AR[:, j, :], CT[:, 256:384], 4 + j % 2,
                            [("read", t, l, "q", j), (t, l, "rot_tables"), (t, l, "roped", j - 2) if j > 1 else bank_reader[4 + j]],
                            (t, l, "swap", j))

                for i in range(7):
                    (gemm if i else gemm_first)(w["q"] + i, KD, 2, XH, XL, h_ready, lambda m: (t, l, "q", 2 * i + m))
                    if i:
                        swap_b(2 * i - 2)
                        swap_b(2 * i - 1)
                fillers = tok_pair(w["v"], "av", h_ready, t, l)
                run(fillers)
                swap_b(12)
                T.after(("read", t, l, "q", 13), bank_reader[6], own=False)
                for n in range(NB):
                    mm = pe.transpose(PS[:, 6, n * P:(n + 1) * P], AR[:, 18, n * P:(n + 1) * P], CT[:, 0:128])
                T.done(mm, t, l, "iw")
                run(fillers)
                for i in range(12):
                    b, j, bank = 1 + i // 4, i % 4, 4 + 2 * (i % 2)
                    T.after((t, l, "dots_read", i - 2) if i >= 2 else (t, l, "roped", 12), (t, l, "iw_read"),
                            bank_reader[7], own=False)
                    for v in range(2):
                        h = slice(64 * v, 64 * v + 64)
                        mm = pe.matmul(PS[:, bank + v, 0:(b + 1) * P], AR[h, 8 + j, b * P:(b + 1) * P],
                                       AR[h, 12, 0:(b + 1) * P], start=True, stop=True)
                    T.done(mm, t, l, "dots", i)
                    if i in (3, 7):
                        run(fillers)
                bank_reader[4] = bank_reader[5] = (t, l, "dots_read", 10)
                bank_reader[6] = bank_reader[7] = (t, l, "dots_read", 11)

                def fillers():
                    for p in range(4):
                        yield from gemm_tiles(w["ga"] + p, KD, 2, XH, XL, h_ready, lambda m: (t, l, "ga", 2 * p + m))
                    for p in range(2):
                        yield from gemm_tiles(w["gq"] + p, KD, 2, XH, XL, h_ready, lambda m: (t, l, "gq", 2 * p + m))

                attention(pairs_b(l), l, t, fillers(), iter(()))
                for p in range(2):
                    (gemm if p else gemm_first)(w["wa"] + p, 4, 4, YH, YL, lambda k: (t, l, "ao_lo", k),
                                                lambda m: (t, l, "wa", 4 * p + m))
                T.after((t, l, "glr"), ("w_gate", l), own=False)
                for n in range(NB):
                    T.after((t, l, "la", n - 2) if n >= 2 else (t, l, "s_read", 15), own=False)
                    T.done(pe.matmul(PS[:, 4 + n % 2, :], AR[0:32, 13, n * P:(n + 1) * P], WG[:, :],
                                     start=True, stop=True), t, l, "gate", n)
                for p in range(2):
                    gemm_tok(w["gk"] + p, h_ready, lambda m: (t, l, "gk", p, m))
                for n in range(NB):
                    T.after((t, l, "decay_read", n - 2) if n >= 2 else (t, l, "la", 3), own=False)
                    T.done(pe.matmul(PS[:, 4 + n % 2, :], CT[:, 384:512], AR[:, 8 + n, :], start=True, stop=True),
                           t, l, "decay", n)
                T.after((t, l, "pt_read", 15), own=False)
                for h in range(GLA_HEADS):
                    for n in range(NB):
                        mm = pe.matmul(PS[:, 6, h * 8 + 2 * n:h * 8 + 2 * n + 2], AR[:, 8 + n, h * P:(h + 1) * P],
                                       CT[:, 512:514], start=True, stop=True)
                T.done(mm, t, l, "totals")
                gemm_tok(w["gv"], h_ready, lambda m: (t, l, "gv", 0, m))
                ring[0] = 2
                gates = gate_tiles(l, w, t)

                def fillers():
                    for h in range(GLA_HEADS):
                        yield from gemm_tiles(w["gv"] + 2 * h + 1, KD, 2, XH, XL, h_ready, lambda m: (t, l, "gr", h, m))
                        if h + 1 < GLA_HEADS:
                            yield from tok_tiles(w["gv"] + 2 * h + 2, h_ready, lambda m: (t, l, "gv", h + 1, m))
                    yield from gates

                def mean(h):
                    column_sums(lambda e: AR[:, 18 + e, :], 2, 2, lambda e: (t, l, "o_copied", h, e),
                                [(t, l, "o_centered", h - 1, 1) if h else bank_reader[2]], (t, l, "o_mean", h))

                def variance(h):
                    column_sums(lambda e: TMP[:, e, :], 2, 3, lambda e: (t, l, "o_sq", h, e),
                                [(t, l, "o_ms_read", h - 1) if h else bank_reader[3]], (t, l, "o_ms", h))

                fill = fillers()
                for h in range(GLA_HEADS):
                    v = AR[:, 14 + 2 * (h % 2):16 + 2 * (h % 2), :].rearrange("p a (b e) -> p (a b) e", b=2)
                    T.after(("read", t, l, "gv", h, 0), ("read", t, l, "gv", h, 1), (t, l, "totals_read"),
                            (t, l, "kd", 3), own=False)

                    def kv(c):
                        hp = 64 * (c % 2)
                        if c % 2:
                            T.after()
                        else:
                            T.after((t, l, "state", h, c - 3) if c >= 4 else ((t, l, "state", h - 1, c + 5) if h else None),
                                    own=False)
                        T.done(pe.matmul(PS[:, 4 + (c // 2) % 2, (c % 2) * 256:(c % 2) * 256 + 256],
                                         AR[hp:hp + 64, 4 + c // 2, h * P:(h + 1) * P],
                                         v[hp:hp + 64, c // 2, :], start=True, stop=True), t, l, "gkv", h, c)

                    if h:
                        mean(h - 1)
                    kv(0)
                    kv(1)
                    for c in range(8):
                        if c % 2 == 0 and c + 2 < 8:
                            kv(c + 2)
                            kv(c + 3)
                        T.after((t, l, "state", h, c), (t, l, "o_out_read", h - 1) if h and c == 0 else None, own=False)
                        for e in range(2):
                            mm = pe.matmul(PS[:, 6 + e, c * 64:(c + 1) * 64],
                                           AR[:, 12, (c % 2) * 256 + e * P:(c % 2) * 256 + (e + 1) * P],
                                           YSCR[:, KD + 4 + h, c * 64:(c + 1) * 64], start=True, stop=True)
                        T.done(mm, t, l, "g_out", h, c)
                        if c % 2:
                            run(fill)
                        if c == 1 and h:
                            variance(h - 1)
                mean(GLA_HEADS - 1)
                run(fill, 2)
                variance(GLA_HEADS - 1)
                bank_reader[2], bank_reader[3] = (t, l, "o_centered", 3, 1), (t, l, "o_ms_read", 3)
                bank_reader[4], bank_reader[5] = (t, l, "state", 3, 5), (t, l, "state", 3, 7)
                bank_reader[6] = bank_reader[7] = (t, l, "o_out_read", 3)
                mixer_gemms(l, w, t, gates)
                ring[0] = 4
                for which in ("ln1", "ln2"):
                    if which == "ln2":
                        ffn(l, t, w["ff"], FF2_GROUPS, 2, *bases(t, l), lambda k: (t, l, "ln1_lo", k))
                    column_sums(lambda k: TMP[:, 2, :], 1, 4, lambda k: (t, l, which + "_sum", KD - 1), [bank_reader[4]],
                                (t, l, which + "_mean"))
                    bank_reader[4] = (t, l, which + "_centered", KD - 1)
                    column_sums(lambda k: TMP[:, k % 2, :], KD, 5, lambda k: (t, l, which + "_sq", k), [bank_reader[5]],
                                (t, l, which + "_ms"))
                    bank_reader[5] = (t, l, which + "_root")
                    if (which, l) != ("ln2", DEPTH - 1):
                        keep_clock(4, 5)

        @block.scalar
        def _(act):
            A = Steps(act, "act", sems["act"], marks, sems)

            def hi(c, k=0, i=0, used=None):
                if not k and c >= NPANELS:
                    return
                s = c % 2
                act.wait_ge(raw_full[s], 16 * (c // 2 + 1) + 8 * k * i)
                if used is not None:
                    act.wait_ge(*used)
                elif c >= 2:
                    who, n = marks.get(("panel", c - 2), ("pe", 1))
                    act.wait_ge(sems[who], n)
                act.activation(WH[:, s, :], RAW[:, s, :], ACT.Copy).then_inc(hi_ready, 1)

            def read(name, dst, func=ACT.Copy, *after, **kw):
                A.after(name, *after)
                A.done(act.activation(dst, bank_of(*name), func, **kw), *(("read",) + name))

            def split_hi(dst, src, after, name, own=True):
                A.after(*after, own=own)
                A.done(act.activation(dst, src, ACT.Copy), *name)

            def squares(src, kt, dst, ready, used, name):
                for k in range(kt):
                    A.after(ready(k), used(k))
                    A.done(act.activation(dst(k), src(k), ACT.Square), *name, k)
                    yield

            def norm_squares(t, l, which, x_ready):
                return squares(lambda k: X[:, k, :], KD, lambda k: TMP[:, k % 2, :], x_ready,
                               lambda k: (t, l, which + "_acc", max(k - 2, 1)) if k >= 2 else None, (t, l, which + "_sq"))

            def root(sums, n, eps, name, after):
                A.after(*after)
                e = 96 if eps == EPS else 97
                A.done(act.activation(TMP[:, 3, :], sums, ACT.Sqrt, scale=1.0 / n, bias=ST[:, e:e + 1]), *name)

            def attention(pairs, l, t, fillers):
                def exponentials(i):
                    U, c, pr = pairs[i], 8 * (i % 2), probs(i, pairs[i]["nk"])
                    A.after((t, l, "negmax", i))
                    for v in range(2):
                        if v:
                            A.after()
                        A.done(act.activation(pr[:, v, :], pr[:, v, :], ACT.Exp, bias=ST[:, c + 2 + v:c + 3 + v],
                                              scale=HD ** -0.5, accum_out=ST[:, c + 4 + v:c + 5 + v]), t, l, "exp", i)
                    if U["sink"] is not None:
                        A.after()
                        A.done(act.activation(ST[:, c + 6:c + 8], ST[:, c + 6:c + 8], ACT.Exp), t, l, "exp", i)

                def read_transposes(i):
                    nk = pairs[i]["nk"]
                    A.after((t, l, "pt", i), (t, l, "o", i - 2) if i >= 2 else None)
                    A.done(act.activation(probs_t(i, nk), PS[:, 6:8, 0:nk], ACT.Copy), t, l, "pt_read", i)

                def read_outputs(i):
                    A.after((t, l, "o", i))
                    for v in range(2):
                        if v:
                            A.after()
                        h = slice(64 * v, 64 * v + 64)
                        A.done(act.activation(pairs[i]["o"][h], PS[h, 2, v * P:(v + 1) * P], ACT.Copy), t, l, "o_read", i)

                exponentials(0)
                for i in range(16):
                    read_transposes(i)
                    if i < 15:
                        exponentials(i + 1)
                    run(fillers)
                    read_outputs(i)
                    if i >= 12:
                        j = i - 12
                        split_hi(YH[:, j, :], (AR[:, 14 + j, :] if t == "a" else AR[:, 8 + j, :]), [], (t, l, "ao_hi", j))
                for _ in fillers:
                    pass

            def gate_reads(l, w, t):
                for p in range(4):
                    hi(w["gb"] + p + 1)
                    for m in range(2):
                        j = 2 * p + m
                        free = (t, l, "r_gated", 3, 1) if j >= 6 else (t, l, "r_ms", 3) if j in (2, 3) else (t, l, "r_gated", 2, 1)
                        read((t, l, "gb", j), SB[:, j, :], ACT.Sigmoid, free if t == "a" else None)
                        yield

            def mixer_gemms(l, w, t, gates, squared=iter(())):
                rot = next_rot(l, t)
                if rot is not None:
                    run(gates, 1)
                    if t == "a":
                        const_dma(act, CT[:, 256:CW], consts_in[1, :, 256:CW], "consts_b")
                        run(gates, 2)
                    const_dma(act, AR[:, 12, :].bitcast(I32), pos_in, ("pos", rot))
                for _ in gates:
                    pass
                if rot is not None:
                    A.after(("b", rot, "angle"))
                    A.done(act.activation(ROT[:, 1, :], AR[:, 13, :], ACT.Sin))
                    A.after()
                    A.done(act.activation(AR[:, 12, :], AR[:, 13, :], ACT.Sin, scale=0.5), "b", rot, "sines")
                if t == "b":
                    for k in range(KD):
                        A.after()
                        A.done(act.activation(X[:, k, :], X[:, k, :], ACT.Identity, scale=DN_ALPHA,
                                              bias=VEC[:, l % 2, VB["b_mix"] + k:VB["b_mix"] + k + 1]), t, l, "x_scaled", k)
                for p in range(4):
                    hi(w["wb"] + p + 1)
                    for m in range(2 * p, 2 * p + 2):
                        split_hi(XH[:, m, :], G[:, m, :], [(t, l, "merged", m)], (t, l, "merged_hi", m))
                for p in range(4):
                    hi(w["wo"] + p + 1)
                    if p:
                        run(squared, 2)

            def ffn(l, t, ff, groups, kt, base_t, base_d, base_h):
                per = 2 + (2 if kt == 4 else 1)
                base_c = base_d - 8 * FF1_GROUPS * DEPTH if kt == 2 else 0
                base_c = base_c // 2
                downs = per - 2

                def up_used(g, p):
                    return up_full, base_t + 4 * g + 2 * (p + 1)

                def down_used(g, p):
                    return down_full, CREDIT + base_d + 8 * g + (8 // downs) * (p + 1)

                def hi_up(gc, gi, i, p):
                    g = gc + gi * i
                    if gi == 0 and gc == 1:
                        used = up_used(0, p)
                    elif downs == 2 or p == 1:
                        act.wait_ge(*up_used(g - 1, p))
                        used = down_used(g - 2, p if downs == 2 else 0)
                    else:
                        used = up_used(g - 1, 1)
                    hi(up_panel(ff, gc, per) + p, per * gi, i, used)

                def hi_down(gc, gi, i, p):
                    g = gc + gi * i
                    last = gi == 0 and gc == groups - 1
                    if downs == 2:
                        used = down_used(g - 1, p) if last else up_used(g + 1, p)
                    else:
                        used = up_used(g, 1) if last else up_used(g + 1, 0)
                    hi(down_panel(ff, gc, per, groups if gi == 0 else 99) + p, per * gi, i, used)

                def up(gc, gi, i):
                    g = gc + gi * i
                    t0 = base_t + 4 * g
                    buf = gc % 2
                    for p in range(2):
                        if p == 0:
                            if not (gi == 0 and gc == 0):
                                hi_up(gc, gi, i, 1)
                        elif gi == 0 and gc == 0:
                            hi_up(1, 0, 0, 0)
                        else:
                            hi_down(gc - 1, gi, i, 0)
                        if kt == 2 and p == 1:
                            for m in range(2):
                                act.wait_ge(up_read, t0 + m + 1)
                                if not (gi == 0 and gc == 0):
                                    act.wait_ge(hid_ready, base_h + 2 * g + m - 1)
                                act.activation(AR[:, 4 + m, :], AR[:, m, :], ACT.Gelu_apprx_tanh).then_inc(gelu_done, 1)
                        for m in range(2):
                            j = 2 * p + m
                            act.wait_ge(up_full, t0 + j + 1)
                            if kt == 2:
                                if not (gi == 0 and gc == 0):
                                    if p == 0:
                                        act.wait_ge(gelu_done, base_c // 2 + 2 * g)
                                    else:
                                        act.wait_ge(hid_ready, base_h + 2 * g)
                                ch = 2 * g + m + (2 * FF2_GROUPS if p else 0)
                                tap, bias = VB["conv_w"] + 88 + ch, VB["conv_b"] + ch
                                act.activation(AR[:, j, :], PS[:, j, :], ACT.Identity, scale=VEC[:, l % 2, bass.ds(tap, 1)],
                                               bias=VEC[:, l % 2, bass.ds(bias, 1)]).then_inc(conv_begun, 1)
                            if kt == 4:
                                if not (gi == 0 and gc == 0 and base_t == 0):
                                    act.wait_ge(hid_ready, base_h + 4 * g + j - 3)
                                act.activation(AR[:, j, :], PS[:, j, :], ACT.Relu).then_inc(up_read, 1)
                        if kt == 4:
                            for m in range(2):
                                j = 2 * p + m
                                act.wait_ge(hid_ready, base_h + 4 * g + j + 1)
                                if not (gi == 0 and gc < 2):
                                    act.wait_ge(down_full, CREDIT + base_d + 8 * (g - 1))
                                act.activation(YH[:, 4 * buf + j, :], AR[:, 4 + j, :], ACT.Copy).then_inc(hid_hi, 1)
                    if kt == 2:
                        for m in range(2):
                            act.wait_ge(hid_ready, base_h + 2 * g + m + 1)
                            if not (gi == 0 and gc < 2):
                                act.wait_ge(down_full, CREDIT + base_d + 8 * (g - 1))
                            act.activation(YH[:, 2 * buf + m, :], AR[:, 6 + m, :], ACT.Copy).then_inc(hid_hi, 1)

                def down(gc, gi, i):
                    last = gi == 0 and gc == groups - 1
                    nxt_up = not (gi == 0 and gc >= groups - 2)
                    if downs == 2:
                        hi_down(gc, gi, i, 1)
                    if nxt_up:
                        hi_up(gc + 2, gi, i, 0)
                    elif not last:
                        hi_down(groups - 1, 0, 0, 0)
                    else:
                        hi(ff + per * groups)

                A.after()
                up(0, 0, 0)
                trips = (groups - 1) // 2
                with act.Fori(0, trips) as i:
                    up(1, 2, i)
                    down(0, 2, i)
                    up(2, 2, i)
                    down(1, 2, i)
                for g in range(2 * trips, groups):
                    if g + 1 < groups:
                        up(g + 1, 0, 0)
                    down(g, 0, 0)

            def warm_root():
                A.after("eps")
                A.done(act.activation(ST[:, 98:99], ST[:, 96:97], ACT.Sqrt))

            def token_root(bank, ready, name):
                A.after(ready)
                A.done(act.activation(ST[:, 100:104], PS[:, bank, 0:NB], ACT.Sqrt, scale=1.0 / D, bias=ST[:, 96:97]), *name)

            def norm(t, l, which, squared, bank, second_panel, to_x=False):
                for _ in squared:
                    pass
                if (t, l, which) == ("a", 0, "n1"):
                    const_dma(act, CT[:, 256:CW], consts_in[0, :, 256:CW], "consts_a")
                    hi(0)
                warm_root()
                token_root(bank, (t, l, which + "_ms"), (t, l, which + "_root"))
                hi(second_panel)
                for k in range(KD):
                    src = X[:, k, :] if to_x else TMP[:, k % 2, :]
                    hn = ("b", 0, "x_hi", k) if to_x else (t, l, ("h_hi" if which == "n1" else "h2_hi"), k)
                    split_hi(XH[:, k, :], src, [(t, l, which + "_scaled", k)], hn, own=False)

            const_dma(act, CT[:, 0:256], consts_in[0, :, 0:256], "ident_ones")
            const_dma(act, VEC[:, 0, :], vec_in[0], "vec0")
            for l in range(DEPTH):
                w, t = at_a(l), "a"
                if l:
                    A.after((t, l - 1, "roped", 12))
                    const_dma(act, ROT[:, :, :], rot_in[0], ("rot", l, 0))
                norm(t, l, "n1", norm_squares(t, l, "n1", lambda k: ("x_in", k // 2) if l == 0 else (t, l - 1, "ffn_out", k)), 4,
                     w["q"] + 1)
                if l == 0:
                    const_dma(act, ROT[:, :, :], rot_in[0], ("rot", l, 0))
                for m in range(2):
                    read((t, l, "q", m), AR[:, m, :])
                hi(w["kv"] + 1)
                read((t, l, "q", 4), AR[:, 4, :])
                read((t, l, "q", 5), AR[:, 18, :])
                hi(w["q"] + 3)
                for m in range(2, 4):
                    read((t, l, "q", m), AR[:, m, :])
                A.after((t, l, "v_tok"))
                A.done(act.activation(AR[:, 5, :], PS[:, 6, :], ACT.Copy), t, l, "v_read")

                def retention_reads(p):
                    hi(w["rq"] + p + 1)
                    for m in range(2):
                        read((t, l, "rqk", 2 * p + m), AR[:, 6 + 2 * p + m, :])
                        yield

                def filler_reads():
                    for p in range(1, 4):
                        yield from retention_reads(p)
                    for p in range(4):
                        hi(w["ga"] + p + 1)
                        for m in range(2):
                            read((t, l, "ga", 2 * p + m), G[:, 2 * p + m, :], ACT.Sigmoid)
                            yield

                for _ in retention_reads(0):
                    pass
                if l == 0:
                    const_dma(act, VEC[:, 1, :], vec_in[1], "vec1")
                A.after((t, l, "roped", 3))
                const_dma(act, ROT[:, :, :], rot_in[1], ("rot", l, 1))
                attention(pairs_a(l), l, t, filler_reads())
                for p in range(2):
                    hi(w["wa"] + p + 1)

                def rv_reads(h):
                    hi(w["rv"] + 2 * h + 1)
                    for m in range(2):
                        read((t, l, "rv", h, m), AR[:, 14 + 2 * (h % 2) + m, :], ACT.Copy, (t, l, "ao_lo", 3),
                             (t, l, "r_out", h - 2, 1) if h >= 2 else None)
                        yield

                gates = gate_reads(l, w, t)

                def retention_fill_reads():
                    for h in range(RET_HEADS):
                        hi(w["rv"] + 2 * h + 2)
                        for m in range(2):
                            read((t, l, "rg", h, m), rg_unit(h, m), ACT.Silu,
                                 (t, l, "r_gated", h - 2, m) if h >= 2 else (t, l, "r_out", h - 1, 1) if h else None)
                            yield
                        if h + 1 < RET_HEADS:
                            yield from rv_reads(h + 1)
                    yield from gates

                for _ in rv_reads(0):
                    pass
                reads = retention_fill_reads()
                for h in range(RET_HEADS + 1):
                    run(reads)
                    if h < RET_HEADS:
                        A.after((t, l, "rkt", h), (t, l, "kv", h - 1) if h else (t, l, "pt", 15))
                        z = CA["zeta"] + h
                        A.done(act.activation(TMP[:, 1, :], PS[:, 5, :], ACT.Copy, scale=CT[:, z:z + 1]), t, l, "kz", h)
                    if h:
                        root(PS[:, 3, :], RET_V, EPS, (t, l, "r_ms_read", h - 1), [(t, l, "r_ms", h - 1, 1), "eps"])
                    run(reads)
                    if h:
                        for e in range(2):
                            i = 2 * (h - 1) + e
                            split_hi(YH[:, i, :], AR[:, 18 + e, :], [(t, l, "r_gated", h - 1, e), (t, l, "wa", 7)],
                                     (t, l, "r_hi", i))
                    if h < RET_HEADS:
                        run(reads, 2 if h + 1 < RET_HEADS else 1)
                        for e in range(2):
                            A.after((t, l, "r_out", h, 1), (t, l, "r_ms", h - 1, 1) if h else None)
                            A.done(act.activation(AR[:, 2 + e, :], PS[:, 4 + e, :], ACT.Square), t, l, "r_sq", h, e)
                        for e in range(2):
                            A.after((t, l, "r_lo", 2 * h - 1) if h else None)
                            A.done(act.activation(AR[:, 18 + e, :], PS[:, 4 + e, :], ACT.Copy), t, l, "r_copied", h, e)
                        marks[(t, l, "r_out_read", h)] = ("act", A.n)
                squared = norm_squares(t, l, "n2", lambda k: ("read", t, l, "wo", k))
                mixer_gemms(l, w, t, gates, squared)
                norm(t, l, "n2", squared, 6, w["ff"] + 1)
                ffn(l, t, w["ff"], FF1_GROUPS, 4, *bases(t, l))
                if l == 0:
                    const_dma(act, VEC[:, 0, :], vec_in[2], "vec2")
            norm("f", 0, "n1", norm_squares("f", 0, "n1", lambda k: ("a", DEPTH - 1, "ffn_out", k)), 4,
                 at_b(0)["q"] + 1, to_x=True)
            const_dma(act, VEC[:, 1, :], vec_in[3], "vec3")

            for l in range(DEPTH):
                w, t = at_b(l), "b"
                const_dma(act, WG[:, :], wgate_in[l], ("w_gate", l))
                j = 0
                for i in range(7):
                    if i:
                        hi(w["q"] + i + 1)
                    for m in range(2):
                        read((t, l, "q", j), AR[:, j if j < 13 else 18, :])
                        j += 1

                def tok_reads(n, name):
                    for p in range(2):
                        hi(n + p + 1)
                        for m in range(2):
                            u0 = (14 if name == "av" else 4) + 2 * m
                            A.after((t, l, name, p, m))
                            A.done(act.activation(AR[:, u0:u0 + 2, p * 256:(p + 1) * 256],
                                                  bank_of(t, l, name, p, m).rearrange("p (a b) -> p a b", a=2), ACT.Copy),
                                   "read", t, l, name, p, m)
                            yield

                fillers = tok_reads(w["v"], "av")
                run(fillers, 2)
                for i in range(12):
                    nk = (i // 4 + 2) * P
                    A.after((t, l, "dots", i), (t, l, "acc", 2 * (i - 2) + 1) if i >= 2 else None)
                    A.done(act.activation(probs(i, nk), PS[:, 4 + 2 * (i % 2):6 + 2 * (i % 2), 0:nk], ACT.Relu, scale=0.125),
                           t, l, "dots_read", i)
                    if i in (3, 7):
                        run(fillers)

                def filler_reads():
                    for p in range(4):
                        hi(w["ga"] + p + 1)
                        for m in range(2):
                            read((t, l, "ga", 2 * p + m), G[:, 2 * p + m, :], ACT.Sigmoid)
                            yield
                    for p in range(2):
                        hi(w["gq"] + p + 1)
                        for m in range(2):
                            read((t, l, "gq", 2 * p + m), YSCR[:, KD + 4 + 2 * p + m, :])
                            yield

                attention(pairs_b(l), l, t, filler_reads())
                for p in range(2):
                    hi(w["wa"] + p + 1)
                for n in range(NB):
                    A.after((t, l, "gate", n), (t, l, "la", n - 2) if n >= 2 else None)
                    A.done(act.activation(TMP[:, n % 2, :], PS[:, 4 + n % 2, :], ACT.Abs))
                    A.after()
                    A.done(act.activation(TMP[:, n % 2, :], TMP[:, n % 2, :], ACT.Exp, scale=-1.0))
                    A.after()
                    A.done(act.activation(TMP[:, n % 2, :], TMP[:, n % 2, :], ACT.Ln, bias=1.0), t, l, "soft", n)
                for _ in tok_reads(w["gk"], "gk"):
                    pass
                for n in range(NB):
                    A.after((t, l, "decay", n), (t, l, "kd", n - 2) if n >= 2 else (t, l, "la", 3))
                    A.done(act.activation(TMP[:, n % 2, :], PS[:, 4 + n % 2, :], ACT.Exp), t, l, "decay_read", n)
                A.after((t, l, "totals"))
                A.done(act.activation(ST[:, 64:96], PS[:, 6, 0:32], ACT.Exp), t, l, "totals_read")

                def gv_reads(h):
                    hi(w["gv"] + 2 * h + 1)
                    for m in range(2):
                        read((t, l, "gv", h, m), AR[:, 14 + 2 * (h % 2) + m, :], ACT.Copy,
                             (t, l, "g_out", h - 2, 7) if h >= 2 else None)
                        yield

                gates = gate_reads(l, w, t)

                def filler_reads():
                    for h in range(GLA_HEADS):
                        hi(w["gv"] + 2 * h + 2)
                        for m in range(2):
                            read((t, l, "gr", h, m), AR[:, 8 + 2 * (h % 2) + m, :], ACT.Silu,
                                 (t, l, "r_gated", h - 2, m) if h >= 2 else (t, l, "totals"))
                            yield
                        if h + 1 < GLA_HEADS:
                            yield from gv_reads(h + 1)
                    yield from gates

                def gla_squares(h):
                    for e in range(2):
                        A.after((t, l, "o_centered", h, e), (t, l, "kd", 3), (t, l, "o_ms", h - 1) if h else None)
                        A.done(act.activation(TMP[:, e, :], AR[:, 18 + e, :], ACT.Square), t, l, "o_sq", h, e)

                def gla_hi(h):
                    for e in range(2):
                        split_hi(YH[:, 2 * h + e, :], AR[:, 18 + e, :], [(t, l, "r_gated", h, e), (t, l, "wa", 7)],
                                 (t, l, "r_hi", 2 * h + e))

                for _ in gv_reads(0):
                    pass
                reads = filler_reads()
                for h in range(GLA_HEADS + 1):
                    if h:
                        gla_squares(h - 1)
                    run(reads)
                    if h:
                        root(PS[:, 3, :], GLA_DV, LN_EPS, (t, l, "o_ms_read", h - 1), [(t, l, "o_ms", h - 1), "eps"])
                    run(reads)
                    if h < GLA_HEADS:
                        run(reads)
                    if h:
                        gla_hi(h - 1)
                    if h < GLA_HEADS:
                        for e in range(2):
                            A.after((t, l, "g_out", h, 7), (t, l, "r_lo", 2 * h - 1) if h else None)
                            A.done(act.activation(AR[:, 18 + e, :], PS[:, 6 + e, :], ACT.Copy, scale=GLA_DK ** -0.5),
                                   t, l, "o_copied", h, e)
                        marks[(t, l, "o_out_read", h)] = ("act", A.n)
                        run(reads)
                mixer_gemms(l, w, t, gates)
                for which, gain in (("ln1", VB["ln1_g"]), ("ln2", VB["ln2_g"])):
                    for _ in squares(lambda k: X[:, k, :], KD, lambda k: TMP[:, k % 2, :], lambda k: (t, l, which + "_centered", k),
                            lambda k: (t, l, which + "_ms", k - 2) if k >= 2 else None, (t, l, which + "_sq")):
                        pass
                    warm_root()
                    root(PS[:, 5, :], D, LN_EPS, (t, l, which + "_root"), [(t, l, which + "_ms"), "eps"])
                    if which == "ln1" or l + 1 < DEPTH:
                        hi(w["ff"] + 1 if which == "ln1" else at_b(l + 1)["q"] + 1)
                    for k in range(KD):
                        g = gain + k
                        A.after((t, l, which + "_scaled", k))
                        A.done(act.activation(X[:, k, :], X[:, k, :], ACT.Identity, scale=VEC[:, l % 2, g:g + 1],
                                              bias=VEC[:, l % 2, g + 8:g + 9]), t, l, which + "_x", k)
                        if which == "ln1":
                            split_hi(XH[:, k, :], X[:, k, :], [], (t, l, "ln1_hi", k))
                        elif l + 1 < DEPTH:
                            split_hi(XH[:, k, :], X[:, k, :], [], (t, l + 1, "x_hi", k))
                    if which == "ln1":
                        for k in range(KD):
                            A.after((t, l, "ln1_lo", k))
                            A.done(act.activation(X[:, k, :], X[:, k, :], ACT.Copy, scale=DN_ALPHA), t, l, "x2_scaled", k)
                        ffn(l, t, w["ff"], FF2_GROUPS, 2, *bases(t, l))

        @block.vector
        def _(dve):
            V = Steps(dve, "dve", sems["dve"], marks, sems)
            dve.sem_inc(down_added, CREDIT)
            V.done(dve.memset(ST[:, 96:97], EPS))
            V.done(dve.memset(ST[:, 97:98], LN_EPS), "eps")

            def lo(dst, src, high, after, name, own=True):
                V.after(*after, own=own)
                V.done(dve.tensor_tensor(dst, src, high.bitcast(F32), ALU.subtract), *name)

            def rope(x, ps, name, after, part=TMP[:, 2, :]):
                V.after(*after)
                V.done(dve.tensor_tensor(part, ps, ROT[:, 1, :], ALU.mult))
                V.after()
                V.done(dve.tensor_tensor(x, x, ROT[:, 0, :], ALU.mult))
                V.after()
                V.done(dve.tensor_tensor(x, x, part, ALU.add), *name)

            def inverse_root(after):
                V.after(*after)
                V.done(dve.reciprocal(TMP[:, 3, :], TMP[:, 3, :]))

            def sums(src, ready, name):
                for k in range(1, KD):
                    a = src(0) if k == 1 else TMP[:, 2, :]
                    V.after(ready(0) if k == 1 else None, ready(k))
                    V.done(dve.tensor_tensor(TMP[:, 2, :], a, src(k), ALU.add), *name, k)
                    yield

            def square_sums(t, l, which):
                return sums(lambda k: TMP[:, k % 2, :], lambda k: (t, l, which + "_sq", k), (t, l, which + "_acc"))

            def x_sums(t, l, which):
                return sums(lambda k: X[:, k, :], lambda k: None, (t, l, which + "_sum"))

            def token_inverse(t, l, which):
                V.after((t, l, which + "_root"))
                V.done(dve.reciprocal(ST[:, 104:108], ST[:, 100:104]))
                V.after()
                V.done(dve.tensor_tensor(TMP[:, 3, :].rearrange("p (c i) -> p c i", c=NB),
                                         CT[:, 0:128].unsqueeze(1).broadcast_to([P, NB, P]),
                                         ST[:, 104:108].unsqueeze(2).broadcast_to([P, NB, P]), ALU.mult),
                       t, l, which + "_diagonal")

            def norm(t, l, which, gain, to_x=False):
                token_inverse(t, l, which)
                h = "h" if which == "n1" else "h2"
                spread_bank = 7 if which == "n2" else 5

                def dst(k):
                    return X[:, k, :] if to_x else TMP[:, k % 2, :]

                def hi_name(k):
                    return ("b", 0, "x_hi", k) if to_x else (t, l, h + "_hi", k)

                def lo_name(k):
                    return ("b", 0, "x_lo", k) if to_x else (t, l, h + "_lo", k)

                gains = VEC[:, 1 if to_x else l % 2, gain:gain + KD]
                for k in range(KD + 1):
                    if k < KD:
                        V.after(*[hi_name(k - 2), lo_name(k - 2)] if k >= 2 else [(t, l, which + "_spread")], own=False)
                        V.done(dve.scalar_tensor_tensor(dst(k), X[:, k, :], gains[:, k:k + 1], PS[:, spread_bank, :],
                                                        ALU.mult, ALU.mult), t, l, which + "_scaled", k)
                    if k:
                        j = k - 1
                        lo(XL[:, j, :], dst(j), XH[:, j, :], [hi_name(j)], lo_name(j), own=False)

            def attention(pairs, l, t, steps, per_pair):
                def maxima(i):
                    U, c, nk = pairs[i], 8 * (i % 2), pairs[i]["nk"]
                    pr = probs(i, nk)
                    V.after((t, l, "s", i), (t, l, "pt", i - 2) if i >= 2 else None, (t, l, "mask", i // 4))
                    V.done(dve.scalar_tensor_tensor(pr, U["mask"].unsqueeze(1).broadcast_to([P, 2, nk]), U["weight"],
                                                    PS[:, 4:6, 0:nk], ALU.mult, ALU.add), t, l, "s_read", i)
                    V.after()
                    V.done(dve.tensor_reduce(ST[:, c:c + 2], pr, AX, ALU.max))
                    V.after()
                    if U["sink"] is None:
                        V.done(dve.tensor_scalar(ST[:, c + 2:c + 4], ST[:, c:c + 2], -(HD ** -0.5), None, ALU.mult),
                               t, l, "negmax", i)
                    else:
                        sinks = ST[:, 16 + U["sink"]:18 + U["sink"]]
                        V.done(dve.scalar_tensor_tensor(ST[:, c + 2:c + 4], ST[:, c:c + 2], -(HD ** -0.5), sinks,
                                                        ALU.mult, ALU.min))
                        V.after()
                        V.done(dve.tensor_tensor(ST[:, c + 6:c + 8], ST[:, c + 2:c + 4], sinks, ALU.subtract),
                               t, l, "negmax", i)

                def normalise(i):
                    U, c, nk = pairs[i], 8 * (i % 2), pairs[i]["nk"]
                    pr = probs(i, nk)
                    V.after((t, l, "exp", i))
                    if U["sink"] is not None:
                        V.done(dve.tensor_tensor(ST[:, c + 4:c + 6], ST[:, c + 4:c + 6], ST[:, c + 6:c + 8], ALU.add))
                        V.after()
                    V.done(dve.reciprocal(ST[:, c:c + 2], ST[:, c + 4:c + 6]))
                    V.after()
                    V.done(dve.tensor_tensor(pr, pr, ST[:, c:c + 2].unsqueeze(2).broadcast_to([P, 2, nk]), ALU.mult),
                           t, l, "p", i)

                for i in range(16):
                    maxima(i)
                    if per_pair > 1:
                        run(steps, per_pair)
                    normalise(i)
                    if per_pair == 1 and i:
                        run(steps)
                for j in range(4):
                    lo(YL[:, j, :], AR[:, 14 + j, :] if t == "a" else AR[:, 8 + j, :], YH[:, j, :],
                       [(t, l, "ao_hi", j)], (t, l, "ao_lo", j))

            def branch_gate(l, t):
                for m in range(8):
                    V.after((t, l, "wa", m), ("read", t, l, "ga", m))
                    V.done(dve.tensor_tensor(G[:, m, :], G[:, m, :], bank_of(t, l, "wa", m), ALU.mult),
                           "read", t, l, "wa", m)

            def angles(l):
                turns, angle = AR[:, 12, :], AR[:, 13, :]
                V.after(("pos", l), "consts_b")
                V.done(dve.tensor_copy(angle, turns.bitcast(I32)))
                V.after()
                V.done(dve.tensor_scalar(angle, angle, CT[:, 514:515], None, ALU.mult))
                V.after()
                V.done(dve.tensor_scalar(turns, angle, 1.0 / (2 * np.pi), 12582912.0, ALU.mult, ALU.add))
                V.after()
                V.done(dve.tensor_scalar(turns, turns, 12582912.0, None, ALU.subtract))
                for part in (6.28125, 2 * np.pi - 6.28125):
                    V.after()
                    V.done(dve.scalar_tensor_tensor(angle, turns, -part, angle, ALU.mult, ALU.add))
                V.after()
                V.done(dve.tensor_scalar(angle, angle, -3.1415925, 3.1415925, ALU.max, ALU.min), "b", l, "angle")

            def rot_tables(l):
                V.after(("b", l, "sines"))
                V.done(dve.tensor_scalar(ROT[:, 1, :], ROT[:, 1, :], CT[:, 515:516], None, ALU.mult))
                V.after()
                V.done(dve.tensor_tensor(AR[:, 12, :], AR[:, 12, :], AR[:, 12, :], ALU.mult))
                V.after()
                V.done(dve.tensor_scalar(ROT[:, 0, :], AR[:, 12, :], -2.0, 1.0, ALU.mult, ALU.add), "b", l, "rot_tables")

            def mixer_gemms(l, t):
                rot = next_rot(l, t)
                if rot is not None:
                    angles(rot)
                for m in range(8):
                    V.after((t, l, "wb", m), ("read", t, l, "gb", m))
                    V.done(dve.tensor_tensor(SB[:, m, :], SB[:, m, :], bank_of(t, l, "wb", m), ALU.mult),
                           "read", t, l, "wb", m)
                    V.after()
                    V.done(dve.tensor_tensor(G[:, m, :], G[:, m, :], SB[:, m, :], ALU.add), t, l, "merged", m)
                    lo(XL[:, m, :], G[:, m, :], XH[:, m, :], [(t, l, "merged_hi", m), (t, l, "gb", 7)],
                       (t, l, "merged_lo", m))
                if rot is not None:
                    rot_tables(rot)
                adding = square_sums(t, l, "n2") if t == "a" else x_sums(t, l, "ln1")
                for m in range(8):
                    V.after((t, l, "wo", m), (t, l, "x_scaled", m) if t == "b" else None)
                    V.done(dve.tensor_tensor(X[:, m, :], X[:, m, :], bank_of(t, l, "wo", m), ALU.add), "read", t, l, "wo", m)
                    if m >= 2:
                        run(adding)
                for _ in adding:
                    pass

            def ffn(l, t, groups, kt, base_t, base_d, base_h, adding):
                base_c = (base_d - 8 * FF1_GROUPS * DEPTH) // 2 if kt == 2 else 0
                V.after(*[(t, l, "x2_scaled", k) for k in range(KD)] if kt == 2 else [])

                def up(gc, gi, i):
                    g = gc + gi * i
                    buf = gc % 2
                    first = gi == 0 and gc == 0
                    for p in range(2):
                        if kt == 2:
                            for m in range(2):
                                j = 2 * p + m
                                ch = 2 * g + m + (2 * FF2_GROUPS if p else 0)
                                for tap in (1, 2):
                                    n = S - tap
                                    wv = VEC[:, l % 2, bass.ds(VB["conv_w"] + 88 - 44 * tap + ch, 1)]
                                    if tap == 1:
                                        dve.wait_ge(conv_begun, base_c + 4 * g + j + 1)
                                    else:
                                        dve.wait_ge(tap_added, base_c + 4 * g + j + 1)
                                    ins = dve.scalar_tensor_tensor(AR[:, j, tap:S], PS[:, j, 0:n], wv, AR[:, j, tap:S],
                                                                   ALU.mult, ALU.add)
                                    ins.then_inc(tap_added if tap == 1 else up_read, 1)
                        if kt == 4:
                            for m in range(2):
                                j = 2 * p + m
                                dve.wait_ge(up_read, base_t + 4 * g + j + 1)
                                if not (first and base_h == 0):
                                    dve.wait_ge(hid_lo, base_h + 4 * g + j - 3)
                                dve.tensor_tensor(AR[:, 4 + j, :], AR[:, j, :], AR[:, j, :], ALU.mult)\
                                   .then_inc(hid_ready, 1)
                            for m in range(2):
                                j = 2 * p + m
                                dve.wait_ge(hid_hi, base_h + 4 * g + j + 1)
                                dve.tensor_tensor(YL[:, 4 * buf + j, :], AR[:, 4 + j, :], YH[:, 4 * buf + j, :].bitcast(F32),
                                                  ALU.subtract).then_inc(hid_lo, 1)
                    if kt == 2:
                        for m in range(2):
                            dve.wait_ge(gelu_done, base_c // 2 + 2 * g + m + 1)
                            dve.wait_ge(up_read, base_t + 4 * g + 3 + m)
                            if not first:
                                dve.wait_ge(hid_lo, base_h + 2 * g + m - 1)
                            dve.tensor_tensor(AR[:, 6 + m, :], AR[:, 4 + m, :], AR[:, 2 + m, :], ALU.mult)\
                               .then_inc(hid_ready, 1)
                        for m in range(2):
                            dve.wait_ge(hid_hi, base_h + 2 * g + m + 1)
                            dve.tensor_tensor(YL[:, 2 * buf + m, :], AR[:, 6 + m, :], YH[:, 2 * buf + m, :].bitcast(F32),
                                              ALU.subtract).then_inc(hid_lo, 1)

                def down(gc, gi, i):
                    g = gc + gi * i
                    for m in range(8):
                        dve.wait_ge(down_full, CREDIT + base_d + 8 * g + m + 1)
                        dve.wait_ge(down_added, CREDIT + base_d + 8 * g + m - 7)
                        dve.tensor_tensor(X[:, m, :], X[:, m, :], PS[:, 4 + m % 4, :], ALU.add).then_inc(down_added, 1)
                        if gi == 0 and gc == groups - 1 and m >= 2:
                            if t == "b":
                                dve.wait_ge(down_added, CREDIT + base_d + 8 * g + m)
                            run(adding)

                up(0, 0, 0)
                trips = (groups - 1) // 2
                with dve.Fori(0, trips) as i:
                    up(1, 2, i)
                    down(0, 2, i)
                    up(2, 2, i)
                    down(1, 2, i)
                for g in range(2 * trips, groups):
                    if g + 1 < groups:
                        up(g + 1, 0, 0)
                    down(g, 0, 0)
                dve.wait_ge(down_added, CREDIT + base_d + 8 * groups)
                for _ in adding:
                    pass

            for l in range(DEPTH):
                t = "a"
                V.after("vec%d" % l)
                o = VA["sinks"]
                V.done(dve.tensor_scalar(ST[:, 16:24], VEC[:, l % 2, o:o + 8], -1.0, None, ALU.mult))
                for b in range(4):
                    marks[(t, l, "mask", b)] = marks.get("consts_a", ("const", 16))
                if l == 0:
                    run(square_sums(t, l, "n1"), KD)
                norm(t, l, "n1", VA["g_mix"])
                for j in (0, 1, 4, 2, 3):
                    rope(AR[:, j, :], PS[:, 4 + j % 2, :], (t, l, "roped", j), [(t, l, "swap", j), ("rot", l, 0)])

                def retention_ropes():
                    for j in range(8):
                        rope(AR[:, 6 + j, :], PS[:, 3, :], (t, l, "roped", 5 + j), [(t, l, "swap", 5 + j), ("rot", l, 1)],
                             YSCR[:, KD + 7, :])
                        yield

                attention(pairs_a(l), l, t, retention_ropes(), 1)
                branch_gate(l, t)
                def per_chunk(c0):
                    return CT[:, c0:c0 + P].unsqueeze(1).broadcast_to([P, NB, P])

                def chunks(ap):
                    return ap.rearrange("p (c i) -> p c i", c=NB)

                for h in range(RET_HEADS + 1):
                    if h < RET_HEADS:
                        dec, xi = CA["decay"] + h * P, CA["xi"] + h * P
                        V.after((t, l, "rs", h), (t, l, "r_out", h - 1, 1) if h else (t, l, "pt", 15))
                        V.done(dve.tensor_tensor(chunks(TMP[:, 0, :]), chunks(PS[:, 4, :]), per_chunk(dec), ALU.mult),
                               t, l, "rs_decayed", h)
                        V.after()
                        V.done(dve.tensor_tensor(chunks(TMP[:, 2, :]), chunks(AR[:, 6 + h, :]), per_chunk(xi), ALU.mult),
                               t, l, "qx", h)
                    if h:
                        inverse_root([(t, l, "r_ms_read", h - 1)])
                        for e in range(2):
                            V.after((t, l, "r_copied", h - 1, e))
                            V.done(dve.tensor_tensor(AR[:, 18 + e, :], AR[:, 18 + e, :], TMP[:, 3, :], ALU.mult))
                            V.after(("read", t, l, "rg", h - 1, e))
                            V.done(dve.tensor_tensor(AR[:, 18 + e, :], AR[:, 18 + e, :], rg_unit(h - 1, e), ALU.mult),
                                   t, l, "r_gated", h - 1, e)
                    if h < RET_HEADS:
                        g_chunk = float(np.exp(np.log1p(-2.0 ** (-5.0 - h)) * P))
                        flat = AR[:, 4:6, :].rearrange("p a s -> p (a s)")
                        V.after((t, l, "kv", h))
                        V.done(dve.tensor_copy(flat[:, 0:256], PS[:, 6, 0:256]), t, l, "state", h, 1)
                        for c in (1, 2):
                            ps = PS[:, 6, 256:512] if c == 1 else PS[:, 7, 0:256]
                            V.after()
                            V.done(dve.scalar_tensor_tensor(flat[:, 256 * c:256 * c + 256], flat[:, 256 * c - 256:256 * c],
                                                            g_chunk, ps, ALU.mult, ALU.add), t, l, "state", h, c + 1)
                    if h:
                        for e in range(2):
                            i = 2 * (h - 1) + e
                            lo(YL[:, i, :], AR[:, 18 + e, :], YH[:, i, :], [(t, l, "r_hi", i)], (t, l, "r_lo", i))
                mixer_gemms(l, t)
                norm(t, l, "n2", VA["g_mlp"])
                ffn(l, t, FF1_GROUPS, 4, *bases(t, l), square_sums(*(("a", l + 1) if l + 1 < DEPTH else ("f", 0)), "n1"))
            norm("f", 0, "n1", VB["g_final"], to_x=True)

            for l in range(DEPTH):
                t = "b"
                V.after("vec2" if l == 0 else "vec3")
                for j in range(13):
                    rope(AR[:, j, :], PS[:, 4 + j % 2, :], (t, l, "roped", j), [(t, l, "swap", j)])
                iw = ST[:, 32:64].rearrange("p (n h) -> p n h", n=NB)
                V.after((t, l, "iw"))
                V.done(dve.tensor_scalar(iw, PS[:, 6, :].rearrange("p (n c) -> p n c", n=NB)[:, :, 32:40], 8 ** -0.5, None,
                                         ALU.mult), t, l, "iw_read")
                V.after()
                V.done(dve.memset(AR[0:32, 13, :], 1.0))
                V.after()
                V.done(dve.tensor_copy(AR[0:16, 13, :], AR[0:16, 18, :]), t, l, "glr")
                V.after()
                m0 = mask_b(0)
                V.done(dve.memset(m0, 0.0))
                V.after()
                V.done(dve.memset(m0[0:64, 64:128], -1.0), t, l, "mask", 0)
                for b in range(1, NB):
                    sc = mask_b(b)
                    for h in range(8):
                        u = 8 * (b - 1) + h
                        src = probs(u // 2, (b + 1) * P)[:, u % 2, :]
                        V.after((t, l, "dots_read", u // 2))
                        wcol = ST[:, 32 + 8 * b + h:33 + 8 * b + h]
                        if h == 0:
                            V.done(dve.tensor_scalar(sc, src, wcol, None, ALU.mult), t, l, "acc", u)
                        else:
                            V.done(dve.scalar_tensor_tensor(sc, src, wcol, sc, ALU.mult, ALU.add), t, l, "acc", u)
                    V.after()
                    V.done(dve.memset(sc[0:64, b * P + 64:(b + 1) * P], NEG))

                def top_k():
                    for b in range(1, NB):
                        sc, other, best = mask_b(b), AR[:, 12, 0:(b + 1) * P], ST[:, 24:32]
                        for r in range(TOPK // 8):
                            src, dst = (sc, other) if r % 2 == 0 else (other, sc)
                            V.after((t, l, "dots", 11))
                            V.done(dve.max(best, src))
                            V.after()
                            V.done(dve.match_replace(dst, best, src, TAKEN))
                            if r == TOPK // 8 - 1:
                                V.after()
                                V.done(dve.tensor_scalar(sc, sc, TAKEN, 1.0, ALU.is_equal, ALU.subtract), t, l, "mask", b)
                            yield

                attention(pairs_b(l), l, t, top_k(), TOPK // 8 // 4)
                branch_gate(l, t)
                for n in range(NB):
                    V.after((t, l, "soft", n), (t, l, "ao_hi", 3))
                    V.done(dve.scalar_tensor_tensor(AR[:, 8 + n, :], PS[:, 4 + n % 2, :], 0.0, TMP[:, n % 2, :],
                                                    ALU.min, ALU.subtract), t, l, "la", n)
                for n in range(NB):
                    V.after((t, l, "decay_read", n), *[("read", t, l, "gk", p, n // 2) for p in range(2)])
                    V.done(dve.tensor_tensor(AR[:, 4 + n, :], AR[:, 4 + n, :], TMP[:, n % 2, :], ALU.mult), t, l, "kd", n)
                def state(h, c):
                    ps = PS[:, 4 + (c // 2) % 2, (c % 2) * 256:(c % 2) * 256 + 256]
                    new, old = AR[:, 12, (c % 2) * 256:(c % 2) * 256 + 256], AR[:, 12, ((c + 1) % 2) * 256:((c + 1) % 2) * 256 + 256]
                    V.after((t, l, "gkv", h, c | 1), (t, l, "totals_read"),
                            (t, l, "g_out", h, c - 2) if c >= 2 else ((t, l, "g_out", h - 1, c + 6) if h else None))
                    if c == 0:
                        V.done(dve.tensor_copy(new, ps), t, l, "state", h, c)
                    else:
                        V.done(dve.scalar_tensor_tensor(new, old, ST[:, 64 + 8 * h + c:65 + 8 * h + c], ps,
                                                        ALU.mult, ALU.add), t, l, "state", h, c)

                def centre(h):
                    for e in range(2):
                        V.after((t, l, "o_mean", h), (t, l, "o_copied", h, e))
                        V.done(dve.scalar_tensor_tensor(AR[:, 18 + e, :], PS[:, 2, :], -1.0 / GLA_DV, AR[:, 18 + e, :],
                                                        ALU.mult, ALU.add), t, l, "o_centered", h, e)

                def gate(h):
                    for e in range(2):
                        g = VB["gla_g"] + 2 * h + e
                        V.after((t, l, "o_sq", h, e))
                        V.done(dve.scalar_tensor_tensor(AR[:, 18 + e, :], AR[:, 18 + e, :], VEC[:, l % 2, g:g + 1],
                                                        TMP[:, 3, :], ALU.mult, ALU.mult))
                        V.after(("read", t, l, "gr", h, e))
                        V.done(dve.tensor_tensor(AR[:, 18 + e, :], AR[:, 18 + e, :], AR[:, 8 + 2 * (h % 2) + e, :], ALU.mult),
                               t, l, "r_gated", h, e)

                for h in range(GLA_HEADS + 1):
                    if h:
                        centre(h - 1)
                    for c in range(4):
                        if h < GLA_HEADS:
                            state(h, c)
                    if h:
                        inverse_root([(t, l, "o_ms_read", h - 1)])
                    if h < GLA_HEADS:
                        state(h, 4)
                        state(h, 5)
                    if h:
                        gate(h - 1)
                    if h < GLA_HEADS:
                        state(h, 6)
                        state(h, 7)
                    if h:
                        for e in range(2):
                            i = 2 * (h - 1) + e
                            lo(YL[:, i, :], AR[:, 18 + e, :], YH[:, i, :], [(t, l, "r_hi", i)], (t, l, "r_lo", i))
                mixer_gemms(l, t)
                for which in ("ln1", "ln2"):
                    if which == "ln2":
                        ffn(l, t, FF2_GROUPS, 2, *bases(t, l), x_sums(t, l, "ln2"))
                    for k in range(KD):
                        V.after((t, l, which + "_mean"), own=False)
                        V.done(dve.scalar_tensor_tensor(X[:, k, :], PS[:, 4, :], -1.0 / D, X[:, k, :], ALU.mult, ALU.add),
                               t, l, which + "_centered", k)
                    inverse_root([(t, l, which + "_root")])
                    marks[(t, l, which + "_inverse")] = ("dve", V.n)
                    for k in range(KD + 1):
                        if k < KD:
                            V.after((t, l, which + "_sq", k), (t, l, which + "_inverse"), own=False)
                            V.done(dve.tensor_tensor(X[:, k, :], X[:, k, :], TMP[:, 3, :], ALU.mult), t, l, which + "_scaled", k)
                        j = k - 1
                        if k and which == "ln1":
                            lo(XL[:, j, :], X[:, j, :], XH[:, j, :], [(t, l, "ln1_hi", j)], (t, l, "ln1_lo", j), own=False)
                        elif k and l + 1 < DEPTH:
                            lo(XL[:, j, :], X[:, j, :], XH[:, j, :], [(t, l + 1, "x_hi", j)], (t, l + 1, "x_lo", j), own=False)


def kernel(**inputs):
    import concourse.bacc as bacc
    from concourse.bass_utils import run_bass_kernel_spmd

    i = {k: np.asarray(v) for k, v in inputs.items()}
    consts, rot = _constants()
    wgate = np.zeros((DEPTH, 32, S), np.float32)
    for l in range(DEPTH):
        wgate[l, 0:GLA_RANK] = i["gla_w_gate_2"][l]
        wgate[l, GLA_RANK] = i["gla_b_gate_2"][l]
    arrays = {
        "stream": _stream(i), "x_t": np.ascontiguousarray(i["x"][0].T), "consts": consts, "rot": rot,
        "vectors": _vectors(i), "w_gate_in": wgate,
        "pos": np.ascontiguousarray(np.broadcast_to(i["positions_2"].astype(np.int32), (P, S))),
    }

    def build(marks):
        nc = bacc.Bacc("TRN2", target_bir_lowering=False, num_devices=1)
        args = [nc.dram_tensor(n, a.shape, mybir.dt.from_np(a.dtype), kind="ExternalInput").ap() for n, a in arrays.items()]
        args.append(nc.dram_tensor("y_t", (D, S), F32, kind="ExternalOutput").ap())
        program(nc, *args, marks)
        return nc

    marks = {}
    build(marks)
    marks["complete"] = True
    nc = build(marks)
    r = run_bass_kernel_spmd(nc, [arrays], core_ids=[0])
    return np.ascontiguousarray(r.results[0]["y_t"].T)[None]
```
